# Optimizing a Trainium2 kernel written in Bass

```python
import jax, jax.numpy as jnp
from jax import lax
import numpy as np

D_MODEL = 2048
BATCH = 1
SEQ = 256
DEPTH = 1

PLE_DIM = 256
ATTN_WIDTH = D_MODEL // 2
CONV_WIDTH = D_MODEL - ATTN_WIDTH
HEAD_DIM = 64
N_Q_HEADS = ATTN_WIDTH // HEAD_DIM
N_KV_HEADS = 4
GQA_GROUP = N_Q_HEADS // N_KV_HEADS
KV_WIDTH = N_KV_HEADS * HEAD_DIM
WINDOW = 128
BLOCK = 128
ROT_DIM = HEAD_DIM // 4
ROPE_THETA = 500000.0
CONV_K = 3
CONV_GROUPS = 16
EPS = 1e-6
NEG_INF = -1e30

SEG_WIDTHS = (ATTN_WIDTH, KV_WIDTH, KV_WIDTH, ATTN_WIDTH,
              CONV_WIDTH, CONV_WIDTH, CONV_WIDTH, CONV_WIDTH)
IN_WIDTH = sum(SEG_WIDTHS)
SPLITS = [int(v) for v in np.cumsum(SEG_WIDTHS)[:-1]]


def rms_norm(x, gain):
    xf = x.astype(jnp.float32)
    y = xf * lax.rsqrt(jnp.mean(xf * xf, axis=-1, keepdims=True) + EPS)
    return (y * gain.astype(jnp.float32)).astype(x.dtype)

def partial_rope(x, pos):
    half = ROT_DIM // 2
    inv_freq = jnp.power(jnp.float32(ROPE_THETA), -jnp.arange(half, dtype=jnp.float32) * 2.0 / ROT_DIM)
    ang = pos.astype(jnp.float32)[:, None] * inv_freq[None, :]
    cos = jnp.cos(ang)[None, :, None, :]
    sin = jnp.sin(ang)[None, :, None, :]
    xr = x[..., :ROT_DIM].astype(jnp.float32)
    x1, x2 = xr[..., :half], xr[..., half:]
    rot = jnp.concatenate([x1 * cos - x2 * sin, x2 * cos + x1 * sin], axis=-1).astype(x.dtype)
    return jnp.concatenate([rot, x[..., ROT_DIM:]], axis=-1)

def sliding_window_attention(q, k, v, sinks):
    b, s = q.shape[0], q.shape[1]
    nb = s // BLOCK
    qb = q.reshape(b, nb, BLOCK, N_KV_HEADS, GQA_GROUP, HEAD_DIM)

    def band(t):
        tb = t.reshape(b, nb, BLOCK, N_KV_HEADS, HEAD_DIM)
        prev = jnp.pad(tb, ((0, 0), (1, 0), (0, 0), (0, 0), (0, 0)))[:, :-1]
        return jnp.concatenate([prev, tb], axis=2)

    kb, vb = band(k), band(v)
    scores = jnp.einsum('bnqhgd,bnkhd->bnhgqk', qb, kb,
                        preferred_element_type=jnp.float32) * (HEAD_DIM ** -0.5)
    q_pos = jnp.arange(nb)[:, None] * BLOCK + jnp.arange(BLOCK)[None, :]
    k_pos = jnp.arange(nb)[:, None] * BLOCK - BLOCK + jnp.arange(2 * BLOCK)[None, :]
    diff = q_pos[:, :, None] - k_pos[:, None, :]
    mask = (diff >= 0) & (diff < WINDOW) & (k_pos[:, None, :] >= 0)
    scores = jnp.where(mask[None, :, None, None], scores, NEG_INF)
    sink = sinks.astype(jnp.float32).reshape(N_KV_HEADS, GQA_GROUP)[None, None, :, :, None, None]
    m = jnp.maximum(jnp.max(scores, axis=-1, keepdims=True), sink)
    e = jnp.exp(scores - m)
    probs = e / (jnp.sum(e, axis=-1, keepdims=True) + jnp.exp(sink - m))
    out = jnp.einsum('bnhgqk,bnkhd->bnqhgd', probs.astype(v.dtype), vb)
    return out.reshape(b, s, N_Q_HEADS * HEAD_DIM)

def short_conv(u, w):
    return lax.conv_general_dilated(
        u, w[:, None, :].astype(u.dtype), window_strides=(1,),
        padding=[(CONV_K - 1, 0)], dimension_numbers=('NWC', 'WIO', 'NWC'),
        feature_group_count=u.shape[-1])

def first_inputs(seed: int = 0) -> dict:
    key = jax.random.key(seed)
    ks = jax.random.split(key, 16)
    f32 = jnp.float32
    nrm = lambda k, shape, scale: jax.random.normal(k, shape, f32) * scale
    return {
        "x": nrm(ks[0], (BATCH, SEQ, D_MODEL), 1.0),
        "p": nrm(ks[1], (DEPTH, BATCH, SEQ, PLE_DIM), 1.0),
        "norm_gain": 1.0 + nrm(ks[2], (DEPTH, D_MODEL), 0.02),
        "w_in": nrm(ks[3], (DEPTH, D_MODEL, IN_WIDTH), D_MODEL ** -0.5),
        "q_norm_gain": 1.0 + nrm(ks[4], (DEPTH, HEAD_DIM), 0.02),
        "k_norm_gain": 1.0 + nrm(ks[5], (DEPTH, HEAD_DIM), 0.02),
        "attn_sinks": nrm(ks[6], (DEPTH, N_Q_HEADS), 0.5),
        "conv_w": nrm(ks[7], (DEPTH, CONV_K, CONV_WIDTH), CONV_K ** -0.5),
        "w_out": nrm(ks[8], (DEPTH, D_MODEL, D_MODEL), D_MODEL ** -0.5),
        "ple_gate_norm_gain": 1.0 + nrm(ks[9], (DEPTH, D_MODEL), 0.02),
        "w_ple_gate": nrm(ks[10], (DEPTH, D_MODEL, D_MODEL), D_MODEL ** -0.5),
        "b_ple_gate": nrm(ks[11], (DEPTH, D_MODEL), 0.01),
        "w_ple_proj": nrm(ks[12], (DEPTH, PLE_DIM, D_MODEL), PLE_DIM ** -0.5),
        "ple_norm_gain": 1.0 + nrm(ks[13], (DEPTH, D_MODEL), 0.02),
    }

def first_block(x, p, norm_gain, w_in, q_norm_gain, k_norm_gain, attn_sinks, conv_w, w_out,
              ple_gate_norm_gain, w_ple_gate, b_ple_gate, w_ple_proj, ple_norm_gain):
    b, s = x.shape[0], x.shape[1]
    pos = jnp.arange(s)
    for i in range(DEPTH):
        h = rms_norm(x, norm_gain[i])
        z = h @ w_in[i]
        q, k, v, g_attn, c_b, c_c, c_h, g_conv = jnp.split(z, SPLITS, axis=-1)

        q = q.reshape(b, s, N_Q_HEADS, HEAD_DIM)
        k = k.reshape(b, s, N_KV_HEADS, HEAD_DIM)
        v = v.reshape(b, s, N_KV_HEADS, HEAD_DIM)
        q = partial_rope(rms_norm(q, q_norm_gain[i]), pos)
        k = partial_rope(rms_norm(k, k_norm_gain[i]), pos)
        y_attn = sliding_window_attention(q, k, v, attn_sinks[i]) * jax.nn.silu(g_attn)

        y_conv = c_b * short_conv(c_c * c_h, conv_w[i]) * jax.nn.silu(g_conv)

        mix = jnp.concatenate([y_attn, y_conv], axis=-1)
        x = x + mix @ w_out[i]

        gate = jax.nn.sigmoid(rms_norm(x, ple_gate_norm_gain[i]) @ w_ple_gate[i] + b_ple_gate[i])
        e = rms_norm(p[i] @ w_ple_proj[i], ple_norm_gain[i])
        x = x + gate * e
    return x


RNN_WIDTH = D_MODEL
RNN_BLOCKS = 16
CONV_WIDTH_2 = 4
RG_C = 8.0
N_HEADS = 16
HEAD_DIM_2 = D_MODEL // N_HEADS
KV_RANK = 512
IDX_HEADS = 16
IDX_DIM = 64
TOPK_MAX = 256
Q_BLOCK = 128
PEER_HEADS = 8
PEER_KEYS = 128
PEER_EXPERTS = PEER_KEYS * PEER_KEYS
PEER_QDIM = 256
PEER_TOPK = 16
PEER_CHUNK = 128

SPLITS_2 = (RNN_WIDTH, N_HEADS * HEAD_DIM_2, KV_RANK, IDX_HEADS * IDX_DIM, IDX_DIM, IDX_HEADS, D_MODEL, D_MODEL)
IN_WIDTH_2 = sum(SPLITS_2)


def rmsnorm(x, g):
    xf = x.astype(jnp.float32)
    y = xf * lax.rsqrt(jnp.mean(xf * xf, axis=-1, keepdims=True) + EPS)
    return (y * g.astype(jnp.float32)).astype(x.dtype)

def layernorm(x, g, b):
    xf = x.astype(jnp.float32)
    mu = jnp.mean(xf, axis=-1, keepdims=True)
    var = jnp.mean(jnp.square(xf - mu), axis=-1, keepdims=True)
    y = (xf - mu) * lax.rsqrt(var + EPS)
    return (y * g.astype(jnp.float32) + b.astype(jnp.float32)).astype(x.dtype)

def causal_conv(x, w, b):
    s = x.shape[1]
    xp = jnp.pad(x, ((0, 0), (CONV_WIDTH_2 - 1, 0), (0, 0)))
    y = b
    for i in range(CONV_WIDTH_2):
        y = y + xp[:, i:i + s] * w[i]
    return y

def rg_lru(x, wa, ba, wx, bx, lam):
    bsz, s, _ = x.shape
    xb = x.reshape(bsz, s, RNN_BLOCKS, -1)
    r = jax.nn.sigmoid(jnp.einsum('bsnc,ncd->bsnd', xb, wa).reshape(bsz, s, -1) + ba)
    i = jax.nn.sigmoid(jnp.einsum('bsnc,ncd->bsnd', xb, wx).reshape(bsz, s, -1) + bx)
    log_a = -RG_C * r.astype(jnp.float32) * jax.nn.softplus(-lam.astype(jnp.float32))
    a = jnp.exp(log_a)
    u = jnp.sqrt(-jnp.expm1(2.0 * log_a)) * (i * x).astype(jnp.float32)

    def combine(c1, c2):
        a1, b1 = c1
        a2, b2 = c2
        return a1 * a2, a2 * b1 + b2

    _, h = lax.associative_scan(combine, (a, u), axis=1)
    return h.astype(x.dtype)

def dsa_attention(q, c_kv, q_idx, k_idx, w_idx, w_uk, w_uv):
    bsz, s = c_kv.shape[:2]
    topk = min(TOPK_MAX, s // 4)
    key_pos = jnp.arange(s)

    def block(blk):
        t0 = blk * Q_BLOCK
        sl = lambda a: lax.dynamic_slice_in_dim(a, t0, Q_BLOCK, axis=1)
        qb, qib, wib = sl(q), sl(q_idx), sl(w_idx)
        qpos = t0 + jnp.arange(Q_BLOCK)
        rel = jax.nn.relu(jnp.einsum('bqhd,bsd->bqhs', qib, k_idx) * IDX_DIM ** -0.5)
        iscore = jnp.einsum('bqhs,bqh->bqs', rel, wib).astype(jnp.float32)
        causal = key_pos[None, :] <= qpos[:, None]
        iscore = jnp.where(causal[None], iscore, -jnp.inf)
        _, sel = lax.top_k(iscore, topk)
        valid = sel <= qpos[None, :, None]
        c_sel = jax.vmap(lambda c, ix: c[ix])(c_kv, sel)
        q_lat = jnp.einsum('bqhd,hcd->bqhc', qb, w_uk)
        logits = jnp.einsum('bqhc,bqkc->bqhk', q_lat, c_sel).astype(jnp.float32) * HEAD_DIM_2 ** -0.5
        logits = jnp.where(valid[:, :, None, :], logits, -jnp.inf)
        p = jax.nn.softmax(logits, axis=-1).astype(c_sel.dtype)
        o_lat = jnp.einsum('bqhk,bqkc->bqhc', p, c_sel)
        o = jnp.einsum('bqhc,hcd->bqhd', o_lat, w_uv)
        return o.reshape(bsz, Q_BLOCK, -1)

    out = lax.map(block, jnp.arange(s // Q_BLOCK))
    return out.transpose(1, 0, 2, 3).reshape(bsz, s, -1)

def peer(x, wq, keys1, keys2, u, v):
    bsz, s, d = x.shape
    t = bsz * s
    xf = x.reshape(t, d)
    q = (xf @ wq).reshape(t, PEER_HEADS, PEER_QDIM)
    half = PEER_QDIM // 2
    s1 = jnp.einsum('thd,kd->thk', q[..., :half], keys1)
    s2 = jnp.einsum('thd,kd->thk', q[..., half:], keys2)
    v1, i1 = lax.top_k(s1, PEER_TOPK)
    v2, i2 = lax.top_k(s2, PEER_TOPK)
    cand_s = (v1[..., :, None] + v2[..., None, :]).reshape(t, PEER_HEADS, -1)
    cand_i = (i1[..., :, None] * PEER_KEYS + i2[..., None, :]).reshape(t, PEER_HEADS, -1)
    top_s, pos = lax.top_k(cand_s, PEER_TOPK)
    expert = jnp.take_along_axis(cand_i, pos, axis=-1).reshape(t, -1)
    gate = jax.nn.softmax(top_s.astype(jnp.float32), axis=-1).astype(x.dtype).reshape(t, -1)
    n_chunks = t // PEER_CHUNK

    def chunk(args):
        xc, ec, gc = args
        z = jnp.einsum('cd,ced->ce', xc, u[ec])
        act = jax.nn.gelu(z, approximate=False) * gc
        return jnp.einsum('ce,ced->cd', act, v[ec])

    out = lax.map(chunk, (xf.reshape(n_chunks, PEER_CHUNK, d),
                          expert.reshape(n_chunks, PEER_CHUNK, -1),
                          gate.reshape(n_chunks, PEER_CHUNK, -1)))
    return out.reshape(bsz, s, d)

def second_inputs(seed: int = 0) -> dict:
    key = jax.random.key(seed)
    ks = jax.random.split(key, 24)
    f32 = jnp.float32
    nrm = lambda k, shape, scale: jax.random.normal(k, shape, f32) * scale
    gain = lambda k, shape: 1.0 + 0.05 * jax.random.normal(k, shape, f32)
    bw = RNN_WIDTH // RNN_BLOCKS
    a_c = jax.random.uniform(ks[9], (DEPTH, RNN_WIDTH), f32, 0.9, 0.999)
    a = a_c ** (1.0 / RG_C)
    rg_lambda = jnp.log(a) - jnp.log1p(-a)
    return {
        "x": nrm(ks[0], (BATCH, SEQ, D_MODEL), 1.0),
        "norm_mix_g": gain(ks[1], (DEPTH, D_MODEL)),
        "w_in": nrm(ks[2], (DEPTH, D_MODEL, IN_WIDTH_2), D_MODEL ** -0.5),
        "conv_w": nrm(ks[3], (DEPTH, CONV_WIDTH_2, RNN_WIDTH), CONV_WIDTH_2 ** -0.5),
        "conv_b": nrm(ks[4], (DEPTH, RNN_WIDTH), 0.02),
        "rg_wa": nrm(ks[5], (DEPTH, RNN_BLOCKS, bw, bw), bw ** -0.5),
        "rg_ba": nrm(ks[6], (DEPTH, RNN_WIDTH), 0.1),
        "rg_wx": nrm(ks[7], (DEPTH, RNN_BLOCKS, bw, bw), bw ** -0.5),
        "rg_bx": nrm(ks[8], (DEPTH, RNN_WIDTH), 0.1),
        "rg_lambda": rg_lambda,
        "kv_norm_g": gain(ks[10], (DEPTH, KV_RANK)),
        "w_uk": nrm(ks[11], (DEPTH, N_HEADS, KV_RANK, HEAD_DIM_2), KV_RANK ** -0.5),
        "w_uv": nrm(ks[12], (DEPTH, N_HEADS, KV_RANK, HEAD_DIM_2), KV_RANK ** -0.5),
        "idx_ln_g": gain(ks[13], (DEPTH, IDX_DIM)),
        "idx_ln_b": nrm(ks[14], (DEPTH, IDX_DIM), 0.02),
        "w_o": nrm(ks[15], (DEPTH, D_MODEL, D_MODEL), D_MODEL ** -0.5),
        "norm_ffn_g": gain(ks[16], (DEPTH, D_MODEL)),
        "peer_wq": nrm(ks[17], (DEPTH, D_MODEL, PEER_HEADS * PEER_QDIM), D_MODEL ** -0.5),
        "peer_keys1": nrm(ks[18], (DEPTH, PEER_KEYS, PEER_QDIM // 2), (PEER_QDIM // 2) ** -0.5),
        "peer_keys2": nrm(ks[19], (DEPTH, PEER_KEYS, PEER_QDIM // 2), (PEER_QDIM // 2) ** -0.5),
        "peer_u": nrm(ks[20], (DEPTH, PEER_EXPERTS, D_MODEL), D_MODEL ** -0.5),
        "peer_v": nrm(ks[21], (DEPTH, PEER_EXPERTS, D_MODEL), PEER_HEADS ** -0.5),
        "norm_final_g": gain(ks[22], (D_MODEL,)),
    }

def second_block(x, norm_mix_g, w_in, conv_w, conv_b, rg_wa, rg_ba, rg_wx, rg_bx, rg_lambda,
              kv_norm_g, w_uk, w_uv, idx_ln_g, idx_ln_b, w_o, norm_ffn_g, peer_wq,
              peer_keys1, peer_keys2, peer_u, peer_v, norm_final_g):
    bsz, s, _ = x.shape
    split_points = [int(p) for p in np.cumsum(SPLITS_2)[:-1]]
    for l in range(DEPTH):
        h = rmsnorm(x, norm_mix_g[l])
        proj = h @ w_in[l]
        xr, q, ckv, qi, ki, wi, gr, ga = jnp.split(proj, split_points, axis=-1)
        y_rnn = rg_lru(causal_conv(xr, conv_w[l], conv_b[l]),
                       rg_wa[l], rg_ba[l], rg_wx[l], rg_bx[l], rg_lambda[l])
        ckv = rmsnorm(ckv, kv_norm_g[l])
        ki = layernorm(ki, idx_ln_g[l], idx_ln_b[l])
        wi = wi * IDX_HEADS ** -0.5
        y_attn = dsa_attention(q.reshape(bsz, s, N_HEADS, HEAD_DIM_2), ckv,
                               qi.reshape(bsz, s, IDX_HEADS, IDX_DIM), ki, wi, w_uk[l], w_uv[l])
        mixed = jax.nn.sigmoid(gr) * y_rnn + jax.nn.sigmoid(ga) * y_attn
        x = x + mixed @ w_o[l]
        x = x + peer(rmsnorm(x, norm_ffn_g[l]), peer_wq[l], peer_keys1[l], peer_keys2[l],
                     peer_u[l], peer_v[l])
    return rmsnorm(x, norm_final_g)


def setup_inputs(seed=0):
    out = dict(first_inputs(seed))
    for name, value in second_inputs(seed + 1).items():
        if name != "x":
            out[name + "_2"] = value
    return out


def reference(
    x, p, norm_gain, w_in, q_norm_gain, k_norm_gain, attn_sinks, conv_w, w_out,
    ple_gate_norm_gain, w_ple_gate, b_ple_gate, w_ple_proj, ple_norm_gain, norm_mix_g_2, w_in_2,
    conv_w_2, conv_b_2, rg_wa_2, rg_ba_2, rg_wx_2, rg_bx_2, rg_lambda_2, kv_norm_g_2, w_uk_2,
    w_uv_2, idx_ln_g_2, idx_ln_b_2, w_o_2, norm_ffn_g_2, peer_wq_2, peer_keys1_2, peer_keys2_2,
    peer_u_2, peer_v_2, norm_final_g_2,
):
    x = first_block(
        x, p, norm_gain, w_in, q_norm_gain, k_norm_gain, attn_sinks, conv_w, w_out,
        ple_gate_norm_gain, w_ple_gate, b_ple_gate, w_ple_proj, ple_norm_gain,
    )
    return second_block(
        x, norm_mix_g_2, w_in_2, conv_w_2, conv_b_2, rg_wa_2, rg_ba_2, rg_wx_2, rg_bx_2,
        rg_lambda_2, kv_norm_g_2, w_uk_2, w_uv_2, idx_ln_g_2, idx_ln_b_2, w_o_2, norm_ffn_g_2,
        peer_wq_2, peer_keys1_2, peer_keys2_2, peer_u_2, peer_v_2, norm_final_g_2,
    )


_drawn_inputs = setup_inputs


def setup_inputs(seed=0):
    import zlib

    import numpy as np

    out = dict(_drawn_inputs(seed))
    spreads = {}
    factors = {'q_norm_gain': 8.0,
     'k_norm_gain': 7.057,
     'attn_sinks': 53.744,
     'ple_gate_norm_gain': 4.661,
     'b_ple_gate': 6.616,
     'ple_norm_gain': 2.919,
     'rg_ba_2': 19.215,
     'rg_bx_2': 11.25,
     'kv_norm_g_2': 3.786,
     'idx_ln_g_2': 2.86,
     'idx_ln_b_2': 4.422,
     'conv_b_2': 3.045,
     'norm_ffn_g_2': 3.527}
    for name, (base, spread) in spreads.items():
        noise = np.random.default_rng([zlib.crc32(name.encode()), seed]).standard_normal(out[name].shape)
        drawn = base * np.exp(spread * noise) if base else spread * noise
        out[name] = __import__('jax').numpy.asarray(drawn.astype(out[name].dtype))
    for name, factor in factors.items():
        out[name] = (out[name] * factor).astype(out[name].dtype)
    return out
```

```python
from contextlib import ExitStack, contextmanager

import numpy as np

import concourse.bass as bass
from concourse import mybir

F32 = mybir.dt.float32
F32R = mybir.dt.float32r
U32 = mybir.dt.uint32
ALU = mybir.AluOpType
ACT = mybir.ActivationFunctionType
X_AXIS = mybir.AxisListType.X

P = 128
S = 256
TT = S // P
D = 2048
KT = D // P
UNIT = 1024
SLOTS = 4
EPS = 1e-6
NEG = -1e30
TAKEN = -3e38

QH, KVH, HD = 16, 4, 64
GROUP = QH // KVH
ATTN_W = QH * HD
KV_W = KVH * HD
QKVG_W = 2 * ATTN_W + 2 * KV_W
CONV_J = (D - ATTN_W) // P
ROT = HD // 4
HALF = ROT // 2

H2 = 16
RANK = 512
RT = RANK // P
IH, ID = 16, 64
TOPK = min(256, S // 4)
PH, PK = 8, 16
KEYS = 128
NB = KEYS
SLOT_N = PH * PK

PARTS = [("ple", 2), ("qkvg", 4 * QKVG_W // 512), ("conv", 4 * CONV_J), ("w_out", 16), ("gate", 16),
         ("ckv", 4), ("kiwi", 2), ("qi", IH * ID // P), ("rnn", 2 * KT), ("heads", 2 * H2), ("w_o", 16),
         ("wqu", 4 * PH), ("u_decode", 2 * PH), ("u_gates", S // 8), ("u_late", NB // 2), ("v", NB)]
EARLY = NB // 2
FIRST = {}
_n = 0
for _name, _count in PARTS:
    FIRST[_name] = _n
    _n += _count
PAIRS = _n
UNITS = 2 * PAIRS

CONST = {}
_n = 0
for _name, _count in [("ident", P), ("iota", P), ("band", TT * 2 * P), ("causal", TT * S), ("cos", TT * HALF),
                      ("sin", TT * HALF)]:
    CONST[_name] = (_n, _n + _count)
    _n += _count
CONST_W = _n
PARAM = {}
_n = 0
for _name, _count in [("norm_gain", KT), ("gate_gain", KT), ("mix_gain", KT), ("ffn_gain", KT),
                      ("conv_w", CONV_J * 3), ("conv_w2", KT * 4), ("conv_b2", KT), ("ba", KT), ("bx", KT),
                      ("lam", KT), ("kv_gain", RT), ("q_gain", HD), ("k_gain", HD), ("sinks", QH),
                      ("idx_g", ID), ("idx_b", ID)]:
    PARAM[_name] = (_n, _n + _count)
    _n += _count
PARAM_W = _n


class Steps:

    def __init__(self, eng, sem):
        self.eng, self.sem, self.n, self.offset = eng, sem, 0, 0

    def __call__(self, instruction):
        instruction.then_inc(self.sem, 1)
        self.n += 1

    def wait(self):
        self.eng.wait_ge(self.sem, self.offset + self.n)

    @contextmanager
    def turns(self, i, per, count):
        base = self.n
        self.offset = i * per
        yield
        assert self.n - base == per, (self.n - base, per)
        self.offset = 0
        self.n = base + per * count


def build(nc, stream, x, p_t, rows, consts, params, rg_w, ukv, keys_t, out):
    ctx = ExitStack()
    with ctx:
        def sb(name, shape, dt=F32):
            return ctx.enter_context(nc.sbuf_tensor(name, shape, dt))

        def sem(name):
            return ctx.enter_context(nc.semaphore(name))

        raw = sb("raw", [P, SLOTS, UNIT])
        w_hi = sb("w_hi", [P, SLOTS, UNIT], F32R)
        w_lo = sb("w_lo", [P, SLOTS, UNIT], F32R)
        act_hi = sb("act_hi", [P, KT, S], F32R)
        act_lo = sb("act_lo", [P, KT, S], F32R)
        big = sb("big", [P, NB * S])
        cst = sb("cst", [P, CONST_W])
        par = sb("par", [P, PARAM_W])
        slot_t = sb("slot_t", [P, 3, S])
        hot = sb("hot", [P, 2, 4, P])
        stat = sb("stat", [P, 176])
        banks = [ctx.enter_context(nc.psum_tensor(f"bank{i}", [P, 512], F32)) for i in range(8)]
        x_kept = nc.dram_tensor("x_kept", (P, TT * D), F32, kind="Internal").ap()
        z_kept = nc.dram_tensor("z_kept", (EARLY, P, S), F32, kind="Internal").ap()

        def at(lo, n):
            return big[:, lo:lo + n]

        def c(name):
            return cst[:, CONST[name][0]:CONST[name][1]]

        def pa(name):
            return par[:, PARAM[name][0]:PARAM[name][1]]

        ident = c("ident")
        iota = c("iota")

        X = at(0, TT * D).rearrange("p (t n) -> p t n", t=TT)
        E = at(4096, TT * D).rearrange("p (t n) -> p t n", t=TT)
        XN = at(8192, TT * D).rearrange("p (t n) -> p t n", t=TT)
        ZT = at(12288, TT * QKVG_W).rearrange("p (t n) -> p t n", t=TT)
        ple_row = at(12288, D)
        gate_row = at(12288, D)
        MIXT = at(17408, KT * S).rearrange("p (k n) -> p k n", k=KT)
        PT = at(17408, 2 * S)
        QT = at(21504, 8 * S).rearrange("p (k n) -> p k n", k=8)
        KTP = at(23552, KVH * 3 * P).rearrange("p (k n) -> p k n", k=KVH)
        VP = at(25088, 3 * KV_W).rearrange("p (k n) -> p k n", k=3)
        KD = at(25856, TT * KVH * 2 * HD)
        YM = at(26880, TT * ATTN_W).rearrange("p (t n) -> p t n", t=TT)
        SC = at(28928, GROUP * 2 * P)
        ET = at(29952, GROUP * 2 * P)
        SC_G = [at(28928, 512), at(29440, 512)]
        QST = at(30976, 2 * P).rearrange("p (k n) -> p k n", k=2)
        KST = at(31232, 2 * P)
        CC = at(31488, S)
        CU = at(31744, S + 4)
        CY = at(32004, S)
        CG = at(32260, S)
        MIX2 = at(4096, KT * S).rearrange("p (k n) -> p k n", k=KT)
        RGW = at(8192, KT * 2 * P).rearrange("p (k n) -> p k n", k=KT)
        RA = at(12288, KT * S).rearrange("p (k n) -> p k n", k=KT)
        RW = at(16384, KT * S).rearrange("p (k n) -> p k n", k=KT)
        RX = at(20480, KT * S).rearrange("p (k n) -> p k n", k=KT)
        QT2 = at(24576, H2 * S).rearrange("p (k n) -> p k n", k=H2)
        CKV = at(28672, TT * RANK).rearrange("p (t n) -> p t n", t=TT)
        UKV = at(28672, 8 * P).rearrange("p (k n) -> p k n", k=8)
        CKVT = at(29696, RT * S).rearrange("p (k n) -> p k n", k=RT)
        ISC = at(30720, TT * S).rearrange("p (t n) -> p t n", t=TT)
        AMASK = at(31232, TT * S)
        KW = at(31744, TT * P).rearrange("p (t n) -> p t n", t=TT)
        KID = at(32000, TT * P).rearrange("p (t n) -> p t n", t=TT)
        KIT = at(32256, S)
        IWORK = at(12288, TT * S).rearrange("p (t n) -> p t n", t=TT)
        QIS = at(13312, 2 * S).rearrange("p (k n) -> p k n", k=2)
        REL = at(14336, 4 * S).rearrange("p (k n) -> p k n", k=4)
        XP = at(4096, S + 4)
        XC = at(4400, S)
        RI = at(4700, 2 * S)
        TH = at(5300, S)
        THD = at(5600, S)
        WST = at(5900, 2 * P)
        KTS = at(8192, S)
        VS = at(8448, S).rearrange("p (k n) -> p k n", k=2)
        LG = at(8704, TT * S).rearrange("p (t n) -> p t n", t=TT)
        PTS = at(9216, 2 * S)
        TG = at(9728, S)
        TA = at(9984, S)
        QS2 = at(10240, S)
        HU = at(10496, S)
        YH = at(10752, S)
        PQS = at(12288, 2 * S).rearrange("p (k n) -> p k n", k=2)
        PS = at(12800, 2 * 2 * P).rearrange("p (a t n) -> p a t n", a=2, t=TT)
        V12 = at(13312, 2 * PH * TT * PK).rearrange("p (h a t k) -> p h a t k", h=PH, a=2, t=TT)
        I12 = at(13824, 2 * PH * TT * PK).bitcast(U32).rearrange("p (h a t k) -> p h a t k", h=PH, a=2, t=TT)
        CAND = at(14336, TT * PK * PK).rearrange("p (t n) -> p t n", t=TT)
        CV = at(14848, PH * TT * PK).rearrange("p (h t k) -> p h t k", h=PH, t=TT)
        CP = at(15104, PH * TT * PK).bitcast(U32).rearrange("p (h t k) -> p h t k", h=PH, t=TT)
        I12F = at(15360, 2 * PH * TT * PK).rearrange("p (h a t k) -> p h a t k", h=PH, a=2, t=TT)
        CA = at(15872, 2 * SLOT_N * TT).rearrange("p (a n) -> p a n", a=2)
        CAU = at(16384, 2 * SLOT_N * TT).bitcast(U32).rearrange("p (a n) -> p a n", a=2)
        PICK = at(16896, 3 * SLOT_N * TT).rearrange("p (a h t k) -> p a h t k", a=3, h=PH, t=TT)
        PICKT = at(17664, 3 * SLOT_N * TT).rearrange("p (a t h k) -> p a t h k", a=3, h=PH, t=TT)
        EQ = at(18432, SLOT_N * TT * PK)
        KEYT = at(22528, 2 * KEYS).rearrange("p (a n) -> p a n", a=2)

        G = big[:, :].rearrange("p (b t) -> p b t", b=NB)
        GZ = c("band").rearrange("p (s n) -> p s n", s=2)
        GB = c("causal").rearrange("p (s n) -> p s n", s=2)
        XF = raw[:, :, :].rearrange("p a b -> p (a b)").rearrange("p (t n) -> p t n", t=TT)
        final_row = at(0, D)
        OUT = at(4096, TT * D).rearrange("p (t n) -> p t n", t=TT)
        SQ = at(8192, TT * D).rearrange("p (t n) -> p t n", t=TT)

        ss = stat[:, 0:2]
        std = stat[:, 2:4]
        rstd = stat[:, 4:6]
        ss40 = stat[:, 8:48]
        nsink = stat[:, 48:64]
        mx = stat[:, 64:68]
        nm = stat[:, 68:72]
        dsink = stat[:, 72:76]
        esum = stat[:, 76:80]
        esink = stat[:, 80:84]
        rec = stat[:, 84:88]
        sp_a = stat[:, 88:104]
        sp_b = stat[:, 104:120]
        sp_c = stat[:, 120:136]
        nba = stat[:, 136:152]
        nbx = stat[:, 152:168]
        top8 = stat[:, 168:176]
        csum = stat[:, 88:104]
        crec = stat[:, 104:120]
        idx8 = stat[:, 8:16]
        c_pos = sp_a
        c_neg = sp_b

        raw_ready = [sem(f"raw_ready{i}") for i in range(SLOTS)]
        hi_ready = sem("hi_ready")
        lo_ready = sem("lo_ready")
        unit_done = sem("unit_done")
        const_ready = sem("const_ready")
        x_ready = sem("x_ready")
        pt_ready = sem("pt_ready")
        ple_row_ready = sem("ple_row_ready")
        gate_row_ready = sem("gate_row_ready")
        rgw_ready = sem("rgw_ready")
        keys_ready = sem("keys_ready")
        ukv_ready = sem("ukv_ready")
        final_ready = sem("final_ready")
        xf_ready = sem("xf_ready")
        x_saved = sem("x_saved")
        out_saved = sem("out_saved")
        v_step = sem("vector_step")
        s_step = sem("scalar_step")
        g_step = sem("gpsimd_step")
        squares = sem("squares")
        mean_ready = sem("mean_ready")
        std_ready = sem("std_ready")
        normed = sem("normed")
        turned = sem("turned")
        act_hi_ready = sem("act_hi_ready")
        act_lo_ready = sem("act_lo_ready")
        ple_done = sem("ple_done")
        ple_taken = sem("ple_taken")
        qkvg_taken_s = [sem(f"qkvg_taken_s{n}") for n in range(2)]
        qkvg_taken_v = [sem(f"qkvg_taken_v{n}") for n in range(2)]
        qk_squares = sem("qk_squares")
        silu_tanh = sem("silu_tanh")
        qk_mean = sem("qk_mean")
        qk_std = sem("qk_std")
        qk_ready = sem("qk_ready")
        qk_turned = sem("qk_turned")
        qk_kept = sem("qk_kept")
        conv_gate = sem("conv_gate")
        conv_gate_used = sem("conv_gate_used")
        conv_c = sem("conv_c")
        conv_h_used = sem("conv_h_used")
        conv_b_used = sem("conv_b_used")
        staged = sem("staged")
        scored = sem("scored")
        sc_masked = sem("sc_masked")
        sc_max = sem("sc_max")
        exps = sem("exps")
        probs_turned = sem("probs_turned")
        probs_kept = sem("probs_kept")
        mixed = sem("mixed")
        mix_used = sem("mix_used")
        ym_turned = sem("ym_turned")
        added = [sem(f"added{n}") for n in range(2)]
        gate_pre = sem("gate_pre")
        gate_tanh = sem("gate_tanh")
        gated = [sem(f"gated{n}") for n in range(2)]
        ckv_kept = sem("ckv_kept")
        kw_kept = sem("kw_kept")
        ckv_squares = sem("ckv_squares")
        ckv_mean = sem("ckv_mean")
        ckv_std = sem("ckv_std")
        ckv_normed = sem("ckv_normed")
        ki_ready = sem("ki_ready")
        ckv_turned = sem("ckv_turned")
        ckvt_kept = sem("ckvt_kept")
        qi_kept = sem("qi_kept")
        qi_scored = sem("qi_scored")
        rel_ready = sem("rel_ready")
        rel_used = sem("rel_used")
        xr_kept = sem("xr_kept")
        xc_ready = sem("xc_ready")
        w_staged = sem("w_staged")
        rg_done = sem("rg_done")
        rg_exp = sem("rg_exp")
        r_ready = sem("r_ready")
        a_ready = sem("a_ready")
        q2_kept = sem("q2_kept")
        th_used = sem("th_used")
        softplus_ready = sem("softplus_ready")
        rw_root = sem("rw_root")
        rw_ready = sem("rw_ready")
        gr_tanh = sem("gr_tanh")
        ga_tanh = sem("ga_tanh")
        gr_used = sem("gr_used")
        k_made = sem("k_made")
        v_made = sem("v_made")
        k_kept = sem("k_kept")
        v_kept = sem("v_kept")
        q_staged = sem("q_staged")
        logits_made = sem("logits_made")
        logits_masked = sem("logits_masked")
        max_ready = sem("max_ready")
        p_exp = sem("p_exp")
        p_ready = sem("p_ready")
        p_turned = sem("p_turned")
        p_kept = sem("p_kept")
        y_made = sem("y_made")
        head_mixed = sem("head_mixed")
        pq_kept = [sem(f"pq_kept{n}") for n in range(2)]
        ps_made = [sem(f"ps_made{n}") for n in range(2)]
        ps_kept = [sem(f"ps_kept{n}") for n in range(2)]
        ps_used = [sem(f"ps_used{n}") for n in range(2)]
        pick_diff = sem("pick_diff")
        pick_exp = sem("pick_exp")
        picks_ready = sem("picks_ready")
        picks_turned = sem("picks_turned")
        slots_kept = sem("slots_kept")
        hot_turn = sem("hot_turn")
        hot1 = sem("hot1")
        hot2 = sem("hot2")
        hot_used = [sem(f"hot_used{n}") for n in range(4)]
        gate_kept = [sem(f"gate_kept{n}") for n in range(2)]
        gelu_ready = [sem(f"gelu_ready{n}") for n in range(2)]
        z_saved = [sem(f"z_saved{n}") for n in range(2)]
        z_back = [sem(f"z_back{n}") for n in range(2)]
        early_ready = [sem(f"early_ready{n}") for n in range(2)]
        act_ready = [sem(f"act_ready{n}") for n in range(2)]
        eh_ready = sem("eh_ready")
        el_ready = sem("el_ready")
        y_added = sem("y_added")
        fin_squares = sem("fin_squares")
        fin_mean = sem("fin_mean")
        fin_std = sem("fin_std")
        fin_ready = sem("fin_ready")

        def unit_slot(odd, u):
            return 2 * odd + u

        def split_hi(act, pair, half, odd, first=False, units=(0, 1)):
            for u in units:
                s = unit_slot(odd, u)
                act.wait_ge(raw_ready[s], 16 * half + 16)
                if not first:
                    act.wait_ge(unit_done, 2 * pair + u - 3)
                act.activation(w_hi[:, s, :], raw[:, s, :], ACT.Copy).then_inc(hi_ready, 1)

        def split_lo(dve, pair, half, odd, first=False, units=(0, 1)):
            for u in units:
                s = unit_slot(odd, u)
                dve.wait_ge(hi_ready, 2 * pair + u + 1)
                if not first:
                    dve.wait_ge(unit_done, 2 * pair + u - 3)
                dve.tensor_tensor(w_lo[:, s, :], raw[:, s, :], w_hi[:, s, :].bitcast(F32),
                                  ALU.subtract).then_inc(lo_ready, 1)

        def ahead(split, eng, part, i, per, k, units=(0, 1)):
            base = FIRST[part] + k + 2
            split(eng, i * per + base, i * (per // 2) + base // 2, base % 2, units=units)

        def pair_of(part, i, per, k):
            return i * per + (FIRST[part] + k)

        def columns_out(pe, pair, odd, out_ap, units=(0, 1)):
            for u in units:
                s = unit_slot(odd, u)
                pe.wait_ge(lo_ready, 2 * pair + u + 1)
                for kk in range(8):
                    k = 8 * u + kk
                    hi = w_hi[:, s, kk * P:(kk + 1) * P]
                    lo = w_lo[:, s, kk * P:(kk + 1) * P]
                    pe.matmul(out_ap, hi, act_hi[:, k, :], start=(k == 0), stop=False)
                    pe.matmul(out_ap, hi, act_lo[:, k, :], start=False, stop=False)
                    mm = pe.matmul(out_ap, lo, act_hi[:, k, :], start=False, stop=(k == KT - 1))
                mm.then_inc(unit_done, 1)

        def tokens_out(pe, part, i, per, k0, outs):
            for uu in range(8):
                pair = pair_of(part, i, per, k0 + uu // 2)
                s = unit_slot((FIRST[part] + k0 + uu // 2) % 2, uu % 2)
                pe.wait_ge(lo_ready, 2 * pair + uu % 2 + 1)
                for kk in range(2):
                    k = 2 * uu + kk
                    hi = w_hi[:, s, kk * 512:(kk + 1) * 512]
                    lo = w_lo[:, s, kk * 512:(kk + 1) * 512]
                    for t in range(TT):
                        a_hi = act_hi[:, k, t * P:(t + 1) * P]
                        a_lo = act_lo[:, k, t * P:(t + 1) * P]
                        pe.matmul(outs[t], a_hi, hi, start=(k == 0), stop=False)
                        pe.matmul(outs[t], a_hi, lo, start=False, stop=False)
                        mm = pe.matmul(outs[t], a_lo, hi, start=False, stop=(k == KT - 1))
                mm.then_inc(unit_done, 1)

        primed = [z_saved, early_ready, scored, rg_done, logits_made, hot2, hot_used, conv_b_used, conv_h_used, conv_gate_used, qi_scored, rel_used, xc_ready, th_used, gr_used, head_mixed, ps_made, ps_used, act_ready, qkvg_taken_s, qkvg_taken_v, probs_kept, mix_used, added, gated, rel_ready, xr_kept, q2_kept, rg_exp, k_kept, v_kept, p_exp, ga_tanh, p_kept, ps_kept, gate_kept, gelu_ready]

        block = ctx.enter_context(nc.Block())

        @block.sync
        def _(sp):
            def load(n, turn, s):
                sp.dma_start(raw[:, s, :], stream[bass.ds(n, 1), :, :].rearrange("o p n -> (o p) n"))\
                  .then_inc(raw_ready[s], 16)

            for s in range(SLOTS):
                sp.dma_start(raw[:, s, :], stream[s, :, :]).then_inc(raw_ready[s], 16)
            with sp.Fori(1, UNITS // SLOTS) as q:
                for s in range(SLOTS):
                    sp.wait_ge(lo_ready, q * SLOTS + (s + 1 - SLOTS))
                    load(q * SLOTS + s, q, s)
            sp.wait_ge(lo_ready, UNITS)
            sp.wait_ge(x_saved, 16)
            sp.dma_start(XF, x_kept.rearrange("p (t n) -> p t n", t=TT)).then_inc(xf_ready, 16)
            sp.wait_ge(fin_ready, 2)
            sp.dma_start(out.rearrange("a (t p) n -> p (a t) n", p=P), OUT).then_inc(out_saved, 16)
            sp.wait_ge(out_saved, 16)

        @block.gpsimd
        def _(pool):
            step = Steps(pool, g_step)
            for one in primed:
                for each in one if isinstance(one, list) else [one]:
                    pool.sem_inc(each, 1)
            with pool.Fori(0, TT) as t:
                with pool.Fori(0, KVH) as g:
                    u = t * KVH + g
                    pool.wait_ge(qk_kept, 16)
                    pool.wait_ge(scored, u + 1)
                    pool.tensor_copy(QST, QT[:, bass.ds(2 * g, 2), bass.ds(t * P, P)]).then_inc(staged, 1)
                    pool.tensor_copy(KST, KTP[:, bass.ds(g, 1), bass.ds(t * P, 2 * P)]
                                     .rearrange("p o n -> p (o n)")).then_inc(staged, 1)
            with pool.Fori(0, KT) as j:
                pool.wait_ge(rgw_ready, 16)
                pool.wait_ge(rg_done, j + 1)
                pool.tensor_copy(WST, RGW[:, bass.ds(j, 1), :].rearrange("p o n -> p (o n)")).then_inc(w_staged, 1)
            pool.wait_ge(q2_kept, H2 + 1)
            with pool.Fori(0, H2) as h:
                pool.wait_ge(logits_made, h + 1)
                pool.tensor_copy(QS2, QT2[:, bass.ds(h, 1), :].rearrange("p o n -> p (o n)")).then_inc(q_staged, 1)
            pool.wait_ge(slots_kept, 3)

            with pool.Fori(0, S // 8) as i:
                pool.wait_ge(hot2, i * 8 + 1)
                pool.tensor_copy(idx8, slot_t[:, 1, bass.ds(i * 8, 8)]).then_inc(g_step, 1)
                pool.wait_ge(g_step, i + 1)
                for s in range(8):
                    pool.wait_ge(hot_used[s % 4], i * 2 + s // 4 + 1)
                    pool.sem_inc(hot_turn, 1)
                    pool.tensor_scalar(hot[:, 1, s % 4, :], iota, idx8[:, s:s + 1], None, ALU.is_equal)\
                        .then_inc(hot2, 1)

        @block.scalar
        def _(act):
            step = Steps(act, s_step)
            act.dma_start(PT, p_t).then_inc(pt_ready, 16)
            act.dma_start(cst[:, :], consts).then_inc(const_ready, 16)
            act.dma_start(par[:, :], params).then_inc(const_ready, 16)
            act.dma_start(X, x.rearrange("a (t p) n -> p (a t) n", p=P)).then_inc(x_ready, 16)
            act.dma_start(ple_row, rows[0, :, :]).then_inc(ple_row_ready, 16)

            def square_sums(i, src):
                if i:
                    act.wait_ge(std_ready, i)
                for t in range(TT):
                    act.activation(XN[:, t, :], src[:, t, :], ACT.Square, accum_out=ss[:, t:t + 1])\
                       .then_inc(squares, 1)
                act.wait_ge(mean_ready, i + 1)
                act.activation(std, ss, ACT.Sqrt).then_inc(std_ready, 1)

            def keep_hi(n, gain):
                for k in range(KT):
                    act.wait_ge(turned, n * KT + k + 1)
                    act.activation(act_hi[:, k, :], banks[k % 8][:, 0:S], ACT.Copy, scale=gain[:, k:k + 1])\
                       .then_inc(act_hi_ready, 1)

            act.wait_ge(pt_ready, 16)
            act.activation(act_hi[:, 0:2, :].rearrange("p k n -> p (k n)"), PT, ACT.Copy).then_inc(ple_taken, 1)
            split_hi(act, 0, 0, 0, first=True)
            split_hi(act, 1, 0, 1, first=True)
            ahead(split_hi, act, "ple", 0, 2, 0)
            ahead(split_hi, act, "ple", 0, 2, 1)
            for cb in range(4):
                act.wait_ge(unit_done, cb + 1)
                act.activation(E[:, 0, cb * 512:(cb + 1) * 512], banks[2 * cb][:, :], ACT.Copy).then_inc(ple_taken, 1)
                act.activation(E[:, 1, cb * 512:(cb + 1) * 512], banks[2 * cb + 1][:, :], ACT.Copy)\
                   .then_inc(ple_taken, 1)
            act.wait_ge(ple_taken, 9)
            square_sums(0, E)
            act.wait_ge(x_ready, 16)
            square_sums(1, X)
            act.wait_ge(const_ready, 32)
            keep_hi(0, pa("norm_gain"))

            def take_qkvg(c_, i, per, k0, n):
                for k in range(4):
                    ahead(split_hi, act, "qkvg", i, per, k0 + k)
                act.wait_ge(unit_done, 2 * pair_of("qkvg", i, per, k0 + 3) + 2)
                act.activation(ZT[:, 0, bass.ds(c_ * 512, 512)], banks[2 * n][:, :], ACT.Copy)\
                   .then_inc(qkvg_taken_s[n], 1)

            act.wait_ge(normed, 1)
            with act.Fori(0, 2) as i:
                take_qkvg(i * 2, i, 8, 0, 0)
                take_qkvg(i * 2 + 1, i, 8, 4, 1)
            take_qkvg(4, 0, 8, 16, 0)
            for n in range(2):
                act.wait_ge(qkvg_taken_s[n], 3 - n + 1)
                act.wait_ge(qkvg_taken_v[n], 3 - n + 1)
            for t in range(TT):
                act.activation(XN[:, t, 0:1280], ZT[:, t, 0:1280], ACT.Square).then_inc(qk_squares, 1)
            act.wait_ge(qk_mean, 1)
            act.activation(ss40, ss40, ACT.Sqrt).then_inc(qk_std, 1)
            act.activation(YM, ZT[:, :, 1536:2560], ACT.Tanh, scale=0.5).then_inc(silu_tanh, 1)
            act.wait_ge(qk_turned, 16)
            for k in range(8):
                act.activation(QT[:, k, :], banks[k // 2][:, (k % 2) * S:(k % 2 + 1) * S], ACT.Copy).then_inc(qk_kept, 1)
            act.wait_ge(qk_turned, 24)
            for g in range(KVH):
                for t in range(TT):
                    act.activation(KTP[:, g, (t + 1) * P:(t + 2) * P],
                                   banks[4 + g // 2][:, (g % 2) * S + t * P:(g % 2) * S + (t + 1) * P],
                                   ACT.Copy).then_inc(qk_kept, 1)

            with act.Fori(0, CONV_J) as j:
                ahead(split_hi, act, "conv", j, 4, 0)
                act.wait_ge(unit_done, 2 * pair_of("conv", j, 4, 0) + 2)
                act.wait_ge(conv_b_used, j + 1)
                act.activation(CG, banks[0][:, 0:S], ACT.Tanh, scale=0.5).then_inc(conv_gate, 1)
                act.wait_ge(sc_max, j + 1)
                for h in range(GROUP):
                    act.activation(SC[:, h * S:(h + 1) * S], SC[:, h * S:(h + 1) * S], ACT.Exp,
                                   bias=nm[:, h:h + 1], accum_out=esum[:, h:h + 1]).then_inc(exps, 1)
                act.activation(esink, dsink, ACT.Exp).then_inc(exps, 1)
                ahead(split_hi, act, "conv", j, 4, 1)
                act.wait_ge(unit_done, 2 * pair_of("conv", j, 4, 1) + 2)
                act.wait_ge(conv_h_used, j + 1)
                act.activation(CC, banks[1][:, 0:S], ACT.Copy).then_inc(conv_c, 1)
                act.wait_ge(probs_turned, j + 1)
                act.activation(ET[:, 0:512], banks[6][:, :], ACT.Copy).then_inc(probs_kept, 1)
                act.activation(ET[:, 512:1024], banks[7][:, :], ACT.Copy).then_inc(probs_kept, 1)
                ahead(split_hi, act, "conv", j, 4, 2)
                ahead(split_hi, act, "conv", j, 4, 3)

            for k in range(8):
                act.wait_ge(ym_turned, k + 1)
                act.activation(act_hi[:, k, :], banks[k][:, 0:S], ACT.Copy).then_inc(act_hi_ready, 1)
            act.activation(act_hi[:, 8:16, :], MIXT[:, 8:16, :], ACT.Copy).then_inc(act_hi_ready, 8)

            def only_split(part, turns):
                with act.Fori(0, turns) as i:
                    for k in range(8):
                        ahead(split_hi, act, part, i, 8, k)

            act.dma_start(gate_row, rows[1, :, :]).then_inc(gate_row_ready, 16)
            only_split("w_out", 2)
            for n in range(2):
                act.wait_ge(added[n], 5)
            square_sums(2, X)
            keep_hi(1, pa("gate_gain"))
            with act.Fori(0, 2) as i:
                for n in range(2):
                    for k in range(4):
                        ahead(split_hi, act, "gate", i, 8, 4 * n + k)
                    for t in range(TT):
                        act.wait_ge(gate_pre, i * 4 + 2 * n + t + 1)
                        act.activation(SC_G[t], SC_G[t], ACT.Tanh, scale=0.5).then_inc(gate_tanh, 1)
            for n in range(2):
                act.wait_ge(gated[n], 5)
            square_sums(3, X)
            keep_hi(2, pa("mix_gain"))

            act.dma_start(RGW, rg_w).then_inc(rgw_ready, 16)
            for k in range(4):
                ahead(split_hi, act, "ckv", 0, 4, k)
            act.wait_ge(unit_done, 2 * pair_of("ckv", 0, 4, 3) + 2)
            for t in range(TT):
                act.activation(CKV[:, t, :], banks[t][:, :], ACT.Copy).then_inc(ckv_kept, 1)
            for k in range(2):
                ahead(split_hi, act, "kiwi", 0, 2, k)
            act.wait_ge(unit_done, 2 * pair_of("kiwi", 0, 2, 0) + 2)
            for t in range(TT):
                act.activation(KW[:, t, 0:80], banks[2 + t][:, 0:80], ACT.Copy).then_inc(kw_kept, 1)
            act.wait_ge(ckv_kept, 2)
            for t in range(TT):
                act.activation(REL[:, 2 * t:2 * t + 2, :].rearrange("p a n -> p (a n)"), CKV[:, t, :], ACT.Square,
                               accum_out=ss[:, t:t + 1]).then_inc(ckv_squares, 1)
            act.wait_ge(ckv_mean, 1)
            act.activation(stat[:, 8:12], stat[:, 8:12], ACT.Sqrt).then_inc(ckv_std, 1)
            for k in range(RT):
                act.wait_ge(ckv_turned, 2 * (k // 2) + 2)
                act.activation(CKVT[:, k, :], banks[4 + k // 2][:, (k % 2) * S:(k % 2 + 1) * S], ACT.Copy,
                               scale=pa("kv_gain")[:, k:k + 1]).then_inc(ckvt_kept, 1)
            act.wait_ge(ckv_turned, RT + 1)
            act.activation(KIT, banks[6][:, 0:S], ACT.Copy).then_inc(ckvt_kept, 1)

            with act.Fori(0, IH // 4) as i:
                for n in range(2):
                    ahead(split_hi, act, "qi", i, 2, n)
                    act.wait_ge(unit_done, 2 * pair_of("qi", i, 2, n) + 2)
                    act.wait_ge(qi_scored, i * 2 + n + 1)
                    act.activation(QIS[:, n, :], banks[n][:, 0:S], ACT.Copy).then_inc(qi_kept, 1)
                    act.wait_ge(qi_scored, i * 2 + n + 2)
                    act.wait_ge(rel_used, i * 8 + 4 * n + 1)
                    for b in range(2):
                        act.activation(REL[:, 2 * b:2 * b + 2, :].rearrange("p a n -> p (a n)"), banks[4 + b][:, :],
                                       ACT.Relu, scale=ID ** -0.5).then_inc(rel_ready, 1)

            act.wait_ge(softplus_ready, 1)
            act.activation(sp_b, sp_a, ACT.Exp, scale=-1.0).then_inc(softplus_ready, 1)
            act.wait_ge(softplus_ready, 3)
            with act.Fori(0, KT) as j:
                ahead(split_hi, act, "rnn", j, 2, 0)
                act.wait_ge(unit_done, 2 * pair_of("rnn", j, 2, 0) + 2)
                act.wait_ge(xc_ready, j + 1)
                act.activation(XP[:, 3:3 + S], banks[0][:, 0:S], ACT.Copy).then_inc(xr_kept, 1)
                ahead(split_hi, act, "rnn", j, 2, 1)
                act.wait_ge(rg_done, j + 2)
                act.wait_ge(th_used, j + 1)
                act.activation(RI[:, 0:S], banks[4][:, 0:S], ACT.Exp, scale=-1.0,
                               bias=nba[:, bass.ds(j, 1)]).then_inc(rg_exp, 1)
                act.activation(RI[:, S:2 * S], banks[4][:, S:2 * S], ACT.Exp, scale=-1.0,
                               bias=nbx[:, bass.ds(j, 1)]).then_inc(rg_exp, 1)
                act.wait_ge(unit_done, 2 * pair_of("rnn", j, 2, 1) + 2)
                act.activation(QT2[:, bass.ds(j, 1), :].rearrange("p o n -> p (o n)"), banks[1][:, 0:S],
                               ACT.Copy).then_inc(q2_kept, 1)
                act.wait_ge(r_ready, j + 1)
                act.activation(RA[:, bass.ds(j, 1), :].rearrange("p o n -> p (o n)"), RI[:, 0:S], ACT.Exp,
                               scale=c_neg[:, bass.ds(j, 1)]).then_inc(a_ready, 1)
                act.activation(TH, RI[:, 0:S], ACT.Tanh, scale=c_pos[:, bass.ds(j, 1)]).then_inc(a_ready, 1)
            act.wait_ge(rw_ready, 1)
            act.activation(RW, RW, ACT.Sqrt).then_inc(rw_root, 1)

            act.wait_ge(ckvt_kept, RT + 1)
            act.dma_start(UKV, ukv[0:1, :, :].rearrange("o p (k n) -> p (o k) n", n=P)).then_inc(ukv_ready, 16)

            def head(h, last=False):
                ahead(split_hi, act, "heads", h, 2, 0)
                act.wait_ge(unit_done, 2 * pair_of("heads", h, 2, 0) + 2)
                act.wait_ge(gr_used, h + 1)
                act.activation(TG, banks[0][:, 0:S], ACT.Tanh, scale=0.5).then_inc(gr_tanh, 1)
                act.wait_ge(k_made, h + 1)
                act.activation(KTS, banks[2][:, 0:S], ACT.Copy).then_inc(k_kept, 1)
                if not last:
                    act.wait_ge(v_made, h + 1)
                    act.dma_start(UKV, ukv[bass.ds(h + 1, 1), :, :].rearrange("o p (k n) -> p (o k) n", n=P))\
                       .then_inc(ukv_ready, 16)
                act.wait_ge(max_ready, h + 1)
                for t in range(TT):
                    act.activation(LG[:, t, :], LG[:, t, :], ACT.Exp, bias=nm[:, t:t + 1],
                                   accum_out=esum[:, t:t + 1]).then_inc(p_exp, 1)
                ahead(split_hi, act, "heads", h, 2, 1)
                act.wait_ge(unit_done, 2 * pair_of("heads", h, 2, 1) + 2)
                act.wait_ge(head_mixed, h + 1)
                act.activation(TA, banks[1][:, 0:S], ACT.Tanh, scale=0.5).then_inc(ga_tanh, 1)
                act.wait_ge(p_turned, h + 1)
                act.activation(PTS, banks[5][:, :], ACT.Copy).then_inc(p_kept, 1)

            with act.Fori(0, H2 - 1) as h:
                head(h)
            head(H2 - 1, last=True)

            act.wait_ge(head_mixed, H2 + 1)
            for k in range(4):
                act.activation(act_hi[:, 4 * k:4 * k + 4, :], MIX2[:, 4 * k:4 * k + 4, :], ACT.Copy)\
                   .then_inc(act_hi_ready, 4)
            only_split("w_o", 2)
            for n in range(2):
                act.wait_ge(added[n], 9)
            act.dma_start(x_kept.rearrange("p (t n) -> p t n", t=TT), X).then_inc(x_saved, 16)
            act.dma_start(KEYT, keys_t).then_inc(keys_ready, 16)
            square_sums(4, X)
            keep_hi(3, pa("ffn_gain"))

            def early(pair, b2, n):
                act.wait_ge(unit_done, 2 * pair + 2)
                act.wait_ge(z_saved[n], b2 * 16 + 1)
                act.activation(GZ[:, n, :], banks[2 + n][:, 0:S], ACT.Gelu).then_inc(gelu_ready[n], 1)
                act.wait_ge(gelu_ready[n], b2 + 2)
                act.dma_start(z_kept[bass.ds(b2 * 2 + n, 1), :, :].rearrange("o p n -> (o p) n"), GZ[:, n, :])\
                   .then_inc(z_saved[n], 16)

            with act.Fori(0, PH) as h:
                def keep_query(a):
                    act.wait_ge(unit_done, 2 * pair_of("wqu", h, 4, a) + 2)
                    act.wait_ge(ps_made[a], h + 1)
                    act.activation(PQS[:, a, :], banks[a][:, 0:S], ACT.Copy).then_inc(pq_kept[a], 1)

                def keep_scores(a):
                    act.wait_ge(ps_made[a], h + 2)
                    act.wait_ge(ps_used[a], h + 1)
                    act.activation(PS[:, a, :, :].rearrange("p t n -> p (t n)"), banks[4 + a][:, 0:S],
                                   ACT.Copy).then_inc(ps_kept[a], 1)

                ahead(split_hi, act, "wqu", h, 4, 0)
                keep_query(0)
                ahead(split_hi, act, "wqu", h, 4, 1)
                keep_query(1)
                keep_scores(0)
                ahead(split_hi, act, "wqu", h, 4, 2)
                early(pair_of("wqu", h, 4, 2), h, 0)
                keep_scores(1)
                ahead(split_hi, act, "wqu", h, 4, 3)
                early(pair_of("wqu", h, 4, 3), h, 1)

            def early_turn(i):
                for n in range(2):
                    ahead(split_hi, act, "u_decode", i, 2, n)
                    early(pair_of("u_decode", i, 2, n), i + PH, n)

            with act.Fori(0, PH // 2) as i:
                early_turn(i)
            act.wait_ge(pick_diff, 1)
            act.activation(CV, CV, ACT.Exp).then_inc(pick_exp, 1)
            with act.Fori(PH // 2, PH) as i:
                early_turn(i)
            for a in range(3):
                act.wait_ge(picks_turned, 2 * a + 2)
                act.activation(slot_t[:, a, :], banks[4 + a][:, 0:S], ACT.Copy).then_inc(slots_kept, 1)
            act.wait_ge(slots_kept, 3)
            act.wait_ge(x_saved, 16)
            with act.Fori(0, S // 16) as i:
                for n in range(2):
                    def keep_gates(m):
                        act.wait_ge(hot_used[3], i * 4 + 2 * n + m + 2)
                        act.activation(G[:, :, bass.ds(i * 16 + (8 * n + 4 * m), 4)],
                                       banks[m][:, :].rearrange("p (t b) -> p b t", t=4), ACT.Copy)\
                           .then_inc(gate_kept[m], 1)

                    ahead(split_hi, act, "u_gates", i, 2, n, units=(0,))
                    keep_gates(0)
                    ahead(split_hi, act, "u_gates", i, 2, n, units=(1,))
                    early(pair_of("u_gates", i, 2, n), i + 2 * PH, n)
                    keep_gates(1)

            for n in range(2):
                act.wait_ge(z_saved[n], 16 * (EARLY // 2) + 1)
            with act.Fori(0, EARLY // 2) as i:
                for n in range(2):
                    ahead(split_hi, act, "u_late", i, 2, n)
                    act.wait_ge(early_ready[n], i + 1)
                    act.dma_start(GB[:, n, :], z_kept[bass.ds(i * 2 + n, 1), :, :].rearrange("o p n -> (o p) n"))\
                       .then_inc(z_back[n], 16)
                    act.wait_ge(unit_done, 2 * pair_of("u_late", i, 2, n) + 2)
                    act.wait_ge(act_ready[n], i + 1)
                    act.activation(GZ[:, n, :], banks[2 + n][:, 0:S], ACT.Gelu).then_inc(gelu_ready[n], 1)

            def expert_hi(b, n, done):
                act.wait_ge(unit_done, done)
                act.activation(act_hi[:, n, :], G[:, bass.ds(b, 1), :].rearrange("p o n -> p (o n)"), ACT.Copy)\
                   .then_inc(eh_ready, 1)

            for n in range(2):
                act.wait_ge(act_ready[n], EARLY // 2 + 1)
                act.wait_ge(early_ready[n], EARLY // 2 + 1)
            for n in range(2):
                expert_hi(n, n, 2 * FIRST["v"])
            with act.Fori(0, NB // 2 - 1) as i:
                for n in range(2):
                    ahead(split_hi, act, "v", i, 2, n)
                    expert_hi(i * 2 + (2 + n), n, 2 * pair_of("v", i, 2, n) + 2)

            act.wait_ge(el_ready, NB)
            act.dma_start(final_row, rows[2, :, :]).then_inc(final_ready, 16)
            act.wait_ge(y_added, 8)
            for t in range(TT):
                act.activation(SQ[:, t, :], XF[:, t, :], ACT.Square, accum_out=ss[:, t:t + 1]).then_inc(fin_squares, 1)
            act.wait_ge(fin_mean, 1)
            act.activation(std, ss, ACT.Sqrt).then_inc(fin_std, 1)

        @block.vector
        def _(dve):
            step = Steps(dve, v_step)
            step(dve.memset(KTP, 0.0))
            step(dve.memset(VP, 0.0))
            step(dve.memset(CU[:, 0:2], 0.0))

            def keep_lo(i, gain):
                for k in range(KT):
                    dve.wait_ge(act_hi_ready, i * KT + k + 1)
                    dve.scalar_tensor_tensor(out=act_lo[:, k, :], in0=banks[k % 8][:, 0:S], scalar=gain[:, k:k + 1],
                                             in1=act_hi[:, k, :].bitcast(F32), op0=ALU.mult, op1=ALU.subtract)\
                       .then_inc(act_lo_ready, 1)

            def root(i, sum_ap, n, std_ap, rstd_ap, squares_, mean_, std_sem, need):
                dve.wait_ge(squares_, need)
                dve.tensor_scalar(sum_ap, sum_ap, 1.0 / n, EPS, ALU.mult, ALU.add).then_inc(mean_, 1)
                dve.wait_ge(std_sem, i + 1)
                step(dve.reciprocal(rstd_ap, std_ap))
                step.wait()

            def norm_rows(i):
                root(i, ss, D, std, rstd, squares, mean_ready, std_ready, TT * (i + 1))

            dve.wait_ge(ple_taken, 1)
            dve.tensor_tensor(act_lo[:, 0:2, :].rearrange("p k n -> p (k n)"), PT,
                              act_hi[:, 0:2, :].rearrange("p k n -> p (k n)").bitcast(F32),
                              ALU.subtract).then_inc(ple_done, 1)
            split_lo(dve, 0, 0, 0, first=True)
            split_lo(dve, 1, 0, 1, first=True)
            ahead(split_lo, dve, "ple", 0, 2, 0)
            ahead(split_lo, dve, "ple", 0, 2, 1)
            norm_rows(0)
            dve.wait_ge(ple_row_ready, 16)
            for t in range(TT):
                ins = dve.scalar_tensor_tensor(out=E[:, t, :], in0=E[:, t, :], scalar=rstd[:, t:t + 1], in1=ple_row,
                                               op0=ALU.mult, op1=ALU.mult)
            ins.then_inc(normed, 1)

            def normed_rows(i, n):
                norm_rows(i)
                for t in range(TT):
                    dve.tensor_scalar(XN[:, t, :], X[:, t, :], rstd[:, t:t + 1], None, ALU.mult).then_inc(normed, 1)

            normed_rows(1, 3)
            dve.wait_ge(const_ready, 32)
            keep_lo(0, pa("norm_gain"))

            def take_qkvg(c_, i, per, k0, n):
                for k in range(4):
                    ahead(split_lo, dve, "qkvg", i, per, k0 + k)
                dve.wait_ge(unit_done, 2 * pair_of("qkvg", i, per, k0 + 3) + 2)
                dve.tensor_copy(ZT[:, 1, bass.ds(c_ * 512, 512)], banks[2 * n + 1][:, :])\
                   .then_inc(qkvg_taken_v[n], 1)

            with dve.Fori(0, 2) as i:
                take_qkvg(i * 2, i, 8, 0, 0)
                take_qkvg(i * 2 + 1, i, 8, 4, 1)
            take_qkvg(4, 0, 8, 16, 0)
            for n in range(2):
                dve.wait_ge(qkvg_taken_v[n], 3 - n + 1)
                dve.wait_ge(qkvg_taken_s[n], 3 - n + 1)
            heads = QH + KVH
            step(dve.tensor_scalar(nsink, pa("sinks"), -1.0, None, ALU.mult))
            for t in range(TT):
                step(dve.tensor_copy(VP[:, 1 + t, :], ZT[:, t, 1280:1536]))
            dve.wait_ge(qk_squares, 2)
            for t in range(TT):
                step(dve.tensor_reduce(ss40[:, t * heads:(t + 1) * heads],
                                       XN[:, t, 0:1280].rearrange("p (h d) -> p h d", d=HD), X_AXIS, ALU.add))
            step.wait()
            dve.tensor_scalar(ss40, ss40, 1.0 / HD, EPS, ALU.mult, ALU.add).then_inc(qk_mean, 1)
            dve.wait_ge(qk_std, 1)
            step(dve.reciprocal(ss40, ss40))
            step.wait()
            zqk = [ZT[:, t, 0:1280].rearrange("p (h d) -> p h d", d=HD) for t in range(TT)]
            for t in range(TT):
                step(dve.tensor_tensor(zqk[t], zqk[t], ss40[:, t * heads:(t + 1) * heads].unsqueeze(2)
                                       .broadcast_to([P, heads, HD]), ALU.mult))
            step.wait()
            for t in range(TT):
                step(dve.tensor_tensor(zqk[t][:, 0:QH, :], zqk[t][:, 0:QH, :],
                                       pa("q_gain").unsqueeze(1).broadcast_to([P, QH, HD]), ALU.mult))
                step(dve.tensor_tensor(zqk[t][:, QH:heads, :], zqk[t][:, QH:heads, :],
                                       pa("k_gain").unsqueeze(1).broadcast_to([P, KVH, HD]), ALU.mult))
            step.wait()
            rot = [SC[:, n * 160:(n + 1) * 160].rearrange("p (h d) -> p h d", d=HALF) for n in range(4)]
            for t in range(TT):
                x1, x2 = zqk[t][:, :, 0:HALF], zqk[t][:, :, HALF:ROT]
                cos = c("cos")[:, t * HALF:(t + 1) * HALF].unsqueeze(1).broadcast_to([P, heads, HALF])
                sin = c("sin")[:, t * HALF:(t + 1) * HALF].unsqueeze(1).broadcast_to([P, heads, HALF])
                step(dve.tensor_tensor(rot[0], x1, cos, ALU.mult))
                step(dve.tensor_tensor(rot[1], x2, sin, ALU.mult))
                step(dve.tensor_tensor(rot[2], x2, cos, ALU.mult))
                step(dve.tensor_tensor(rot[3], x1, sin, ALU.mult))
                step.wait()
                step(dve.tensor_tensor(x1, rot[0], rot[1], ALU.subtract))
                step(dve.tensor_tensor(x2, rot[2], rot[3], ALU.add))
                step.wait()
            kd = KD.rearrange("p (t g r d) -> p t g r d", t=TT, g=KVH, r=2)
            for t in range(TT):
                for r in range(2):
                    ins = dve.tensor_copy(kd[:, t, :, r, :], zqk[t][:, QH:heads, :])
            ins.then_inc(qk_ready, 1)
            dve.wait_ge(silu_tanh, 1)
            for t in range(TT):
                step(dve.scalar_tensor_tensor(out=ZT[:, t, 1536:2560], in0=YM[:, t, :], scalar=1.0,
                                              in1=ZT[:, t, 1536:2560], op0=ALU.add, op1=ALU.mult))
            step.wait()

            def att_scores(u, g):
                dve.wait_ge(scored, u + 2)
                for b in range(2):
                    step(dve.scalar_tensor_tensor(
                        out=SC[:, b * 512:(b + 1) * 512].rearrange("p (h n) -> p h n", h=2),
                        in0=banks[4 + b][:, :].rearrange("p (h n) -> p h n", h=2), scalar=HD ** -0.5,
                        in1=band_t.unsqueeze(1).broadcast_to([P, 2, S]), op0=ALU.mult, op1=ALU.add))
                step.wait()
                step(dve.tensor_reduce(mx, SC.rearrange("p (h n) -> p h n", h=GROUP), X_AXIS, ALU.max))
                step.wait()
                step(dve.scalar_tensor_tensor(out=nm, in0=mx, scalar=-1.0, in1=nsink[:, bass.ds(g * GROUP, GROUP)],
                                              op0=ALU.mult, op1=ALU.min))
                step.wait()
                dve.tensor_tensor(dsink, nm, nsink[:, bass.ds(g * GROUP, GROUP)], ALU.subtract).then_inc(sc_max, 1)

            for t in range(TT):
                band_t = c("band")[:, t * S:(t + 1) * S]
                with dve.Fori(0, KVH) as g:
                    j = g + t * KVH
                    with step.turns(g, 11, KVH):
                        cw = pa("conv_w")
                        att_scores(j, g)
                        ahead(split_lo, dve, "conv", j, 4, 0)
                        dve.wait_ge(conv_gate, j + 1)
                        dve.scalar_tensor_tensor(out=CG, in0=CG, scalar=1.0, in1=banks[0][:, 0:S], op0=ALU.add,
                                                 op1=ALU.mult).then_inc(conv_gate_used, 1)
                        dve.wait_ge(exps, j * 5 + 5)
                        step(dve.tensor_tensor(rec, esum, esink, ALU.add))
                        step.wait()
                        step(dve.reciprocal(rec, rec))
                        ahead(split_lo, dve, "conv", j, 4, 1)
                        ahead(split_lo, dve, "conv", j, 4, 2)
                        dve.wait_ge(conv_c, j + 1)
                        dve.wait_ge(unit_done, 2 * pair_of("conv", j, 4, 2) + 2)
                        dve.tensor_tensor(CU[:, 2:2 + S], CC, banks[2][:, 0:S], ALU.mult).then_inc(conv_h_used, 1)
                        dve.wait_ge(conv_h_used, j + 2)
                        step(dve.tensor_scalar(CY, CU[:, 0:S], cw[:, bass.ds(j * 3, 1)], None, ALU.mult))
                        step.wait()
                        for tap in range(1, 3):
                            step(dve.scalar_tensor_tensor(out=CY, in0=CU[:, tap:tap + S],
                                                          scalar=cw[:, bass.ds(j * 3 + tap, 1)], in1=CY,
                                                          op0=ALU.mult, op1=ALU.add))
                            step.wait()
                        dve.wait_ge(mixed, j + 1)
                        step(dve.tensor_tensor(ET[:, 0:S].rearrange("p (b a d) -> p b a d", b=2, a=2),
                                               banks[4][:, 0:S].rearrange("p (b a d) -> p b a d", b=2, a=2),
                                               rec.rearrange("p (a b) -> p b a", a=2).unsqueeze(3)
                                               .broadcast_to([P, 2, 2, HD]), ALU.mult))
                        step.wait()
                        dve.scalar_tensor_tensor(out=YM[:, t, bass.ds(g * S, S)], in0=ET[:, 0:S], scalar=0.5,
                                                 in1=ZT[:, t, bass.ds(g * S + 1536, S)], op0=ALU.mult,
                                                 op1=ALU.mult).then_inc(mix_used, 1)
                        ahead(split_lo, dve, "conv", j, 4, 3)
                        dve.wait_ge(unit_done, 2 * pair_of("conv", j, 4, 3) + 2)
                        step(dve.tensor_tensor(CY, CY, banks[3][:, 0:S], ALU.mult))
                        step.wait()
                        dve.wait_ge(conv_gate_used, j + 2)
                        dve.scalar_tensor_tensor(out=MIXT[:, bass.ds(j + 8, 1), :].rearrange("p o n -> p (o n)"),
                                                 in0=CY, scalar=0.5, in1=CG, op0=ALU.mult, op1=ALU.mult)\
                           .then_inc(conv_b_used, 1)

            for k in range(8):
                dve.wait_ge(act_hi_ready, KT + k + 1)
                dve.tensor_tensor(act_lo[:, k, :], banks[k][:, 0:S], act_hi[:, k, :].bitcast(F32), ALU.subtract)\
                   .then_inc(act_lo_ready, 1)
            dve.wait_ge(act_hi_ready, 2 * KT)
            dve.tensor_tensor(act_lo[:, 8:16, :], MIXT[:, 8:16, :], act_hi[:, 8:16, :].bitcast(F32), ALU.subtract)\
               .then_inc(act_lo_ready, 8)

            def add_blocks(part):
                with dve.Fori(0, 2) as i:
                    for n in range(2):
                        for k in range(4):
                            ahead(split_lo, dve, part, i, 8, 4 * n + k)
                        dve.wait_ge(unit_done, 2 * pair_of(part, i, 8, 4 * n + 3) + 2)
                        for t in range(TT):
                            xs = X[:, t, bass.ds(i * 1024 + n * 512, 512)]
                            dve.tensor_tensor(xs, xs, banks[2 * n + t][:, :], ALU.add).then_inc(added[n], 1)

            add_blocks("w_out")
            for n in range(2):
                dve.wait_ge(added[n], 5)
            normed_rows(2, 5)
            keep_lo(2, pa("gate_gain"))
            dve.wait_ge(gate_row_ready, 16)
            with dve.Fori(0, 2) as i, step.turns(i, 4, 2):
                for n in range(2):
                    for k in range(4):
                        ahead(split_lo, dve, "gate", i, 8, 4 * n + k)
                    dve.wait_ge(unit_done, 2 * pair_of("gate", i, 8, 4 * n + 3) + 2)
                    col = i * 1024 + n * 512
                    for t in range(TT):
                        dve.tensor_tensor(SC_G[t], banks[2 * n + t][:, :], gate_row[:, bass.ds(col, 512)], ALU.add)\
                           .then_inc(gate_pre, 1)
                    for t in range(TT):
                        dve.wait_ge(gate_tanh, i * 4 + 2 * n + t + 1)
                        step(dve.scalar_tensor_tensor(out=SC_G[t], in0=SC_G[t], scalar=1.0,
                                                      in1=E[:, t, bass.ds(col, 512)], op0=ALU.add, op1=ALU.mult))
                    step.wait()
                    for t in range(TT):
                        xs = X[:, t, bass.ds(col, 512)]
                        dve.scalar_tensor_tensor(out=xs, in0=SC_G[t], scalar=0.5, in1=xs, op0=ALU.mult, op1=ALU.add)\
                           .then_inc(gated[n], 1)
            for n in range(2):
                dve.wait_ge(gated[n], 5)
            normed_rows(3, 7)
            keep_lo(3, pa("mix_gain"))

            for k in range(4):
                ahead(split_lo, dve, "ckv", 0, 4, k)
            for k in range(2):
                ahead(split_lo, dve, "kiwi", 0, 2, k)
            dve.wait_ge(kw_kept, 2)
            ki = KW[:, :, 0:ID]
            kc = KID[:, :, 0:ID]
            step(dve.tensor_reduce(mx[:, 0:2], ki, X_AXIS, ALU.add))
            step.wait()
            step(dve.tensor_scalar(mx[:, 0:2], mx[:, 0:2], 1.0 / ID, None, ALU.mult))
            step.wait()
            step(dve.tensor_tensor(kc, ki, mx[:, 0:2].unsqueeze(2).broadcast_to([P, TT, ID]), ALU.subtract))
            step.wait()
            step(dve.tensor_tensor(KID[:, :, ID:P], kc, kc, ALU.mult))
            step.wait()
            step(dve.tensor_reduce(stat[:, 10:12], KID[:, :, ID:P], X_AXIS, ALU.add))
            step.wait()
            step(dve.tensor_scalar(stat[:, 10:12], stat[:, 10:12], 1.0 / ID, EPS, ALU.mult, ALU.add))
            dve.wait_ge(ckv_squares, 2)
            dve.tensor_scalar(stat[:, 8:10], ss, 1.0 / RANK, EPS, ALU.mult, ALU.add).then_inc(ckv_mean, 1)
            dve.wait_ge(ckv_std, 1)
            step(dve.reciprocal(stat[:, 8:12], stat[:, 8:12]))
            step.wait()
            for t in range(TT):
                dve.tensor_scalar(CKV[:, t, :], CKV[:, t, :], stat[:, 8 + t:9 + t], None, ALU.mult)\
                   .then_inc(ckv_normed, 1)
            step(dve.tensor_tensor(kc, kc, stat[:, 10:12].unsqueeze(2).broadcast_to([P, TT, ID]), ALU.mult))
            step.wait()
            step(dve.tensor_tensor(kc, kc, pa("idx_g").unsqueeze(1).broadcast_to([P, TT, ID]), ALU.mult))
            step.wait()
            step(dve.tensor_tensor(kc, kc, pa("idx_b").unsqueeze(1).broadcast_to([P, TT, ID]), ALU.add))
            step.wait()
            dve.tensor_copy(KID[:, :, ID:P], kc).then_inc(ki_ready, 1)
            step(dve.tensor_scalar(KW[:, :, ID:ID + IH], KW[:, :, ID:ID + IH], IH ** -0.5, None, ALU.mult))
            step(dve.memset(ISC, 0.0))
            step.wait()
            with dve.Fori(0, IH // 4) as i:
                for n in range(2):
                    ahead(split_lo, dve, "qi", i, 2, n)
                    dve.wait_ge(rel_ready, i * 4 + 2 * n + 3)
                    for hh in range(2):
                        for t in range(TT):
                            dve.scalar_tensor_tensor(
                                out=ISC[:, t, :], in0=REL[:, 2 * hh + t, :],
                                scalar=KW[:, t, bass.ds(i * 4 + (2 * n + hh + ID), 1)],
                                in1=ISC[:, t, :], op0=ALU.mult, op1=ALU.add).then_inc(rel_used, 1)
                        dve.wait_ge(rel_used, i * 8 + 4 * n + 2 * hh + 3)

            for t in range(TT):
                step(dve.tensor_tensor(IWORK[:, t, :], ISC[:, t, :], c("causal")[:, t * S:(t + 1) * S], ALU.add))
                step.wait()
                for _ in range(TOPK // 8):
                    step(dve.max(top8, IWORK[:, t, :]))
                    step.wait()
                    step(dve.match_replace(IWORK[:, t, :], top8, IWORK[:, t, :], TAKEN))
                    step.wait()
            step(dve.tensor_scalar(IWORK, IWORK, TAKEN / 2, 1.0, ALU.is_le, ALU.subtract))
            step.wait()
            step(dve.scalar_tensor_tensor(out=AMASK, in0=IWORK.rearrange("p t n -> p (t n)"), scalar=-NEG,
                                          in1=c("causal"), op0=ALU.mult, op1=ALU.add))

            lam = pa("lam")
            step(dve.tensor_scalar(sp_c, lam, -1.0, None, ALU.mult))
            step.wait()
            dve.tensor_tensor(sp_a, lam, sp_c, ALU.max).then_inc(softplus_ready, 1)
            step(dve.tensor_scalar(nba, pa("ba"), -1.0, None, ALU.mult))
            step(dve.tensor_scalar(nbx, pa("bx"), -1.0, None, ALU.mult))
            dve.wait_ge(softplus_ready, 2)
            step(dve.tensor_scalar(sp_c, sp_b, 2.0, None, ALU.add))
            step.wait()
            step(dve.reciprocal(sp_c, sp_c))
            step.wait()
            step(dve.tensor_tensor(sp_b, sp_b, sp_c, ALU.mult))
            step.wait()
            step(dve.tensor_tensor(sp_c, sp_b, sp_b, ALU.mult))
            step.wait()
            step(dve.tensor_scalar(sp_a, sp_c, 1.0 / 19, 1.0 / 17, ALU.mult, ALU.add))
            step.wait()
            for odd in range(15, 0, -2):
                step(dve.tensor_tensor(sp_a, sp_a, sp_c, ALU.mult))
                step.wait()
                step(dve.tensor_scalar(sp_a, sp_a, 1.0 / odd, None, ALU.add))
                step.wait()
            step(dve.scalar_tensor_tensor(out=sp_a, in0=sp_a, scalar=2.0, in1=sp_b, op0=ALU.mult, op1=ALU.mult))
            step(dve.tensor_scalar(sp_c, lam, -1.0, 0.0, ALU.mult, ALU.max))
            step.wait()
            step(dve.tensor_tensor(sp_a, sp_a, sp_c, ALU.add))
            step.wait()
            step(dve.tensor_scalar(sp_b, sp_a, -8.0, None, ALU.mult))
            step(dve.memset(XP[:, 0:3], 0.0))
            dve.tensor_scalar(sp_a, sp_a, 8.0, None, ALU.mult).then_inc(softplus_ready, 1)

            cw2, cb2 = pa("conv_w2"), pa("conv_b2")
            with dve.Fori(0, KT) as j:
                with step.turns(j, 7, KT):
                    ahead(split_lo, dve, "rnn", j, 2, 0)
                    dve.wait_ge(xr_kept, j + 2)
                    step(dve.tensor_scalar(XC, XP[:, 0:S], cw2[:, bass.ds(j * 4, 1)], cb2[:, bass.ds(j, 1)],
                                           ALU.mult, ALU.add))
                    step.wait()
                    for tap in range(1, 4):
                        ins = dve.scalar_tensor_tensor(out=XC, in0=XP[:, tap:tap + S],
                                                       scalar=cw2[:, bass.ds(j * 4 + tap, 1)], in1=XC,
                                                       op0=ALU.mult, op1=ALU.add)
                        if tap < 3:
                            step(ins)
                            step.wait()
                        else:
                            ins.then_inc(xc_ready, 1)
                    ahead(split_lo, dve, "rnn", j, 2, 1)
                    dve.wait_ge(rg_exp, j * 2 + 3)
                    step(dve.tensor_scalar(RI, RI, 1.0, None, ALU.add))
                    step.wait()
                    dve.reciprocal(RI, RI).then_inc(r_ready, 1)
                    dve.wait_ge(r_ready, j + 1)
                    step(dve.tensor_tensor(RX[:, bass.ds(j, 1), :].rearrange("p o n -> p (o n)"), RI[:, S:2 * S], XC,
                                           ALU.mult))
                    dve.wait_ge(a_ready, j * 2 + 2)
                    step(dve.tensor_scalar(THD, TH, 1.0, None, ALU.add))
                    step.wait()
                    step(dve.reciprocal(THD, THD))
                    step.wait()
                    dve.scalar_tensor_tensor(out=RW[:, bass.ds(j, 1), :].rearrange("p o n -> p (o n)"), in0=TH,
                                             scalar=2.0, in1=THD, op0=ALU.mult, op1=ALU.mult).then_inc(th_used, 1)
            dve.wait_ge(th_used, KT + 1)
            dve.memset(RA[:, :, 0:1], 0.0).then_inc(rw_ready, 1)
            dve.wait_ge(rw_root, 1)

            with dve.Fori(0, H2) as h:
                with step.turns(h, 7, H2):
                    row = lambda r: r[:, bass.ds(h, 1), :].rearrange("p o n -> p (o n)")
                    step(dve.tensor_tensor(HU, row(RW), row(RX), ALU.mult))
                    step.wait()
                    step(dve.tensor_tensor_scan(HU, row(RA), HU, 0.0, ALU.mult, ALU.add))
                    ahead(split_lo, dve, "heads", h, 2, 0)
                    dve.wait_ge(v_made, h + 1)
                    dve.tensor_copy(VS.rearrange("p k n -> p (k n)"), banks[3][:, 0:S]).then_inc(v_kept, 1)
                    dve.wait_ge(gr_tanh, h + 1)
                    step.wait()
                    dve.scalar_tensor_tensor(out=HU, in0=TG, scalar=1.0, in1=HU, op0=ALU.add, op1=ALU.mult)\
                       .then_inc(gr_used, 1)
                    dve.wait_ge(logits_made, h + 2)
                    step(dve.scalar_tensor_tensor(out=LG.rearrange("p t n -> p (t n)"), in0=banks[4][:, :],
                                                  scalar=float(P) ** -0.5, in1=AMASK, op0=ALU.mult, op1=ALU.add))
                    step.wait()
                    step(dve.tensor_reduce(mx[:, 0:2], LG, X_AXIS, ALU.max))
                    step.wait()
                    dve.tensor_scalar(nm[:, 0:2], mx[:, 0:2], -1.0, None, ALU.mult).then_inc(max_ready, 1)
                    dve.wait_ge(p_exp, h * 2 + 3)
                    step(dve.reciprocal(rec[:, 0:2], esum[:, 0:2]))
                    step.wait()
                    for t in range(TT):
                        dve.tensor_scalar(LG[:, t, :], LG[:, t, :], rec[:, t:t + 1], None, ALU.mult)\
                           .then_inc(p_ready, 1)
                    ahead(split_lo, dve, "heads", h, 2, 1)
                    dve.wait_ge(ga_tanh, h + 2)
                    dve.wait_ge(y_made, h + 1)
                    dve.wait_ge(gr_used, h + 2)
                    step(dve.scalar_tensor_tensor(out=YH, in0=TA, scalar=1.0, in1=banks[6][:, 0:S], op0=ALU.add,
                                                  op1=ALU.mult))
                    step.wait()
                    step(dve.tensor_tensor(YH, YH, HU, ALU.add))
                    step.wait()
                    dve.tensor_scalar(row(MIX2), YH, 0.5, None, ALU.mult).then_inc(head_mixed, 1)

            for k in range(4):
                dve.wait_ge(act_hi_ready, 4 * KT + 4 * k + 4)
                dve.tensor_tensor(act_lo[:, 4 * k:4 * k + 4, :], MIX2[:, 4 * k:4 * k + 4, :],
                                  act_hi[:, 4 * k:4 * k + 4, :].bitcast(F32), ALU.subtract).then_inc(act_lo_ready, 4)
            add_blocks("w_o")
            for n in range(2):
                dve.wait_ge(added[n], 9)
            normed_rows(4, 9)
            keep_lo(5, pa("ffn_gain"))

            def top16(vals, idx, work):
                step(dve.max(vals[:, 0:8], work))
                step.wait()
                step(dve.max_index(idx[:, 0:8], vals[:, 0:8], work))
                step.wait()
                step(dve.match_replace(work, vals[:, 0:8], work, TAKEN))
                step.wait()
                step(dve.max(vals[:, 8:16], work))
                step.wait()
                return dve.max_index(idx[:, 8:16], vals[:, 8:16], work)

            for h in range(PH):
                ahead(split_lo, dve, "wqu", h, 4, 0)
                for a in range(2):
                    ahead(split_lo, dve, "wqu", h, 4, 1 + a)
                    dve.wait_ge(ps_kept[a], h + 2)
                    for t in range(TT):
                        ins = top16(V12[:, h, a, t, :], I12[:, h, a, t, :], PS[:, a, t, :])
                        if t == TT - 1:
                            ins.then_inc(ps_used[a], 1)
                        else:
                            step(ins)
                ahead(split_lo, dve, "wqu", h, 4, 3)
                for a in range(2):
                    dve.wait_ge(ps_used[a], h + 2)
                for t in range(TT):
                    step(dve.tensor_tensor(CAND[:, t, :].rearrange("p (a b) -> p a b", a=PK),
                                           V12[:, h, 0, t, :].unsqueeze(2).broadcast_to([P, PK, PK]),
                                           V12[:, h, 1, t, :].unsqueeze(1).broadcast_to([P, PK, PK]), ALU.add))
                    step.wait()
                    step(top16(CV[:, h, t, :], CP[:, h, t, :], CAND[:, t, :]))
            step.wait()
            lows = iter(range(2 * PH))

            def more(count=1):
                for _ in range(count):
                    ahead(split_lo, dve, "u_decode", 0, 2, next(lows))

            cv = CV.rearrange("p h t k -> p (h t) k")
            step(dve.tensor_copy(crec, cv[:, :, 0:1].rearrange("p a o -> p (a o)")))
            step.wait()
            dve.tensor_tensor(cv, cv, crec.unsqueeze(2).broadcast_to([P, PH * TT, PK]), ALU.subtract)\
               .then_inc(pick_diff, 1)
            more()
            cp = CP.rearrange("p h t k -> p (h t k)")
            step(dve.tensor_scalar(CAU[:, 0, :], cp, 4, None, ALU.logical_shift_right))
            step(dve.tensor_scalar(CAU[:, 1, :], cp, 15, None, ALU.bitwise_and))
            step(dve.tensor_copy(I12F.rearrange("p h a t k -> p (h a t k)"),
                                 I12.rearrange("p h a t k -> p (h a t k)")))
            step.wait()
            step(dve.tensor_copy(CA.rearrange("p a n -> p (a n)"), CAU.rearrange("p a n -> p (a n)")))
            more()
            step.wait()
            for a in range(2):
                step(dve.tensor_tensor(EQ.rearrange("p (n j) -> p n j", j=PK),
                                       CA[:, a, :].unsqueeze(2).broadcast_to([P, SLOT_N * TT, PK]),
                                       iota[:, 0:PK].unsqueeze(1).broadcast_to([P, SLOT_N * TT, PK]), ALU.is_equal))
                more(2)
                step.wait()
                for h in range(PH):
                    eq = EQ[:, h * TT * PK * PK:(h + 1) * TT * PK * PK].rearrange("p (t k j) -> p t k j", t=TT, k=PK)
                    step(dve.tensor_tensor(eq, eq, I12F[:, h, a, :, :].unsqueeze(2).broadcast_to([P, TT, PK, PK]),
                                           ALU.mult))
                    if h % 4 == 3:
                        more()
                step.wait()
                step(dve.tensor_reduce(PICK[:, a, :, :, :].rearrange("p h t k -> p (h t k)"),
                                       EQ.rearrange("p (n j) -> p n j", j=PK), X_AXIS, ALU.add))
                more(2)
                step.wait()
            dve.wait_ge(pick_exp, 1)
            step(dve.tensor_reduce(csum, cv, X_AXIS, ALU.add))
            more()
            step.wait()
            step(dve.reciprocal(crec, csum))
            step.wait()
            step(dve.tensor_tensor(PICK[:, 2, :, :, :].rearrange("p h t k -> p (h t) k"), cv,
                                   crec.unsqueeze(2).broadcast_to([P, PH * TT, PK]), ALU.mult))
            step.wait()
            for a in range(3):
                ins = dve.tensor_copy(PICKT[:, a, :, :, :].rearrange("p t h k -> p h t k"), PICK[:, a, :, :, :])
                ins.then_inc(picks_ready, 1)
            for _ in lows:
                ahead(split_lo, dve, "u_decode", 0, 2, _)

            dve.wait_ge(slots_kept, 3)
            with dve.Fori(0, S // 16) as i:
                for n in range(2):
                    for s in range(8):
                        tok = i * 16 + (8 * n + s)
                        dve.wait_ge(hot_used[s % 4], i * 4 + (2 * n + s // 4) + 1)
                        dve.tensor_scalar(hot[:, 0, s % 4, :], iota, slot_t[:, 0, bass.ds(tok, 1)],
                                          slot_t[:, 2, bass.ds(tok, 1)], ALU.is_equal, ALU.mult).then_inc(hot1, 1)
                        if s % 4 == 3:
                            ahead(split_lo, dve, "u_gates", i, 2, n, units=(s // 4,))
            for n in range(2):
                dve.wait_ge(gate_kept[n], S // 8 + 1)

            with dve.Fori(0, EARLY // 2) as i:
                for n in range(2):
                    ahead(split_lo, dve, "u_late", i, 2, n)
                    dve.wait_ge(gelu_ready[n], i + (EARLY // 2 + 1) + 1)
                    late = G[:, bass.ds(i * 2 + (EARLY + n), 1), :].rearrange("p o n -> p (o n)")
                    dve.tensor_tensor(late, GZ[:, n, :], late, ALU.mult).then_inc(act_ready[n], 1)
                    dve.wait_ge(z_back[n], i * 16 + 16)
                    back = G[:, bass.ds(i * 2 + n, 1), :].rearrange("p o n -> p (o n)")
                    dve.tensor_tensor(back, GB[:, n, :], back, ALU.mult).then_inc(early_ready[n], 1)

            def expert_lo(b, n, need):
                dve.wait_ge(eh_ready, need)
                dve.tensor_tensor(act_lo[:, n, :], G[:, bass.ds(b, 1), :].rearrange("p o n -> p (o n)"),
                                  act_hi[:, n, :].bitcast(F32), ALU.subtract).then_inc(el_ready, 1)

            for n in range(2):
                dve.wait_ge(act_ready[n], EARLY // 2 + 1)
                dve.wait_ge(early_ready[n], EARLY // 2 + 1)
            for n in range(2):
                expert_lo(n, n, n + 1)
            with dve.Fori(0, NB // 2 - 1) as i:
                for n in range(2):
                    ahead(split_lo, dve, "v", i, 2, n)
                    expert_lo(i * 2 + (2 + n), n, i * 2 + (3 + n))

            dve.wait_ge(xf_ready, 16)
            dve.wait_ge(unit_done, UNITS)
            for t in range(TT):
                for cb in range(4):
                    xs = XF[:, t, cb * 512:(cb + 1) * 512]
                    dve.tensor_tensor(xs, xs, banks[4 * t + cb][:, :], ALU.add).then_inc(y_added, 1)
            root(0, ss, D, std, rstd, fin_squares, fin_mean, fin_std, 2)
            dve.wait_ge(final_ready, 16)
            for t in range(TT):
                dve.scalar_tensor_tensor(out=OUT[:, t, :], in0=XF[:, t, :], scalar=rstd[:, t:t + 1], in1=final_row,
                                         op0=ALU.mult, op1=ALU.mult).then_inc(fin_ready, 1)

        @block.tensor
        def _(pe):
            def turn_rows(n, fill, need):
                pe.wait_ge(normed, need)
                for k in range(KT):
                    if k >= 8:
                        pe.wait_ge(act_lo_ready, fill * KT + k - 7)
                    for t in range(TT):
                        ins = pe.transpose(banks[k % 8][:, t * P:(t + 1) * P], XN[:, t, k * P:(k + 1) * P], ident)
                    ins.then_inc(turned, 1)

            pe.wait_ge(ple_done, 1)
            for cb in range(4):
                pe.wait_ge(lo_ready, cb + 1)
                for kk in range(2):
                    hi = w_hi[:, cb, kk * 512:(kk + 1) * 512]
                    lo = w_lo[:, cb, kk * 512:(kk + 1) * 512]
                    for t in range(TT):
                        o = banks[2 * cb + t][:, :]
                        a_hi = act_hi[:, kk, t * P:(t + 1) * P]
                        a_lo = act_lo[:, kk, t * P:(t + 1) * P]
                        pe.matmul(o, a_hi, hi, start=(kk == 0), stop=False)
                        pe.matmul(o, a_hi, lo, start=False, stop=False)
                        mm = pe.matmul(o, a_lo, hi, start=False, stop=(kk == 1))
                mm.then_inc(unit_done, 1)
            pe.wait_ge(const_ready, 32)
            pe.wait_ge(ple_taken, 9)
            turn_rows(0, 0, 3)
            pe.wait_ge(act_lo_ready, KT)
            with pe.Fori(0, 2) as i:
                for n in range(2):
                    pe.wait_ge(qkvg_taken_s[n], i + 1)
                    pe.wait_ge(qkvg_taken_v[n], i + 1)
                    tokens_out(pe, "qkvg", i, 8, 4 * n, [banks[2 * n][:, :], banks[2 * n + 1][:, :]])
            pe.wait_ge(qkvg_taken_s[0], 3)
            pe.wait_ge(qkvg_taken_v[0], 3)
            tokens_out(pe, "qkvg", 0, 8, 16, [banks[0][:, :], banks[1][:, :]])
            pe.wait_ge(qk_ready, 1)
            for k in range(8):
                for t in range(TT):
                    pe.transpose(banks[k // 2][:, (k % 2) * S + t * P:(k % 2) * S + (t + 1) * P],
                                 ZT[:, t, k * P:(k + 1) * P], ident).then_inc(qk_turned, 1)
            for g in range(KVH):
                for t in range(TT):
                    off = (t * KVH + g) * P
                    pe.transpose(banks[4 + g // 2][:, (g % 2) * S + t * P:(g % 2) * S + (t + 1) * P],
                                 KD[:, off:off + P], ident).then_inc(qk_turned, 1)
            pe.wait_ge(qk_kept, 16)

            def conv_pair(j, n):
                pe.wait_ge([conv_gate_used, conv_h_used, conv_h_used, conv_b_used][n], j + 1)
                columns_out(pe, pair_of("conv", j, 4, n), n % 2, banks[n][:, 0:S])

            order = [0, 2, 1, 3]
            with pe.Fori(0, TT) as t:
                with pe.Fori(0, KVH) as g:
                    j = t * KVH + g
                    pe.wait_ge(staged, j * 2 + 2)
                    pe.wait_ge(mix_used, j + 1)
                    for h in range(GROUP):
                        lo = (h % 2) * HD
                        ins = pe.matmul(banks[4 + h % 2][:, (h // 2) * S:(h // 2 + 1) * S],
                                        QST[lo:lo + HD, h // 2, :], KST[lo:lo + HD, :], start=True, stop=True)
                    ins.then_inc(scored, 1)
                    conv_pair(j, 0)
                    conv_pair(j, 1)
                    pe.wait_ge(exps, j * 5 + 4)
                    pe.wait_ge(probs_kept, j * 2 + 1)
                    for kb in range(2):
                        for h in range(GROUP):
                            ins = pe.transpose(banks[6 + kb][:, h * P:(h + 1) * P],
                                               SC[:, h * S + kb * P:h * S + (kb + 1) * P], ident)
                    ins.then_inc(probs_turned, 1)
                    conv_pair(j, 2)
                    pe.wait_ge(probs_kept, j * 2 + 3)
                    for h in range(GROUP):
                        for kb in range(2):
                            ins = pe.matmul(banks[4][:, order[h] * HD:(order[h] + 1) * HD],
                                            ET[:, kb * 512 + h * P:kb * 512 + (h + 1) * P],
                                            VP[:, bass.ds(t + kb, 1), bass.ds(g * HD, HD)]
                                            .rearrange("p o n -> p (o n)"), start=(kb == 0), stop=(kb == 1))
                    ins.then_inc(mixed, 1)
                    conv_pair(j, 3)

            pe.wait_ge(mix_used, CONV_J + 1)
            pe.wait_ge(conv_b_used, CONV_J + 1)
            for k in range(8):
                for t in range(TT):
                    ins = pe.transpose(banks[k][:, t * P:(t + 1) * P], YM[:, t, k * P:(k + 1) * P], ident)
                ins.then_inc(ym_turned, 1)
            pe.wait_ge(act_lo_ready, 2 * KT)

            def blocks_out(part, taken, base):
                with pe.Fori(0, 2) as i:
                    for n in range(2):
                        pe.wait_ge(taken[n], i * 2 + base + 1)
                        tokens_out(pe, part, i, 8, 4 * n, [banks[2 * n][:, :], banks[2 * n + 1][:, :]])

            blocks_out("w_out", added, 0)
            turn_rows(1, 2, 5)
            pe.wait_ge(act_lo_ready, 3 * KT)
            blocks_out("gate", gated, 0)
            turn_rows(2, 3, 7)
            pe.wait_ge(act_lo_ready, 4 * KT)

            tokens_out(pe, "ckv", 0, 4, 0, [banks[0][:, :], banks[1][:, :]])
            for u in range(2):
                pair = pair_of("kiwi", 0, 2, 0)
                s = unit_slot(0, u)
                pe.wait_ge(lo_ready, 2 * pair + u + 1)
                for kk in range(8):
                    k = 8 * u + kk
                    for t in range(TT):
                        o = banks[2 + t][:, 0:80]
                        a_hi = act_hi[:, k, t * P:(t + 1) * P]
                        a_lo = act_lo[:, k, t * P:(t + 1) * P]
                        hi = w_hi[:, s, kk * P:kk * P + 80]
                        lo = w_lo[:, s, kk * P:kk * P + 80]
                        pe.matmul(o, a_hi, hi, start=(k == 0), stop=False)
                        pe.matmul(o, a_hi, lo, start=False, stop=False)
                        mm = pe.matmul(o, a_lo, hi, start=False, stop=(k == KT - 1))
                mm.then_inc(unit_done, 1)
            for u in range(2):
                pe.wait_ge(lo_ready, 2 * pair_of("kiwi", 0, 2, 1) + u + 1)
                pe.matmul(banks[7][:, 0:2], w_hi[:, 2 + u, 0:P], act_hi[:, 0, 0:2], start=True, stop=True)\
                  .then_inc(unit_done, 1)
            pe.wait_ge(ckv_normed, 2)
            for k in range(RT):
                for t in range(TT):
                    ins = pe.transpose(banks[4 + k // 2][:, (k % 2) * S + t * P:(k % 2) * S + (t + 1) * P],
                                       CKV[:, t, k * P:(k + 1) * P], ident)
                ins.then_inc(ckv_turned, 1)
            pe.wait_ge(ki_ready, 1)
            for t in range(TT):
                ins = pe.transpose(banks[6][:, t * P:(t + 1) * P], KID[:, t, :], ident)
            ins.then_inc(ckv_turned, 1)
            pe.wait_ge(ckvt_kept, RT + 1)

            with pe.Fori(0, IH // 4) as i:
                for n in range(2):
                    columns_out(pe, pair_of("qi", i, 2, n), n, banks[n][:, 0:S])
                    pe.wait_ge(qi_kept, i * 2 + n + 1)
                    pe.wait_ge(rel_ready, i * 4 + 2 * n + 1)
                    for hh in range(2):
                        for t in range(TT):
                            ins = pe.matmul(banks[4 + hh][:, t * S:(t + 1) * S],
                                            QIS[hh * ID:(hh + 1) * ID, n, t * P:(t + 1) * P],
                                            KIT[hh * ID:(hh + 1) * ID, :], start=True, stop=True)
                    ins.then_inc(qi_scored, 1)

            with pe.Fori(0, KT) as j:
                pe.wait_ge(xr_kept, j + 1)
                columns_out(pe, pair_of("rnn", j, 2, 0), 0, banks[0][:, 0:S])
                pe.wait_ge(q2_kept, j + 1)
                columns_out(pe, pair_of("rnn", j, 2, 1), 1, banks[1][:, 0:S])
                pe.wait_ge(xc_ready, j + 2)
                pe.wait_ge(w_staged, j + 1)
                pe.wait_ge(rg_exp, j * 2 + 1)
                for a in range(2):
                    ins = pe.matmul(banks[4][:, a * S:(a + 1) * S], WST[:, a * P:(a + 1) * P], XC, start=True,
                                    stop=True)
                ins.then_inc(rg_done, 1)

            with pe.Fori(0, H2) as h:
                pe.wait_ge(ukv_ready, h * 16 + 16)
                pe.wait_ge(k_kept, h + 1)
                for k in range(RT):
                    ins = pe.matmul(banks[2][:, 0:S], UKV[:, k, :], CKVT[:, k, :], start=(k == 0), stop=(k == RT - 1))
                ins.then_inc(k_made, 1)
                pe.wait_ge(v_kept, h + 1)
                for st in range(2):
                    for k in range(RT):
                        ins = pe.matmul(banks[3][:, st * P:(st + 1) * P], CKVT[:, k, st * P:(st + 1) * P],
                                        UKV[:, RT + k, :], start=(k == 0), stop=(k == RT - 1))
                ins.then_inc(v_made, 1)
                pe.wait_ge(gr_used, h + 1)
                columns_out(pe, pair_of("heads", h, 2, 0), 0, banks[0][:, 0:S])
                pe.wait_ge(k_kept, h + 2)
                pe.wait_ge(q_staged, h + 1)
                pe.wait_ge(p_exp, h * 2 + 1)
                for t in range(TT):
                    ins = pe.matmul(banks[4][:, t * S:(t + 1) * S], QS2[:, t * P:(t + 1) * P], KTS, start=True,
                                    stop=True)
                ins.then_inc(logits_made, 1)
                pe.wait_ge(ga_tanh, h + 1)
                columns_out(pe, pair_of("heads", h, 2, 1), 1, banks[1][:, 0:S])
                pe.wait_ge(p_ready, h * 2 + 2)
                pe.wait_ge(p_kept, h + 1)
                for st in range(2):
                    for t in range(TT):
                        ins = pe.transpose(banks[5][:, st * S + t * P:st * S + (t + 1) * P],
                                           LG[:, t, st * P:(st + 1) * P], ident)
                ins.then_inc(p_turned, 1)
                pe.wait_ge(p_kept, h + 2)
                pe.wait_ge(v_kept, h + 2)
                pe.wait_ge(head_mixed, h + 1)
                for st in range(2):
                    ins = pe.matmul(banks[6][:, 0:S], VS[:, st, :], PTS[:, st * S:(st + 1) * S], start=(st == 0),
                                    stop=(st == 1))
                ins.then_inc(y_made, 1)

            pe.wait_ge(act_lo_ready, 5 * KT)
            blocks_out("w_o", added, 4)
            turn_rows(3, 5, 9)
            pe.wait_ge(act_lo_ready, 6 * KT)
            def experts_in(pair, b2, n, units=(0, 1)):
                if units[0] == 0:
                    pe.wait_ge(gelu_ready[n], b2 + 1)
                columns_out(pe, pair, n, banks[2 + n][:, 0:S], units)

            pe.wait_ge(keys_ready, 16)
            with pe.Fori(0, PH) as h:
                for a in range(2):
                    pe.wait_ge(pq_kept[a], h)
                    columns_out(pe, pair_of("wqu", h, 4, a), a, banks[a][:, 0:S])
                for a in range(2):
                    pe.wait_ge(pq_kept[a], h + 1)
                    pe.wait_ge(ps_kept[a], h + 1)
                    for t in range(TT):
                        ins = pe.matmul(banks[4 + a][:, t * P:(t + 1) * P], PQS[:, a, t * P:(t + 1) * P], KEYT[:, a, :],
                                        start=True, stop=True)
                    ins.then_inc(ps_made[a], 1)
                    experts_in(pair_of("wqu", h, 4, 2 + a), h, a)
            with pe.Fori(0, PH) as i:
                for n in range(2):
                    experts_in(pair_of("u_decode", i, 2, n), i + PH, n)
            for a in range(2):
                pe.wait_ge(ps_kept[a], PH + 1)
            for a in range(3):
                pe.wait_ge(picks_ready, a + 1)
                for t in range(TT):
                    pe.transpose(banks[4 + a][:, t * P:(t + 1) * P],
                                 PICKT[:, a, t, :, :].rearrange("p h k -> p (h k)"),
                                 ident).then_inc(picks_turned, 1)
            with pe.Fori(0, S // 16) as i:
                for n in range(2):
                    for m in range(2):
                        experts_in(pair_of("u_gates", i, 2, n), i + 2 * PH, n, units=(m,))
                        pe.wait_ge(gate_kept[m], i * 2 + n + 1)
                        for s in range(4):
                            pe.wait_ge(hot1, i * 16 + (8 * n + 4 * m + s + 1))
                            pe.wait_ge(hot2, i * 16 + (8 * n + 4 * m + s + 1) + 1)
                            pe.matmul(banks[m][:, s * P:(s + 1) * P], hot[:, 1, s, :], hot[:, 0, s, :], start=True,
                                      stop=True).then_inc(hot_used[s], 1)
            with pe.Fori(0, EARLY // 2) as i:
                for n in range(2):
                    experts_in(pair_of("u_late", i, 2, n), i + EARLY // 2, n)
            for n in range(2):
                pe.wait_ge(gelu_ready[n], NB // 2 + 1)
                pe.wait_ge(gate_kept[n], S // 8 + 1)

            def expert(i, n, first=False, last=False):
                pe.wait_ge(el_ready, i * 2 + n + 1)
                for u in range(2):
                    pe.wait_ge(lo_ready, 2 * pair_of("v", i, 2, n) + u + 1)
                    s = unit_slot(n, u)
                    for t in range(TT):
                        for cc in range(2):
                            o = banks[4 * t + 2 * u + cc][:, :]
                            a_hi = act_hi[:, n, t * P:(t + 1) * P]
                            a_lo = act_lo[:, n, t * P:(t + 1) * P]
                            hi = w_hi[:, s, cc * 512:(cc + 1) * 512]
                            lo = w_lo[:, s, cc * 512:(cc + 1) * 512]
                            pe.matmul(o, a_hi, hi, start=first, stop=False, skip_group_check=True)
                            pe.matmul(o, a_hi, lo, start=False, stop=False, skip_group_check=True)
                            mm = pe.matmul(o, a_lo, hi, start=False, stop=last, skip_group_check=True)
                    mm.then_inc(unit_done, 1)

            expert(0, 0, first=True)
            expert(0, 1)
            with pe.Fori(1, NB // 2 - 1) as i:
                expert(i, 0)
                expert(i, 1)
            expert(NB // 2 - 1, 0)
            expert(NB // 2 - 1, 1, last=True)


def _columns(w):
    n = w.shape[1] // P
    return w.reshape(2, 8, P, n, P).transpose(3, 0, 2, 1, 4).reshape(2 * n, P, UNIT)


def _tokens(w):
    n = w.shape[1] // 512
    return w.reshape(8, 2, P, n, 512).transpose(3, 0, 2, 1, 4).reshape(8 * n, P, UNIT)


def _interleave(parts, n):
    return np.stack([a.reshape(n, 2, P, UNIT) for a in parts], 1).reshape(-1, P, UNIT)


def _by_partition(v):
    return np.ascontiguousarray(v.reshape(-1, P).T)


def _stream(i):
    w1, w2 = i["w_in"][0], i["w_in_2"][0]
    o = QKVG_W
    cb, cc, ch, gc = (_columns(w1[:, o + n * 1024:o + (n + 1) * 1024]) for n in range(4))
    cut = {"xr": (0, 2048), "q": (2048, 4096), "ckv": (4096, 4608), "qi": (4608, 5632), "kw": (5632, 5712),
           "gr": (5712, 7760), "ga": (7760, 9808)}
    part = {k: w2[:, a:b] for k, (a, b) in cut.items()}
    kw = np.pad(part["kw"], ((0, 0), (0, P - 80)))
    u = i["peer_u_2"][0].reshape(NB, P, 2, 8, P).transpose(0, 2, 4, 3, 1).reshape(2 * NB, P, UNIT)
    v = i["peer_v_2"][0].reshape(NB, P, 2, UNIT).transpose(0, 2, 1, 3).reshape(2 * NB, P, UNIT)
    wq = _columns(i["peer_wq_2"][0])
    wqu = np.stack([a.reshape(PH, 4, P, UNIT) for a in (wq, u[0:4 * PH])], 1).reshape(-1, P, UNIT)
    return np.concatenate([
        i["w_ple_proj"][0].reshape(2, P, 4, 512).transpose(2, 1, 0, 3).reshape(4, P, UNIT),
        _tokens(w1[:, :o]),
        _interleave([gc, cc, ch, cb], CONV_J),
        _tokens(i["w_out"][0]),
        _tokens(i["w_ple_gate"][0]),
        _tokens(part["ckv"]),
        _columns(kw), np.zeros((2, P, UNIT), np.float32),
        _columns(part["qi"]),
        _interleave([_columns(part["xr"]), _columns(part["q"])], KT),
        _interleave([_columns(part["gr"]), _columns(part["ga"])], KT),
        _tokens(i["w_o_2"][0]),
        wqu,
        u[4 * PH:], v,
    ])


def _constants():
    f = np.float32
    q = np.arange(P)[:, None]
    j = np.arange(2 * P)[None, :]
    inside = (j > q) & (j <= q + P)
    band = [np.where(inside & (j >= P), 0, NEG), np.where(inside, 0, NEG)]
    causal = [np.where(j <= q + t * P, 0, NEG) for t in range(TT)]
    freq = np.power(f(500000.0), -np.arange(HALF, dtype=f) * f(2.0) / f(ROT))
    ang = np.arange(S, dtype=f)[:, None] * freq[None, :]
    rope = [fn(ang).reshape(TT, P, HALF).transpose(1, 0, 2).reshape(P, -1) for fn in (np.cos, np.sin)]
    iota = np.broadcast_to(np.arange(P), (P, P))
    return np.concatenate([np.eye(P), iota, *band, *causal, *rope], 1).astype(f)


def _parameters(i):
    def rep(v):
        return np.broadcast_to(v.reshape(1, -1), (P, v.size))

    sinks = i["attn_sinks"][0].reshape(KVH, 2, 2).transpose(0, 2, 1)
    cw = i["conv_w"][0].reshape(3, CONV_J, P).transpose(2, 1, 0).reshape(P, -1)
    cw2 = i["conv_w_2"][0].reshape(4, KT, P).transpose(2, 1, 0).reshape(P, -1)
    return np.concatenate([
        _by_partition(i["norm_gain"]), _by_partition(i["ple_gate_norm_gain"]), _by_partition(i["norm_mix_g_2"]),
        _by_partition(i["norm_ffn_g_2"]), cw, cw2, _by_partition(i["conv_b_2"]), _by_partition(i["rg_ba_2"]),
        _by_partition(i["rg_bx_2"]), _by_partition(i["rg_lambda_2"]), _by_partition(i["kv_norm_g_2"]),
        rep(i["q_norm_gain"]), rep(i["k_norm_gain"]), rep(sinks), rep(i["idx_ln_g_2"]),
        rep(i["idx_ln_b_2"]),
    ], 1)


def _arrays(i):
    uk = i["w_uk_2"][0].reshape(H2, RT, P, P).transpose(0, 2, 1, 3)
    uv = i["w_uv_2"][0].reshape(H2, RT, P, P).transpose(0, 2, 1, 3)
    return {
        "stream": _stream(i),
        "x": np.ascontiguousarray(i["x"]),
        "p_t": np.ascontiguousarray(i["p"][0, 0].T.reshape(2, P, S).transpose(1, 0, 2).reshape(P, -1)),
        "rows": np.stack([np.broadcast_to(i[n].reshape(1, D), (P, D))
                          for n in ("ple_norm_gain", "b_ple_gate", "norm_final_g_2")]),
        "consts": _constants(),
        "params": _parameters(i),
        "rg_w": np.stack([i["rg_wa_2"][0], i["rg_wx_2"][0]], 1).transpose(2, 0, 1, 3).reshape(P, -1).copy(),
        "ukv": np.concatenate([uk, uv], 2).reshape(H2, P, 8 * P),
        "keys_t": np.concatenate([i["peer_keys1_2"][0].T, i["peer_keys2_2"][0].T], 1),
    }


def kernel(**inputs):
    import concourse.bacc as bacc
    from concourse.bass_utils import run_bass_kernel_spmd as run

    arrays = _arrays({k: np.asarray(v) for k, v in inputs.items()})
    nc = bacc.Bacc("TRN2", target_bir_lowering=False, num_devices=1, dynamic_dma_scratch_size=1024)
    args = {k: nc.dram_tensor(f"in_{k}", a.shape, F32, kind="ExternalInput").ap() for k, a in arrays.items()}
    out = nc.dram_tensor("out", (1, S, D), F32, kind="ExternalOutput").ap()
    build(nc, out=out, **args)
    r = run(nc, [{f"in_{k}": a for k, a in arrays.items()}], core_ids=[0])
    return r.results[0]["out"]
```

```python
from contextlib import ExitStack, contextmanager

import numpy as np

import concourse.bass as bass
from concourse import mybir

F32 = mybir.dt.float32
F32R = mybir.dt.float32r
U32 = mybir.dt.uint32
ALU = mybir.AluOpType
ACT = mybir.ActivationFunctionType
X_AXIS = mybir.AxisListType.X

P = 128
S = 256
TT = S // P
D = 2048
KT = D // P
UNIT = 1024
SLOTS = 4
EPS = 1e-6
NEG = -1e30
TAKEN = -3e38

QH, KVH, HD = 16, 4, 64
GROUP = QH // KVH
ATTN_W = QH * HD
KV_W = KVH * HD
QKVG_W = 2 * ATTN_W + 2 * KV_W
CONV_J = (D - ATTN_W) // P
ROT = HD // 4
HALF = ROT // 2

H2 = 16
RANK = 512
RT = RANK // P
IH, ID = 16, 64
TOPK = min(256, S // 4)
PH, PK = 8, 16
KEYS = 128
NB = KEYS
SLOT_N = PH * PK

PARTS = [("ple", 2), ("qkvg", 4 * QKVG_W // 512), ("conv", 4 * CONV_J), ("w_out", 16), ("gate", 16),
         ("ckv", 4), ("kiwi", 2), ("qi", IH * ID // P), ("rnn", 2 * KT), ("heads", 2 * H2), ("w_o", 16),
         ("wqu", 4 * PH), ("u_decode", 2 * PH), ("u_gates", S // 8), ("u_late", NB // 2), ("v", NB)]
EARLY = NB // 2
FIRST = {}
_n = 0
for _name, _count in PARTS:
    FIRST[_name] = _n
    _n += _count
PAIRS = _n
UNITS = 2 * PAIRS

CONST = {}
_n = 0
for _name, _count in [("ident", P), ("iota", P), ("band", TT * 2 * P), ("causal", TT * S), ("cos", TT * HALF),
                      ("sin", TT * HALF)]:
    CONST[_name] = (_n, _n + _count)
    _n += _count
CONST_W = _n
PARAM = {}
_n = 0
for _name, _count in [("norm_gain", KT), ("gate_gain", KT), ("mix_gain", KT), ("ffn_gain", KT),
                      ("conv_w", CONV_J * 3), ("conv_w2", KT * 4), ("conv_b2", KT), ("ba", KT), ("bx", KT),
                      ("lam", KT), ("kv_gain", RT), ("q_gain", HD), ("k_gain", HD), ("sinks", QH),
                      ("idx_g", ID), ("idx_b", ID)]:
    PARAM[_name] = (_n, _n + _count)
    _n += _count
PARAM_W = _n


class Steps:

    def __init__(self, eng, sem):
        self.eng, self.sem, self.n, self.offset = eng, sem, 0, 0

    def __call__(self, instruction):
        instruction.then_inc(self.sem, 1)
        self.n += 1

    def wait(self):
        self.eng.wait_ge(self.sem, self.offset + self.n)

    @contextmanager
    def turns(self, i, per, count):
        base = self.n
        self.offset = i * per
        yield
        assert self.n - base == per, (self.n - base, per)
        self.offset = 0
        self.n = base + per * count


def build(nc, stream, x, p_t, rows, consts, params, rg_w, ukv, keys_t, out):
    ctx = ExitStack()
    with ctx:
        def sb(name, shape, dt=F32):
            return ctx.enter_context(nc.sbuf_tensor(name, shape, dt))

        def sem(name):
            return ctx.enter_context(nc.semaphore(name))

        raw = sb("raw", [P, SLOTS, UNIT])
        w_hi = sb("w_hi", [P, SLOTS, UNIT], F32R)
        w_lo = sb("w_lo", [P, SLOTS, UNIT], F32R)
        act_hi = sb("act_hi", [P, KT, S], F32R)
        act_lo = sb("act_lo", [P, KT, S], F32R)
        big = sb("big", [P, NB * S])
        cst = sb("cst", [P, CONST_W])
        par = sb("par", [P, PARAM_W])
        slot_t = sb("slot_t", [P, 3, S])
        hot = sb("hot", [P, 2, 4, P])
        stat = sb("stat", [P, 176])
        banks = [ctx.enter_context(nc.psum_tensor(f"bank{i}", [P, 512], F32)) for i in range(8)]
        x_kept = nc.dram_tensor("x_kept", (P, TT * D), F32, kind="Internal").ap()
        z_kept = nc.dram_tensor("z_kept", (EARLY, P, S), F32, kind="Internal").ap()

        def at(lo, n):
            return big[:, lo:lo + n]

        def c(name):
            return cst[:, CONST[name][0]:CONST[name][1]]

        def pa(name):
            return par[:, PARAM[name][0]:PARAM[name][1]]

        ident = c("ident")
        iota = c("iota")

        X = at(0, TT * D).rearrange("p (t n) -> p t n", t=TT)
        E = at(4096, TT * D).rearrange("p (t n) -> p t n", t=TT)
        XN = at(8192, TT * D).rearrange("p (t n) -> p t n", t=TT)
        ZT = at(12288, TT * QKVG_W).rearrange("p (t n) -> p t n", t=TT)
        ple_row = at(12288, D)
        gate_row = at(12288, D)
        MIXT = at(17408, KT * S).rearrange("p (k n) -> p k n", k=KT)
        PT = at(17408, 2 * S)
        QT = at(21504, 8 * S).rearrange("p (k n) -> p k n", k=8)
        KTP = at(23552, KVH * 3 * P).rearrange("p (k n) -> p k n", k=KVH)
        VP = at(25088, 3 * KV_W).rearrange("p (k n) -> p k n", k=3)
        KD = at(25856, TT * KVH * 2 * HD)
        YM = at(26880, TT * ATTN_W).rearrange("p (t n) -> p t n", t=TT)
        SC = at(28928, GROUP * 2 * P)
        ET = at(29952, GROUP * 2 * P)
        SC_G = [at(28928, 512), at(29440, 512)]
        QST = at(30976, 2 * P).rearrange("p (k n) -> p k n", k=2)
        KST = at(31232, 2 * P)
        CC = at(31488, S)
        CU = at(31744, S + 4)
        CY = at(32004, S)
        CG = at(32260, S)
        MIX2 = at(4096, KT * S).rearrange("p (k n) -> p k n", k=KT)
        RGW = at(8192, KT * 2 * P).rearrange("p (k n) -> p k n", k=KT)
        RA = at(12288, KT * S).rearrange("p (k n) -> p k n", k=KT)
        RW = at(16384, KT * S).rearrange("p (k n) -> p k n", k=KT)
        RX = at(20480, KT * S).rearrange("p (k n) -> p k n", k=KT)
        QT2 = at(24576, H2 * S).rearrange("p (k n) -> p k n", k=H2)
        CKV = at(28672, TT * RANK).rearrange("p (t n) -> p t n", t=TT)
        UKV = at(28672, 8 * P).rearrange("p (k n) -> p k n", k=8)
        CKVT = at(29696, RT * S).rearrange("p (k n) -> p k n", k=RT)
        ISC = at(30720, TT * S).rearrange("p (t n) -> p t n", t=TT)
        AMASK = at(31232, TT * S)
        KW = at(31744, TT * P).rearrange("p (t n) -> p t n", t=TT)
        KID = at(32000, TT * P).rearrange("p (t n) -> p t n", t=TT)
        KIT = at(32256, S)
        KWT = at(15360, S)
        IWORK = at(6200, TT * S).rearrange("p (t n) -> p t n", t=TT)
        QIS = at(13312, 2 * S).rearrange("p (k n) -> p k n", k=2)
        REL = at(14336, 4 * S).rearrange("p (k n) -> p k n", k=4)
        XP = at(4096, S + 4)
        XC = at(4400, S)
        RI = at(4700, 2 * S)
        TH = at(5300, S)
        THD = at(5600, S)
        WST = at(5900, 2 * P)
        KTS = at(8192, S)
        VS = at(8448, S).rearrange("p (k n) -> p k n", k=2)
        LG = at(8704, TT * S).rearrange("p (t n) -> p t n", t=TT)
        PTS = at(9216, 2 * S)
        TG = at(9728, S)
        TA = at(9984, S)
        QS2 = at(10240, S)
        HU = at(10496, S)
        YH = at(10752, S)
        PQS = at(12288, 2 * S).rearrange("p (k n) -> p k n", k=2)
        PS = at(12800, 2 * 2 * P).rearrange("p (a t n) -> p a t n", a=2, t=TT)
        V12 = at(13312, 2 * PH * TT * PK).rearrange("p (h a t k) -> p h a t k", h=PH, a=2, t=TT)
        I12 = at(13824, 2 * PH * TT * PK).bitcast(U32).rearrange("p (h a t k) -> p h a t k", h=PH, a=2, t=TT)
        CAND = at(14336, TT * PK * PK).rearrange("p (t n) -> p t n", t=TT)
        CV = at(14848, PH * TT * PK).rearrange("p (h t k) -> p h t k", h=PH, t=TT)
        CP = at(15104, PH * TT * PK).bitcast(U32).rearrange("p (h t k) -> p h t k", h=PH, t=TT)
        I12F = at(15360, 2 * PH * TT * PK).rearrange("p (h a t k) -> p h a t k", h=PH, a=2, t=TT)
        CA = at(15872, 2 * SLOT_N * TT).rearrange("p (a n) -> p a n", a=2)
        CAU = at(16384, 2 * SLOT_N * TT).bitcast(U32).rearrange("p (a n) -> p a n", a=2)
        PICK = at(16896, 3 * SLOT_N * TT).rearrange("p (a h t k) -> p a h t k", a=3, h=PH, t=TT)
        PICKT = at(17664, 3 * SLOT_N * TT).rearrange("p (a t h k) -> p a t h k", a=3, h=PH, t=TT)
        EQ = at(18432, SLOT_N * TT * PK)
        KEYT = at(22528, 2 * KEYS).rearrange("p (a n) -> p a n", a=2)

        G = big[:, :].rearrange("p (b t) -> p b t", b=NB)
        GZ = c("band").rearrange("p (s n) -> p s n", s=2)
        GB = c("causal").rearrange("p (s n) -> p s n", s=2)
        XF = raw[:, :, :].rearrange("p a b -> p (a b)").rearrange("p (t n) -> p t n", t=TT)
        final_row = at(0, D)
        OUT = at(4096, TT * D).rearrange("p (t n) -> p t n", t=TT)
        SQ = at(8192, TT * D).rearrange("p (t n) -> p t n", t=TT)

        ss = stat[:, 0:2]
        std = stat[:, 2:4]
        rstd = stat[:, 4:6]
        warm = stat[:, 6:7]
        ss40 = stat[:, 8:48]
        ss4 = stat[:, 8:16]
        nsink = stat[:, 48:64]
        mx = stat[:, 64:68]
        nm = stat[:, 68:72]
        dsink = stat[:, 72:76]
        esum = stat[:, 76:80]
        esink = stat[:, 80:84]
        rec = stat[:, 84:88]
        sp_a = stat[:, 88:104]
        sp_b = stat[:, 104:120]
        sp_c = stat[:, 120:136]
        nba = stat[:, 136:152]
        hbx = stat[:, 152:168]
        top8 = [stat[:, 168:176], stat[:, 8:16]]
        csum = stat[:, 88:104]
        crec = stat[:, 104:120]
        idx8 = stat[:, 8:16]
        c_pos = sp_a
        c_neg = sp_b

        raw_ready = [sem(f"raw_ready{i}") for i in range(SLOTS)]
        hi_ready = sem("hi_ready")
        lo_ready = sem("lo_ready")
        unit_done = sem("unit_done")
        const_ready = sem("const_ready")
        x_ready = [sem(f"x_ready{t}") for t in range(TT)]
        pt_ready = sem("pt_ready")
        ple_row_ready = sem("ple_row_ready")
        gate_row_ready = sem("gate_row_ready")
        rgw_ready = sem("rgw_ready")
        keys_ready = sem("keys_ready")
        ukv_ready = sem("ukv_ready")
        final_ready = sem("final_ready")
        xf_ready = [sem(f"xf_ready{t}") for t in range(TT)]
        x_saved = sem("x_saved")
        out_saved = sem("out_saved")
        v_step = sem("vector_step")
        s_step = sem("scalar_step")
        g_step = sem("gpsimd_step")
        squares = sem("squares")
        warm_ready = sem("warm_ready")
        mean_ready = sem("mean_ready")
        std_ready = sem("std_ready")
        normed = sem("normed")
        e_normed = sem("e_normed")
        turned = sem("turned")
        act_hi_ready = sem("act_hi_ready")
        act_lo_ready = sem("act_lo_ready")
        ple_done = sem("ple_done")
        ple_taken = sem("ple_taken")
        qkvg_taken_s = [sem(f"qkvg_taken_s{n}") for n in range(2)]
        qkvg_taken_v = [sem(f"qkvg_taken_v{n}") for n in range(2)]
        qk_squares = sem("qk_squares")
        silu_tanh = sem("silu_tanh")
        qk_mean = sem("qk_mean")
        qk_std = sem("qk_std")
        qk_ready = sem("qk_ready")
        qk_turned = sem("qk_turned")
        qk_kept = sem("qk_kept")
        conv_gate = sem("conv_gate")
        conv_gate_used = sem("conv_gate_used")
        conv_c = sem("conv_c")
        conv_h_used = sem("conv_h_used")
        conv_b_used = sem("conv_b_used")
        staged = sem("staged")
        scored = sem("scored")
        sc_max = sem("sc_max")
        exps = sem("exps")
        probs_turned = sem("probs_turned")
        probs_kept = sem("probs_kept")
        mixed = sem("mixed")
        mix_used = sem("mix_used")
        ym_turned = sem("ym_turned")
        added = [sem(f"added{n}") for n in range(2)]
        gate_pre = sem("gate_pre")
        gate_tanh = sem("gate_tanh")
        gated = [sem(f"gated{n}") for n in range(2)]
        ckv_kept = sem("ckv_kept")
        kwt_kept = sem("kwt_kept")
        kw_turned = sem("kw_turned")
        kw_kept = sem("kw_kept")
        ckv_squares = sem("ckv_squares")
        ckv_mean = sem("ckv_mean")
        ckv_std = sem("ckv_std")
        ckv_normed = sem("ckv_normed")
        ki_ready = sem("ki_ready")
        ckv_turned = sem("ckv_turned")
        ckvt_kept = sem("ckvt_kept")
        qi_kept = sem("qi_kept")
        qi_scored = sem("qi_scored")
        rel_ready = sem("rel_ready")
        rel_used = sem("rel_used")
        xr_kept = sem("xr_kept")
        xc_ready = sem("xc_ready")
        w_staged = sem("w_staged")
        rg_done = sem("rg_done")
        rg_exp = sem("rg_exp")
        r_ready = sem("r_ready")
        a_ready = sem("a_ready")
        q2_kept = sem("q2_kept")
        th_used = sem("th_used")
        softplus_ready = sem("softplus_ready")
        rw_root = sem("rw_root")
        rw_ready = sem("rw_ready")
        gr_tanh = sem("gr_tanh")
        ga_tanh = sem("ga_tanh")
        gr_used = sem("gr_used")
        k_made = sem("k_made")
        v_made = sem("v_made")
        k_kept = sem("k_kept")
        v_kept = sem("v_kept")
        q_staged = sem("q_staged")
        logits_made = sem("logits_made")
        max_ready = sem("max_ready")
        p_exp = sem("p_exp")
        p_ready = sem("p_ready")
        p_turned = sem("p_turned")
        p_kept = sem("p_kept")
        y_made = sem("y_made")
        head_mixed = sem("head_mixed")
        pq_kept = [sem(f"pq_kept{n}") for n in range(2)]
        ps_made = [sem(f"ps_made{n}") for n in range(2)]
        ps_kept = [sem(f"ps_kept{n}") for n in range(2)]
        ps_used = [sem(f"ps_used{n}") for n in range(2)]
        pick_diff = sem("pick_diff")
        pick_exp = sem("pick_exp")
        picks_ready = sem("picks_ready")
        picks_turned = sem("picks_turned")
        slots_kept = sem("slots_kept")
        hot_turn = sem("hot_turn")
        hot1 = sem("hot1")
        hot2 = sem("hot2")
        hot_used = [sem(f"hot_used{n}") for n in range(4)]
        gate_kept = [sem(f"gate_kept{n}") for n in range(2)]
        gelu_ready = [sem(f"gelu_ready{n}") for n in range(2)]
        z_saved = [sem(f"z_saved{n}") for n in range(2)]
        z_back = [sem(f"z_back{n}") for n in range(2)]
        early_ready = [sem(f"early_ready{n}") for n in range(2)]
        act_ready = [sem(f"act_ready{n}") for n in range(2)]
        eh_ready = sem("eh_ready")
        el_ready = sem("el_ready")
        y_added = sem("y_added")
        fin_squares = sem("fin_squares")
        fin_mean = sem("fin_mean")
        fin_std = sem("fin_std")
        fin_ready = sem("fin_ready")

        def unit_slot(odd, u):
            return 2 * odd + u

        def split_hi(act, pair, half, odd, first=False, units=(0, 1)):
            for u in units:
                s = unit_slot(odd, u)
                act.wait_ge(raw_ready[s], 16 * half + 16)
                if not first:
                    act.wait_ge(unit_done, 2 * pair + u - 3)
                act.activation(w_hi[:, s, :], raw[:, s, :], ACT.Copy).then_inc(hi_ready, 1)

        def split_lo(dve, pair, half, odd, first=False, units=(0, 1)):
            for u in units:
                s = unit_slot(odd, u)
                dve.wait_ge(hi_ready, 2 * pair + u + 1)
                if not first:
                    dve.wait_ge(unit_done, 2 * pair + u - 3)
                dve.tensor_tensor(w_lo[:, s, :], raw[:, s, :], w_hi[:, s, :].bitcast(F32),
                                  ALU.subtract).then_inc(lo_ready, 1)

        def ahead(split, eng, part, i, per, k, units=(0, 1)):
            base = FIRST[part] + k + 2
            split(eng, i * per + base, i * (per // 2) + base // 2, base % 2, units=units)

        def pair_of(part, i, per, k):
            return i * per + (FIRST[part] + k)

        def columns_out(pe, pair, odd, out_ap, units=(0, 1), fills=None):
            for u in units:
                if fills and u == 1:
                    pe.wait_ge(act_lo_ready, fills * KT)
                s = unit_slot(odd, u)
                pe.wait_ge(lo_ready, 2 * pair + u + 1)
                for kk in range(8):
                    k = 8 * u + kk
                    hi = w_hi[:, s, kk * P:(kk + 1) * P]
                    lo = w_lo[:, s, kk * P:(kk + 1) * P]
                    pe.matmul(out_ap, hi, act_hi[:, k, :], start=(k == 0), stop=False)
                    pe.matmul(out_ap, hi, act_lo[:, k, :], start=False, stop=False)
                    mm = pe.matmul(out_ap, lo, act_hi[:, k, :], start=False, stop=(k == KT - 1))
                mm.then_inc(unit_done, 1)

        def tokens_out(pe, part, i, per, k0, outs, fills):
            for uu in range(8):
                if uu == 4:
                    pe.wait_ge(act_lo_ready, fills * KT)
                pair = pair_of(part, i, per, k0 + uu // 2)
                s = unit_slot((FIRST[part] + k0 + uu // 2) % 2, uu % 2)
                pe.wait_ge(lo_ready, 2 * pair + uu % 2 + 1)
                for kk in range(2):
                    k = 2 * uu + kk
                    hi = w_hi[:, s, kk * 512:(kk + 1) * 512]
                    lo = w_lo[:, s, kk * 512:(kk + 1) * 512]
                    for t in range(TT):
                        a_hi = act_hi[:, k, t * P:(t + 1) * P]
                        a_lo = act_lo[:, k, t * P:(t + 1) * P]
                        pe.matmul(outs[t], a_hi, hi, start=(k == 0), stop=False)
                        pe.matmul(outs[t], a_hi, lo, start=False, stop=False)
                        mm = pe.matmul(outs[t], a_lo, hi, start=False, stop=(k == KT - 1))
                mm.then_inc(unit_done, 1)

        primed = [y_made, z_saved, early_ready, scored, rg_done, logits_made, hot2, hot_used, conv_b_used,
                  conv_h_used, conv_gate_used, qi_scored, rel_used, xc_ready, th_used, gr_used, head_mixed, ps_made,
                  ps_used, act_ready, qkvg_taken_s, qkvg_taken_v, probs_kept, mix_used, added, gated, rel_ready,
                  xr_kept, q2_kept, rg_exp, k_kept, v_kept, p_exp, ga_tanh, p_kept, ps_kept, gate_kept, gelu_ready]

        block = ctx.enter_context(nc.Block())

        @block.sync
        def _(sp):
            def load(n, turn, s):
                sp.dma_start(raw[:, s, :], stream[bass.ds(n, 1), :, :].rearrange("o p n -> (o p) n"))\
                  .then_inc(raw_ready[s], 16)

            sp.dma_start(PT, p_t).then_inc(pt_ready, 16)
            for s in range(SLOTS):
                sp.dma_start(raw[:, s, :], stream[s, :, :]).then_inc(raw_ready[s], 16)
                if s % 2:
                    t = s // 2
                    sp.dma_start(X[:, t, :], x[0, t * P:(t + 1) * P, :]).then_inc(x_ready[t], 16)
            sp.dma_start(cst[:, :], consts).then_inc(const_ready, 16)
            sp.dma_start(par[:, :], params).then_inc(const_ready, 16)
            sp.dma_start(ple_row, rows[0, :, :]).then_inc(ple_row_ready, 16)
            with sp.Fori(1, UNITS // SLOTS) as q:
                for s in range(SLOTS):
                    sp.wait_ge(lo_ready, q * SLOTS + (s + 1 - SLOTS))
                    load(q * SLOTS + s, q, s)
            sp.wait_ge(x_saved, 16)
            for t in range(TT):
                sp.wait_ge(lo_ready, UNITS - 2 + 2 * t)
                sp.dma_start(XF[:, t, :], x_kept[:, t * D:(t + 1) * D]).then_inc(xf_ready[t], 16)
            for t in range(TT):
                for half in range(2):
                    cols = slice(half * 1024, (half + 1) * 1024)
                    sp.wait_ge(fin_ready, 2 * t + half + 1)
                    sp.dma_start(out[0, t * P:(t + 1) * P, cols], OUT[:, t, cols]).then_inc(out_saved, 16)
            sp.wait_ge(out_saved, 32 * TT)

        @block.gpsimd
        def _(pool):
            step = Steps(pool, g_step)
            for one in primed:
                for each in one if isinstance(one, list) else [one]:
                    pool.sem_inc(each, 1)
            with pool.Fori(0, TT) as t:
                with pool.Fori(0, KVH) as g:
                    u = t * KVH + g
                    pool.wait_ge(qk_kept, 12)
                    pool.wait_ge(scored, u + 1)
                    pool.tensor_copy(QST, QT[:, bass.ds(2 * g, 2), bass.ds(t * P, P)]).then_inc(staged, 1)
                    pool.tensor_copy(KST, KTP[:, bass.ds(g, 1), bass.ds(t * P, 2 * P)]
                                     .rearrange("p o n -> p (o n)")).then_inc(staged, 1)
            with pool.Fori(0, KT) as j:
                pool.wait_ge(rgw_ready, 16)
                pool.wait_ge(rg_done, j + 1)
                pool.tensor_copy(WST, RGW[:, bass.ds(j, 1), :].rearrange("p o n -> p (o n)")).then_inc(w_staged, 1)
            pool.wait_ge(q2_kept, H2 + 1)
            with pool.Fori(0, H2) as h:
                pool.wait_ge(logits_made, h + 1)
                pool.tensor_copy(QS2, QT2[:, bass.ds(h, 1), :].rearrange("p o n -> p (o n)")).then_inc(q_staged, 1)
            pool.wait_ge(slots_kept, 3)

            with pool.Fori(0, S // 8) as i:
                pool.wait_ge(hot2, i * 8 + 1)
                pool.tensor_copy(idx8, slot_t[:, 1, bass.ds(i * 8, 8)]).then_inc(g_step, 1)
                pool.wait_ge(g_step, i + 1)
                for s in range(8):
                    pool.wait_ge(hot_used[s % 4], i * 2 + s // 4 + 1)
                    pool.sem_inc(hot_turn, 1)
                    pool.tensor_scalar(hot[:, 1, s % 4, :], iota, idx8[:, s:s + 1], None, ALU.is_equal)\
                        .then_inc(hot2, 1)

        @block.scalar
        def _(act):
            step = Steps(act, s_step)
            act.wait_ge(warm_ready, 1)

            def warm_root():
                act.activation(warm, warm, ACT.Sqrt).then_inc(s_step, 1)

            warm_root()

            def square_sums(i, src):
                if i:
                    act.wait_ge(std_ready, i)
                for t in range(TT):
                    if not i:
                        act.wait_ge(x_ready[t], 16)
                    act.activation(XN[:, t, :], src[:, t, :], ACT.Square, accum_out=ss[:, t:t + 1])\
                       .then_inc(squares, 1)
                act.wait_ge(mean_ready, i + 1)
                act.activation(std, ss, ACT.Sqrt).then_inc(std_ready, 1)

            def keep_hi(n, gain):
                for k in range(KT):
                    act.wait_ge(turned, n * KT + k + 1)
                    act.activation(act_hi[:, k, :], banks[k % 8][:, 0:S], ACT.Copy, scale=gain[:, k:k + 1])\
                       .then_inc(act_hi_ready, 1)

            act.wait_ge(pt_ready, 16)
            act.activation(act_hi[:, 0:2, :].rearrange("p k n -> p (k n)"), PT, ACT.Copy).then_inc(ple_taken, 1)
            split_hi(act, 0, 0, 0, first=True)
            split_hi(act, 1, 0, 1, first=True)
            square_sums(0, X)
            for cb in range(4):
                act.wait_ge(unit_done, cb + 1)
                act.activation(E[:, 0, cb * 512:(cb + 1) * 512], banks[2 * cb][:, :], ACT.Copy).then_inc(ple_taken, 1)
            ahead(split_hi, act, "ple", 0, 2, 0)
            act.wait_ge(const_ready, 32)
            keep_hi(0, pa("norm_gain"))
            ahead(split_hi, act, "ple", 0, 2, 1)
            act.wait_ge(ple_taken, 9)
            act.wait_ge(turned, KT)
            square_sums(1, E)

            def take_qkvg(c_, i, per, k0, n):
                for k in range(4):
                    ahead(split_hi, act, "qkvg", i, per, k0 + k)
                act.wait_ge(e_normed, 1)
                act.wait_ge(unit_done, 2 * pair_of("qkvg", i, per, k0 + 3) + 2)
                act.activation(ZT[:, 0, bass.ds(c_ * 512, 512)], banks[2 * n][:, :], ACT.Copy)\
                   .then_inc(qkvg_taken_s[n], 1)

            for b in range(3):
                take_qkvg(b, 0, 8, 4 * b, b % 2)
            act.wait_ge(qkvg_taken_s[0], 3)
            act.wait_ge(qkvg_taken_s[1], 2)
            act.wait_ge(qkvg_taken_v[0], 3)
            act.wait_ge(qkvg_taken_v[1], 2)
            for t in range(TT):
                act.activation(XN[:, t, 0:1280], ZT[:, t, 0:1280], ACT.Square).then_inc(qk_squares, 1)
            act.wait_ge(qk_mean, 1)
            act.activation(ss40, ss40, ACT.Sqrt).then_inc(qk_std, 1)
            for b in range(3, 5):
                take_qkvg(b, 0, 8, 4 * b, b % 2)
            act.wait_ge(qk_turned, 16)
            for k in range(8):
                act.activation(QT[:, k, :], banks[4 + k // 2][:, (k % 2) * S:(k % 2 + 1) * S], ACT.Copy)\
                   .then_inc(qk_kept, 1)

            for n in range(2):
                act.wait_ge(qkvg_taken_s[n], 3 - n + 1)
                act.wait_ge(qkvg_taken_v[n], 3 - n + 1)
            act.activation(YM, ZT[:, :, 1536:2560], ACT.Tanh, scale=0.5).then_inc(silu_tanh, 1)
            with act.Fori(0, CONV_J) as j:
                ahead(split_hi, act, "conv", j, 4, 0)
                act.wait_ge(unit_done, 2 * pair_of("conv", j, 4, 0) + 2)
                act.wait_ge(conv_b_used, j + 1)
                act.activation(CG, banks[0][:, 0:S], ACT.Tanh, scale=0.5).then_inc(conv_gate, 1)
                act.wait_ge(sc_max, j + 1)
                for h in range(GROUP):
                    act.activation(SC[:, h * S:(h + 1) * S], SC[:, h * S:(h + 1) * S], ACT.Exp,
                                   bias=nm[:, h:h + 1], accum_out=esum[:, h:h + 1]).then_inc(exps, 1)
                act.activation(esink, dsink, ACT.Exp).then_inc(exps, 1)
                ahead(split_hi, act, "conv", j, 4, 1)
                act.wait_ge(unit_done, 2 * pair_of("conv", j, 4, 1) + 2)
                act.wait_ge(conv_h_used, j + 1)
                act.activation(CC, banks[1][:, 0:S], ACT.Copy).then_inc(conv_c, 1)
                ahead(split_hi, act, "conv", j, 4, 2)
                act.wait_ge(probs_turned, j + 1)
                act.activation(ET[:, 0:512], banks[6][:, :], ACT.Copy).then_inc(probs_kept, 1)
                act.activation(ET[:, 512:1024], banks[7][:, :], ACT.Copy).then_inc(probs_kept, 1)
                ahead(split_hi, act, "conv", j, 4, 3)

            for k in range(8):
                act.wait_ge(ym_turned, k + 1)
                act.activation(act_hi[:, k, :], banks[k][:, 0:S], ACT.Copy).then_inc(act_hi_ready, 1)
            act.activation(act_hi[:, 8:16, :], MIXT[:, 8:16, :], ACT.Copy).then_inc(act_hi_ready, 8)

            def block_squares(taken, base, b):
                act.wait_ge(taken[b % 2], base + b // 2 * 2 + 3)
                for t in range(TT):
                    cols = slice(b * 512, (b + 1) * 512)
                    act.activation(XN[:, t, cols], X[:, t, cols], ACT.Square,
                                   accum_out=ss4[:, 4 * t + b:4 * t + b + 1]).then_inc(squares, 1)

            def root_of_sums(i):
                act.wait_ge(mean_ready, i + 1)
                act.activation(std, ss, ACT.Sqrt).then_inc(std_ready, 1)

            def split_and_square(part, base, i):
                for k in range(16):
                    if k == 15:
                        warm_root()
                        block_squares(added, base, 3)
                        root_of_sums(i)
                    ahead(split_hi, act, part, 0, 8, k)
                    if part == "w_out" and k == 5:
                        act.wait_ge(softplus_ready, 1)
                        act.activation(sp_b, sp_a, ACT.Exp, scale=-1.0).then_inc(softplus_ready, 1)
                    if k >= 4 and k % 4 == 1:
                        block_squares(added, base, k // 4 - 1)

            act.dma_start(gate_row, rows[1, :, :]).then_inc(gate_row_ready, 16)
            split_and_square("w_out", 0, 2)
            keep_hi(1, pa("gate_gain"))
            for b in range(4):
                for k in range(4):
                    if k == 3:
                        for t in range(TT):
                            act.wait_ge(gate_pre, 2 * b + t + 1)
                            act.activation(SC_G[t], SC_G[t], ACT.Tanh, scale=0.5).then_inc(gate_tanh, 1)
                    if 4 * b + k < 15:
                        ahead(split_hi, act, "gate", 0, 8, 4 * b + k)
                    if b and k == 1:
                        block_squares(gated, 0, b - 1)
            warm_root()
            block_squares(gated, 0, 3)
            root_of_sums(3)
            ahead(split_hi, act, "gate", 0, 8, 15)
            keep_hi(2, pa("mix_gain"))

            act.dma_start(RGW, rg_w).then_inc(rgw_ready, 16)
            for k in range(4):
                ahead(split_hi, act, "ckv", 0, 4, k)
            act.wait_ge(unit_done, 2 * pair_of("ckv", 0, 4, 3) + 2)
            for t in range(TT):
                act.activation(CKV[:, t, :], banks[t][:, :], ACT.Copy).then_inc(ckv_kept, 1)
            act.wait_ge(unit_done, 2 * pair_of("kiwi", 0, 2, 0) + 2)
            act.activation(KWT, banks[2][:, 0:S], ACT.Copy).then_inc(kwt_kept, 1)
            ahead(split_hi, act, "kiwi", 0, 2, 0)
            act.wait_ge(kw_turned, 1)
            for t in range(TT):
                act.activation(KW[:, t, 0:80], banks[3][:, t * P:t * P + 80], ACT.Copy).then_inc(kw_kept, 1)
            ahead(split_hi, act, "kiwi", 0, 2, 1)
            act.wait_ge(ckv_kept, 2)
            for t in range(TT):
                act.activation(REL[:, 2 * t:2 * t + 2, :].rearrange("p a n -> p (a n)"), CKV[:, t, :], ACT.Square,
                               accum_out=ss[:, t:t + 1]).then_inc(ckv_squares, 1)
            act.wait_ge(ckv_mean, 1)
            act.activation(stat[:, 8:12], stat[:, 8:12], ACT.Sqrt).then_inc(ckv_std, 1)
            def index_queries(i, n):
                ahead(split_hi, act, "qi", i, 2, n)
                act.wait_ge(unit_done, 2 * pair_of("qi", i, 2, n) + 2)
                if n >= 2:
                    act.wait_ge(qi_scored, i * 2 + n - 1 + 1)
                act.activation(QIS[:, n % 2, :], banks[n % 2][:, 0:S], ACT.Copy).then_inc(qi_kept, 1)

            def index_relu(i, n):
                act.wait_ge(qi_scored, i * 2 + n + 2)
                act.wait_ge(rel_used, i * 8 + 4 * n + 1)
                for b in range(2):
                    act.activation(REL[:, 2 * b:2 * b + 2, :].rearrange("p a n -> p (a n)"), banks[4 + b][:, :],
                                   ACT.Relu, scale=ID ** -0.5).then_inc(rel_ready, 1)

            for n in range(2):
                index_queries(0, n)
            for k in range(RT):
                act.wait_ge(ckv_turned, 2 * (k // 2) + 2)
                act.activation(CKVT[:, k, :], banks[4 + k // 2][:, (k % 2) * S:(k % 2 + 1) * S], ACT.Copy,
                               scale=pa("kv_gain")[:, k:k + 1]).then_inc(ckvt_kept, 1)
            act.wait_ge(ckv_turned, RT + 1)
            act.dma_start(UKV, ukv[0:1, :, :].rearrange("o p (k n) -> p (o k) n", n=P)).then_inc(ukv_ready, 16)
            act.activation(KIT, banks[6][:, 0:S], ACT.Copy).then_inc(ckvt_kept, 1)

            with act.Fori(0, IH // 4 - 1) as i:
                for n in range(2):
                    index_relu(i, n)
                    index_queries(i, n + 2)
            for n in range(2):
                index_relu(IH // 4 - 1, n)

            act.wait_ge(softplus_ready, 3)
            def rnn_gates(j):
                act.wait_ge(rg_done, j + 2)
                act.wait_ge(th_used, j + 1)
                act.activation(RI[:, 0:S], banks[4][:, 0:S], ACT.Exp, scale=-1.0,
                               bias=nba[:, bass.ds(j, 1)]).then_inc(rg_exp, 1)
                act.activation(RI[:, S:2 * S], banks[4][:, S:2 * S], ACT.Tanh, scale=0.5,
                               bias=hbx[:, bass.ds(j, 1)]).then_inc(rg_exp, 1)

            def rnn_decay(j):
                act.wait_ge(r_ready, j + 1)
                act.activation(RA[:, bass.ds(j, 1), :].rearrange("p o n -> p (o n)"), RI[:, 0:S], ACT.Exp,
                               scale=c_neg[:, bass.ds(j, 1)]).then_inc(a_ready, 1)
                act.activation(TH, RI[:, 0:S], ACT.Tanh, scale=c_pos[:, bass.ds(j, 1)]).then_inc(a_ready, 1)

            def rnn_block(j, first=False):
                ahead(split_hi, act, "rnn", j, 2, 0, units=(0,))
                act.wait_ge(unit_done, 2 * pair_of("rnn", j, 2, 0) + 2)
                act.wait_ge(xc_ready, j + 1)
                act.activation(XP[:, 3:3 + S], banks[0][:, 0:S], ACT.Copy).then_inc(xr_kept, 1)
                if not first:
                    rnn_gates(j - 1)
                ahead(split_hi, act, "rnn", j, 2, 0, units=(1,))
                if not first:
                    rnn_decay(j - 1)
                ahead(split_hi, act, "rnn", j, 2, 1)
                act.wait_ge(unit_done, 2 * pair_of("rnn", j, 2, 1) + 2)
                act.activation(QT2[:, bass.ds(j, 1), :].rearrange("p o n -> p (o n)"), banks[1][:, 0:S],
                               ACT.Copy).then_inc(q2_kept, 1)

            rnn_block(0, first=True)
            with act.Fori(1, KT) as j:
                rnn_block(j)
            rnn_gates(KT - 1)
            rnn_decay(KT - 1)



            def head(h, first=False, last=False):
                act.wait_ge(k_made, h + 1)
                act.wait_ge(logits_made, h + 1)
                act.activation(KTS, banks[2][:, 0:S], ACT.Copy).then_inc(k_kept, 1)
                if not last:
                    act.wait_ge(v_made, h + 1)
                    act.dma_start(UKV, ukv[bass.ds(h + 1, 1), :, :].rearrange("o p (k n) -> p (o k) n", n=P))\
                       .then_inc(ukv_ready, 16)
                ahead(split_hi, act, "heads", h, 2, 0)
                act.wait_ge(unit_done, 2 * pair_of("heads", h, 2, 0) + 2)
                act.wait_ge(gr_used, h + 1)
                act.activation(TG, banks[0][:, 0:S], ACT.Tanh, scale=0.5).then_inc(gr_tanh, 1)
                if first:
                    act.wait_ge(rw_ready, 1)
                    act.activation(RW, RW, ACT.Sqrt, scale=0.25).then_inc(rw_root, 1)
                act.wait_ge(max_ready, h + 1)
                for t in range(TT):
                    act.activation(LG[:, t, :], LG[:, t, :], ACT.Exp, bias=nm[:, t:t + 1],
                                   accum_out=esum[:, t:t + 1]).then_inc(p_exp, 1)
                ahead(split_hi, act, "heads", h, 2, 1)
                act.wait_ge(unit_done, 2 * pair_of("heads", h, 2, 1) + 2)
                act.wait_ge(head_mixed, h + 1)
                act.activation(TA, banks[1][:, 0:S], ACT.Tanh, scale=0.5).then_inc(ga_tanh, 1)
                act.wait_ge(p_turned, h + 1)
                act.wait_ge(y_made, h + 1)
                act.activation(PTS, banks[5][:, :], ACT.Copy).then_inc(p_kept, 1)

            head(0, first=True)
            with act.Fori(1, H2 - 1) as h:
                head(h)
            head(H2 - 1, last=True)

            for k in range(4):
                act.wait_ge(head_mixed, 4 * k + 5)
                act.activation(act_hi[:, 4 * k:4 * k + 4, :], MIX2[:, 4 * k:4 * k + 4, :], ACT.Copy)\
                   .then_inc(act_hi_ready, 4)
            split_and_square("w_o", 4, 4)
            act.dma_start(x_kept.rearrange("p (t n) -> p t n", t=TT), X).then_inc(x_saved, 16)
            act.dma_start(KEYT, keys_t).then_inc(keys_ready, 16)
            keep_hi(3, pa("ffn_gain"))

            def early(pair, b2, n):
                act.wait_ge(unit_done, 2 * pair + 2)
                act.wait_ge(z_saved[n], b2 * 16 + 1)
                act.activation(GZ[:, n, :], banks[2 + n][:, 0:S], ACT.Gelu).then_inc(gelu_ready[n], 1)
                act.wait_ge(gelu_ready[n], b2 + 2)
                act.dma_start(z_kept[bass.ds(b2 * 2 + n, 1), :, :].rearrange("o p n -> (o p) n"), GZ[:, n, :])\
                   .then_inc(z_saved[n], 16)

            with act.Fori(0, PH) as h:
                def keep_query(a):
                    act.wait_ge(unit_done, 2 * pair_of("wqu", h, 4, a) + 2)
                    act.wait_ge(ps_made[a], h + 1)
                    act.activation(PQS[:, a, :], banks[a][:, 0:S], ACT.Copy).then_inc(pq_kept[a], 1)

                def keep_scores(a):
                    act.wait_ge(ps_made[a], h + 2)
                    act.wait_ge(ps_used[a], h + 1)
                    act.activation(PS[:, a, :, :].rearrange("p t n -> p (t n)"), banks[4 + a][:, 0:S],
                                   ACT.Copy).then_inc(ps_kept[a], 1)

                ahead(split_hi, act, "wqu", h, 4, 0)
                keep_query(0)
                ahead(split_hi, act, "wqu", h, 4, 1)
                keep_query(1)
                keep_scores(0)
                ahead(split_hi, act, "wqu", h, 4, 2)
                early(pair_of("wqu", h, 4, 2), h, 0)
                keep_scores(1)
                ahead(split_hi, act, "wqu", h, 4, 3)
                early(pair_of("wqu", h, 4, 3), h, 1)

            def early_turn(i):
                for n in range(2):
                    ahead(split_hi, act, "u_decode", i, 2, n)
                    early(pair_of("u_decode", i, 2, n), i + PH, n)

            with act.Fori(0, PH // 2) as i:
                early_turn(i)
            act.wait_ge(pick_diff, 1)
            act.activation(CV, CV, ACT.Exp).then_inc(pick_exp, 1)
            with act.Fori(PH // 2, PH) as i:
                early_turn(i)
            for a in range(3):
                act.wait_ge(picks_turned, 2 * a + 2)
                act.activation(slot_t[:, a, :], banks[4 + a][:, 0:S], ACT.Copy).then_inc(slots_kept, 1)
            act.wait_ge(slots_kept, 3)
            act.wait_ge(x_saved, 16)
            with act.Fori(0, S // 16) as i:
                for n in range(2):
                    def keep_gates(m):
                        act.wait_ge(hot_used[3], i * 4 + 2 * n + m + 2)
                        act.activation(G[:, :, bass.ds(i * 16 + (8 * n + 4 * m), 4)],
                                       banks[m][:, :].rearrange("p (t b) -> p b t", t=4), ACT.Copy)\
                           .then_inc(gate_kept[m], 1)

                    ahead(split_hi, act, "u_gates", i, 2, n, units=(0,))
                    keep_gates(0)
                    ahead(split_hi, act, "u_gates", i, 2, n, units=(1,))
                    early(pair_of("u_gates", i, 2, n), i + 2 * PH, n)
                    keep_gates(1)

            for n in range(2):
                act.wait_ge(z_saved[n], 16 * (EARLY // 2) + 1)
            with act.Fori(0, EARLY // 2) as i:
                for n in range(2):
                    act.wait_ge(early_ready[n], i + 1)
                    act.dma_start(GB[:, n, :], z_kept[bass.ds(i * 2 + n, 1), :, :].rearrange("o p n -> (o p) n"))\
                       .then_inc(z_back[n], 16)
                    ahead(split_hi, act, "u_late", i, 2, n)
                    act.wait_ge(unit_done, 2 * pair_of("u_late", i, 2, n) + 2)
                    act.wait_ge(act_ready[n], i + 1)
                    act.activation(GZ[:, n, :], banks[2 + n][:, 0:S], ACT.Gelu).then_inc(gelu_ready[n], 1)

            def expert_hi(b, n, done):
                act.wait_ge(unit_done, done)
                act.activation(act_hi[:, n, :], G[:, bass.ds(b, 1), :].rearrange("p o n -> p (o n)"), ACT.Copy)\
                   .then_inc(eh_ready, 1)

            for n in range(2):
                act.wait_ge(early_ready[n], 2)
                expert_hi(n, n, 2 * FIRST["v"])
            for n in range(2):
                act.wait_ge(act_ready[n], EARLY // 2 + 1)
                act.wait_ge(early_ready[n], EARLY // 2 + 1)
            with act.Fori(0, NB // 2 - 1) as i:
                for n in range(2):
                    ahead(split_hi, act, "v", i, 2, n)
                    expert_hi(i * 2 + (2 + n), n, 2 * pair_of("v", i, 2, n) + 2)

            act.wait_ge(el_ready, NB)
            act.dma_start(final_row, rows[2, :, :]).then_inc(final_ready, 16)
            warm_root()
            for cb in range(4):
                for t in range(TT):
                    cols = slice(cb * 512, (cb + 1) * 512)
                    act.wait_ge(y_added, cb * TT + t + 1)
                    act.activation(SQ[:, t, cols], XF[:, t, cols], ACT.Square,
                                   accum_out=ss4[:, 4 * t + cb:4 * t + cb + 1]).then_inc(fin_squares, 1)
            act.wait_ge(fin_mean, 1)
            act.activation(std, ss, ACT.Sqrt).then_inc(fin_std, 1)

        @block.vector
        def _(dve):
            step = Steps(dve, v_step)
            dve.memset(warm, 1.0).then_inc(warm_ready, 1)
            step(dve.memset(KTP, 0.0))
            step(dve.memset(VP, 0.0))
            step(dve.memset(CU[:, 0:2], 0.0))

            def keep_lo(i, gain):
                for k in range(KT):
                    dve.wait_ge(act_hi_ready, i * KT + k + 1)
                    dve.scalar_tensor_tensor(out=act_lo[:, k, :], in0=banks[k % 8][:, 0:S], scalar=gain[:, k:k + 1],
                                             in1=act_hi[:, k, :].bitcast(F32), op0=ALU.mult, op1=ALU.subtract)\
                       .then_inc(act_lo_ready, 1)

            def root(i, sum_ap, n, std_ap, rstd_ap, squares_, mean_, std_sem, need):
                dve.wait_ge(squares_, need)
                dve.tensor_scalar(sum_ap, sum_ap, 1.0 / n, EPS, ALU.mult, ALU.add).then_inc(mean_, 1)
                dve.wait_ge(std_sem, i + 1)
                step(dve.reciprocal(rstd_ap, std_ap))
                step.wait()

            def norm_rows(i):
                if i >= 2:
                    dve.wait_ge(squares, 2 * TT + 4 * TT * (i - 1))
                    step(dve.tensor_reduce(ss, ss4.rearrange("p (t b) -> p t b", b=4), X_AXIS, ALU.add))
                    step.wait()
                root(i, ss, D, std, rstd, squares, mean_ready, std_ready,
                     TT * (i + 1) if i < 2 else 2 * TT + 4 * TT * (i - 1))

            dve.wait_ge(ple_taken, 1)
            dve.tensor_tensor(act_lo[:, 0:2, :].rearrange("p k n -> p (k n)"), PT,
                              act_hi[:, 0:2, :].rearrange("p k n -> p (k n)").bitcast(F32),
                              ALU.subtract).then_inc(ple_done, 1)
            split_lo(dve, 0, 0, 0, first=True)
            split_lo(dve, 1, 0, 1, first=True)
            def normed_rows(i):
                norm_rows(i)
                for cc in range(4):
                    for t in range(TT):
                        cols = slice(cc * 512, (cc + 1) * 512)
                        ins = dve.tensor_scalar(XN[:, t, cols], X[:, t, cols], rstd[:, t:t + 1], None, ALU.mult)
                    ins.then_inc(normed, 1)

            normed_rows(0)
            for cb in range(4):
                dve.wait_ge(unit_done, cb + 1)
                dve.tensor_copy(E[:, 1, cb * 512:(cb + 1) * 512], banks[2 * cb + 1][:, :]).then_inc(ple_taken, 1)
            ahead(split_lo, dve, "ple", 0, 2, 0)
            dve.wait_ge(const_ready, 32)
            keep_lo(0, pa("norm_gain"))
            ahead(split_lo, dve, "ple", 0, 2, 1)
            norm_rows(1)
            dve.wait_ge(ple_row_ready, 16)
            dve.wait_ge(ple_taken, 9)
            for t in range(TT):
                ins = dve.scalar_tensor_tensor(out=E[:, t, :], in0=E[:, t, :], scalar=rstd[:, t:t + 1], in1=ple_row,
                                               op0=ALU.mult, op1=ALU.mult)
                if t == 0:
                    ahead(split_lo, dve, "qkvg", 0, 8, 0)
            ins.then_inc(e_normed, 1)

            def take_qkvg(c_, i, per, k0, n):
                for k in range(0 if c_ else 1, 4):
                    ahead(split_lo, dve, "qkvg", i, per, k0 + k)
                dve.wait_ge(unit_done, 2 * pair_of("qkvg", i, per, k0 + 3) + 2)
                dve.tensor_copy(ZT[:, 1, bass.ds(c_ * 512, 512)], banks[2 * n + 1][:, :])\
                   .then_inc(qkvg_taken_v[n], 1)

            for b in range(3):
                take_qkvg(b, 0, 8, 4 * b, b % 2)
            dve.wait_ge(qkvg_taken_s[0], 3)
            dve.wait_ge(qkvg_taken_s[1], 2)
            dve.wait_ge(qkvg_taken_v[0], 3)
            dve.wait_ge(qkvg_taken_v[1], 2)
            lows = iter(range(12, 20))

            def more():
                ahead(split_lo, dve, "qkvg", 0, 8, next(lows))

            heads = QH + KVH
            step(dve.tensor_scalar(nsink, pa("sinks"), -1.0, None, ALU.mult))
            for t in range(TT):
                step(dve.tensor_copy(VP[:, 1 + t, :], ZT[:, t, 1280:1536]))
            dve.wait_ge(qk_squares, 2)
            for t in range(TT):
                step(dve.tensor_reduce(ss40[:, t * heads:(t + 1) * heads],
                                       XN[:, t, 0:1280].rearrange("p (h d) -> p h d", d=HD), X_AXIS, ALU.add))
            step.wait()
            dve.tensor_scalar(ss40, ss40, 1.0 / HD, EPS, ALU.mult, ALU.add).then_inc(qk_mean, 1)
            dve.wait_ge(qk_std, 1)
            step(dve.reciprocal(ss40, ss40))
            more()
            step.wait()
            zqk = [ZT[:, t, 0:1280].rearrange("p (h d) -> p h d", d=HD) for t in range(TT)]
            for t in range(TT):
                step(dve.tensor_tensor(zqk[t], zqk[t], ss40[:, t * heads:(t + 1) * heads].unsqueeze(2)
                                       .broadcast_to([P, heads, HD]), ALU.mult))
            more()
            step.wait()
            for t in range(TT):
                step(dve.tensor_tensor(zqk[t][:, 0:QH, :], zqk[t][:, 0:QH, :],
                                       pa("q_gain").unsqueeze(1).broadcast_to([P, QH, HD]), ALU.mult))
                step(dve.tensor_tensor(zqk[t][:, QH:heads, :], zqk[t][:, QH:heads, :],
                                       pa("k_gain").unsqueeze(1).broadcast_to([P, KVH, HD]), ALU.mult))
            more()
            step.wait()
            rot = [SC[:, n * 160:(n + 1) * 160].rearrange("p (h d) -> p h d", d=HALF) for n in range(4)]
            for t in range(TT):
                x1, x2 = zqk[t][:, :, 0:HALF], zqk[t][:, :, HALF:ROT]
                cos = c("cos")[:, t * HALF:(t + 1) * HALF].unsqueeze(1).broadcast_to([P, heads, HALF])
                sin = c("sin")[:, t * HALF:(t + 1) * HALF].unsqueeze(1).broadcast_to([P, heads, HALF])
                step(dve.tensor_tensor(rot[0], x1, cos, ALU.mult))
                step(dve.tensor_tensor(rot[1], x2, sin, ALU.mult))
                step(dve.tensor_tensor(rot[2], x2, cos, ALU.mult))
                step(dve.tensor_tensor(rot[3], x1, sin, ALU.mult))
                step.wait()
                step(dve.tensor_tensor(x1, rot[0], rot[1], ALU.subtract))
                step(dve.tensor_tensor(x2, rot[2], rot[3], ALU.add))
                step.wait()
            kd = KD.rearrange("p (t g r d) -> p t g r d", t=TT, g=KVH, r=2)
            for t in range(TT):
                for r in range(2):
                    ins = dve.tensor_copy(kd[:, t, :, r, :], zqk[t][:, QH:heads, :])
            ins.then_inc(qk_ready, 1)

            def keep_block(b, n):
                dve.wait_ge(unit_done, 2 * pair_of("qkvg", 0, 8, 4 * b + 3) + 2)
                dve.tensor_copy(ZT[:, 1, b * 512:(b + 1) * 512], banks[2 * n + 1][:, :]).then_inc(qkvg_taken_v[n], 1)

            more()
            keep_block(3, 1)
            for _ in range(4):
                more()
            keep_block(4, 0)
            dve.wait_ge(qk_turned, 24)
            for g in range(KVH):
                dve.tensor_copy(KTP[:, g, P:3 * P], banks[2 + g // 2][:, (g % 2) * S:(g % 2 + 1) * S])\
                   .then_inc(qk_kept, 1)

            dve.wait_ge(silu_tanh, 1)
            for t in range(TT):
                step(dve.scalar_tensor_tensor(out=ZT[:, t, 1536:2560], in0=YM[:, t, :], scalar=1.0,
                                              in1=ZT[:, t, 1536:2560], op0=ALU.add, op1=ALU.mult))
            step.wait()

            def att_scores(u, g):
                dve.wait_ge(scored, u + 2)
                for b in range(2):
                    step(dve.scalar_tensor_tensor(
                        out=SC[:, b * 512:(b + 1) * 512].rearrange("p (h n) -> p h n", h=2),
                        in0=banks[4 + b][:, :].rearrange("p (h n) -> p h n", h=2), scalar=HD ** -0.5,
                        in1=band_t.unsqueeze(1).broadcast_to([P, 2, S]), op0=ALU.mult, op1=ALU.add))
                step.wait()
                step(dve.tensor_reduce(mx, SC.rearrange("p (h n) -> p h n", h=GROUP), X_AXIS, ALU.max))
                step.wait()
                step(dve.scalar_tensor_tensor(out=nm, in0=mx, scalar=-1.0, in1=nsink[:, bass.ds(g * GROUP, GROUP)],
                                              op0=ALU.mult, op1=ALU.min))
                step.wait()
                dve.tensor_tensor(dsink, nm, nsink[:, bass.ds(g * GROUP, GROUP)], ALU.subtract).then_inc(sc_max, 1)

            for t in range(TT):
                band_t = c("band")[:, t * S:(t + 1) * S]
                with dve.Fori(0, KVH) as g:
                    j = g + t * KVH
                    with step.turns(g, 11, KVH):
                        cw = pa("conv_w")
                        ahead(split_lo, dve, "conv", j, 4, 0)
                        att_scores(j, g)
                        dve.wait_ge(conv_gate, j + 1)
                        dve.scalar_tensor_tensor(out=CG, in0=CG, scalar=1.0, in1=banks[0][:, 0:S], op0=ALU.add,
                                                 op1=ALU.mult).then_inc(conv_gate_used, 1)
                        dve.wait_ge(exps, j * 5 + 5)
                        step(dve.tensor_tensor(rec, esum, esink, ALU.add))
                        step.wait()
                        step(dve.reciprocal(rec, rec))
                        ahead(split_lo, dve, "conv", j, 4, 1)
                        ahead(split_lo, dve, "conv", j, 4, 2)
                        dve.wait_ge(conv_c, j + 1)
                        dve.wait_ge(unit_done, 2 * pair_of("conv", j, 4, 2) + 2)
                        dve.tensor_tensor(CU[:, 2:2 + S], CC, banks[2][:, 0:S], ALU.mult).then_inc(conv_h_used, 1)
                        dve.wait_ge(conv_h_used, j + 2)
                        step(dve.tensor_scalar(CY, CU[:, 0:S], cw[:, bass.ds(j * 3, 1)], None, ALU.mult))
                        step.wait()
                        for tap in range(1, 3):
                            step(dve.scalar_tensor_tensor(out=CY, in0=CU[:, tap:tap + S],
                                                          scalar=cw[:, bass.ds(j * 3 + tap, 1)], in1=CY,
                                                          op0=ALU.mult, op1=ALU.add))
                            step.wait()
                        ahead(split_lo, dve, "conv", j, 4, 3)
                        dve.wait_ge(unit_done, 2 * pair_of("conv", j, 4, 3) + 2)
                        step(dve.tensor_tensor(CY, CY, banks[3][:, 0:S], ALU.mult))
                        step.wait()
                        dve.wait_ge(conv_gate_used, j + 2)
                        dve.scalar_tensor_tensor(out=MIXT[:, bass.ds(j + 8, 1), :].rearrange("p o n -> p (o n)"),
                                                 in0=CY, scalar=0.5, in1=CG, op0=ALU.mult, op1=ALU.mult)\
                           .then_inc(conv_b_used, 1)
                        dve.wait_ge(mixed, j + 1)
                        step(dve.tensor_tensor(ET[:, 0:S].rearrange("p (b a d) -> p b a d", b=2, a=2),
                                               banks[4][:, 0:S].rearrange("p (b a d) -> p b a d", b=2, a=2),
                                               rec.rearrange("p (a b) -> p b a", a=2).unsqueeze(3)
                                               .broadcast_to([P, 2, 2, HD]), ALU.mult))
                        step.wait()
                        dve.scalar_tensor_tensor(out=YM[:, t, bass.ds(g * S, S)], in0=ET[:, 0:S], scalar=0.5,
                                                 in1=ZT[:, t, bass.ds(g * S + 1536, S)], op0=ALU.mult,
                                                 op1=ALU.mult).then_inc(mix_used, 1)

            for k in range(8):
                dve.wait_ge(act_hi_ready, KT + k + 1)
                dve.tensor_tensor(act_lo[:, k, :], banks[k][:, 0:S], act_hi[:, k, :].bitcast(F32), ALU.subtract)\
                   .then_inc(act_lo_ready, 1)
            dve.wait_ge(act_hi_ready, 2 * KT)
            dve.tensor_tensor(act_lo[:, 8:16, :], MIXT[:, 8:16, :], act_hi[:, 8:16, :].bitcast(F32), ALU.subtract)\
               .then_inc(act_lo_ready, 8)

            def softplus():
                lam = pa("lam")
                step(dve.tensor_scalar(sp_c, lam, -1.0, None, ALU.mult))
                step.wait()
                dve.tensor_tensor(sp_a, lam, sp_c, ALU.max).then_inc(softplus_ready, 1)
                step(dve.tensor_scalar(nba, pa("ba"), -1.0, None, ALU.mult))
                step(dve.tensor_scalar(hbx, pa("bx"), 0.5, None, ALU.mult))
                dve.wait_ge(softplus_ready, 2)
                step(dve.tensor_scalar(sp_c, sp_b, 2.0, None, ALU.add))
                step.wait()
                step(dve.reciprocal(sp_c, sp_c))
                step.wait()
                step(dve.tensor_tensor(sp_b, sp_b, sp_c, ALU.mult))
                step.wait()
                step(dve.tensor_tensor(sp_c, sp_b, sp_b, ALU.mult))
                step.wait()
                step(dve.tensor_scalar(sp_a, sp_c, 1.0 / 19, 1.0 / 17, ALU.mult, ALU.add))
                step.wait()
                for odd in range(15, 0, -2):
                    step(dve.tensor_tensor(sp_a, sp_a, sp_c, ALU.mult))
                    step.wait()
                    step(dve.tensor_scalar(sp_a, sp_a, 1.0 / odd, None, ALU.add))
                    step.wait()
                step(dve.scalar_tensor_tensor(out=sp_a, in0=sp_a, scalar=2.0, in1=sp_b, op0=ALU.mult, op1=ALU.mult))
                step(dve.tensor_scalar(sp_c, lam, -1.0, 0.0, ALU.mult, ALU.max))
                step.wait()
                step(dve.tensor_tensor(sp_a, sp_a, sp_c, ALU.add))
                step.wait()
                step(dve.tensor_scalar(sp_b, sp_a, -8.0, None, ALU.mult))
                dve.tensor_scalar(sp_a, sp_a, 8.0, None, ALU.mult).then_inc(softplus_ready, 1)

            def add_blocks(part):
                for b in range(4):
                    n = b % 2
                    for k in range(3):
                        ahead(split_lo, dve, part, 0, 8, 4 * b + k)
                        if part == "w_out" and (b, k) == (1, 1):
                            softplus()
                    dve.wait_ge(unit_done, 2 * pair_of(part, 0, 8, 4 * b + 3) + 2)
                    for t in range(TT):
                        xs = X[:, t, b * 512:(b + 1) * 512]
                        dve.tensor_tensor(xs, xs, banks[2 * n + t][:, :], ALU.add).then_inc(added[n], 1)
                    if b < 3:
                        ahead(split_lo, dve, part, 0, 8, 4 * b + 3)

            add_blocks("w_out")
            for n in range(2):
                dve.wait_ge(added[n], 5)
            normed_rows(2)
            keep_lo(2, pa("gate_gain"))
            ahead(split_lo, dve, "w_out", 0, 8, 15)
            dve.wait_ge(gate_row_ready, 16)
            for b in range(4):
                n = b % 2
                for k in range(3):
                    ahead(split_lo, dve, "gate", 0, 8, 4 * b + k)
                dve.wait_ge(unit_done, 2 * pair_of("gate", 0, 8, 4 * b + 3) + 2)
                cols = slice(b * 512, (b + 1) * 512)
                for t in range(TT):
                    dve.tensor_tensor(SC_G[t], banks[2 * n + t][:, :], gate_row[:, cols], ALU.add)\
                       .then_inc(gate_pre, 1)
                if b < 3:
                    ahead(split_lo, dve, "gate", 0, 8, 4 * b + 3)
                for t in range(TT):
                    dve.wait_ge(gate_tanh, 2 * b + t + 1)
                    step(dve.scalar_tensor_tensor(out=SC_G[t], in0=SC_G[t], scalar=1.0, in1=E[:, t, cols],
                                                  op0=ALU.add, op1=ALU.mult))
                for t in range(TT):
                    step.wait()
                    xs = X[:, t, cols]
                    dve.scalar_tensor_tensor(out=xs, in0=SC_G[t], scalar=0.5, in1=xs, op0=ALU.mult, op1=ALU.add)\
                       .then_inc(gated[n], 1)
            for n in range(2):
                dve.wait_ge(gated[n], 5)
            normed_rows(3)
            keep_lo(3, pa("mix_gain"))
            ahead(split_lo, dve, "gate", 0, 8, 15)

            for k in range(4):
                ahead(split_lo, dve, "ckv", 0, 4, k)
            for k in range(2):
                ahead(split_lo, dve, "kiwi", 0, 2, k)
            dve.wait_ge(kw_kept, 2)
            ki = KW[:, :, 0:ID]
            kc = KID[:, :, 0:ID]
            step(dve.tensor_reduce(mx[:, 0:2], ki, X_AXIS, ALU.add))
            step.wait()
            step(dve.tensor_scalar(mx[:, 0:2], mx[:, 0:2], 1.0 / ID, None, ALU.mult))
            step.wait()
            step(dve.tensor_tensor(kc, ki, mx[:, 0:2].unsqueeze(2).broadcast_to([P, TT, ID]), ALU.subtract))
            step.wait()
            step(dve.tensor_tensor(KID[:, :, ID:P], kc, kc, ALU.mult))
            step.wait()
            step(dve.tensor_reduce(stat[:, 10:12], KID[:, :, ID:P], X_AXIS, ALU.add))
            step.wait()
            step(dve.tensor_scalar(stat[:, 10:12], stat[:, 10:12], 1.0 / ID, EPS, ALU.mult, ALU.add))
            dve.wait_ge(ckv_squares, 2)
            dve.tensor_scalar(stat[:, 8:10], ss, 1.0 / RANK, EPS, ALU.mult, ALU.add).then_inc(ckv_mean, 1)
            dve.wait_ge(ckv_std, 1)
            step(dve.reciprocal(stat[:, 8:12], stat[:, 8:12]))
            step.wait()
            for t in range(TT):
                dve.tensor_scalar(CKV[:, t, :], CKV[:, t, :], stat[:, 8 + t:9 + t], None, ALU.mult)\
                   .then_inc(ckv_normed, 1)
            ahead(split_lo, dve, "qi", 0, 2, 0)
            step(dve.tensor_tensor(kc, kc, stat[:, 10:12].unsqueeze(2).broadcast_to([P, TT, ID]), ALU.mult))
            step.wait()
            step(dve.tensor_tensor(kc, kc, pa("idx_g").unsqueeze(1).broadcast_to([P, TT, ID]), ALU.mult))
            step.wait()
            step(dve.tensor_tensor(kc, kc, pa("idx_b").unsqueeze(1).broadcast_to([P, TT, ID]), ALU.add))
            step.wait()
            dve.tensor_copy(KID[:, :, ID:P], kc).then_inc(ki_ready, 1)
            step(dve.tensor_scalar(KW[:, :, ID:ID + IH], KW[:, :, ID:ID + IH], IH ** -0.5, None, ALU.mult))
            step(dve.memset(ISC, 0.0))
            step.wait()
            def index_sum(i, n):
                dve.wait_ge(rel_ready, i * 4 + 2 * n + 3)
                for hh in range(2):
                    for t in range(TT):
                        dve.scalar_tensor_tensor(
                            out=ISC[:, t, :], in0=REL[:, 2 * hh + t, :],
                            scalar=KW[:, t, bass.ds(i * 4 + (2 * n + hh + ID), 1)],
                            in1=ISC[:, t, :], op0=ALU.mult, op1=ALU.add).then_inc(rel_used, 1)
                    dve.wait_ge(rel_used, i * 8 + 4 * n + 2 * hh + 3)

            ahead(split_lo, dve, "qi", 0, 2, 1)
            with dve.Fori(0, IH // 4 - 1) as i:
                for n in range(2):
                    index_sum(i, n)
                    ahead(split_lo, dve, "qi", i, 2, n + 2)
            for n in range(2):
                index_sum(IH // 4 - 1, n)

            for t in range(TT):
                step(dve.tensor_tensor(IWORK[:, t, :], ISC[:, t, :], c("causal")[:, t * S:(t + 1) * S], ALU.add))

            def next_eight():
                for t in range(TT):
                    step.wait()
                    step(dve.max(top8[t], IWORK[:, t, :]))
                for t in range(TT):
                    step.wait()
                    step(dve.match_replace(IWORK[:, t, :], top8[t], IWORK[:, t, :], TAKEN))

            step(dve.memset(XP[:, 0:3], 0.0))
            step.wait()

            cw2, cb2 = pa("conv_w2"), pa("conv_b2")

            def rnn_gates(j):
                dve.wait_ge(rg_exp, j * 2 + 3)
                step(dve.tensor_scalar(RI[:, 0:S], RI[:, 0:S], 1.0, None, ALU.add))
                step.wait()
                dve.reciprocal(RI[:, 0:S], RI[:, 0:S]).then_inc(r_ready, 1)
                step(dve.scalar_tensor_tensor(out=RX[:, bass.ds(j, 1), :].rearrange("p o n -> p (o n)"),
                                              in0=RI[:, S:2 * S], scalar=1.0, in1=XC, op0=ALU.add, op1=ALU.mult))

            def rnn_input(j):
                dve.wait_ge(a_ready, j * 2 + 2)
                decay = RA[:, bass.ds(j, 1), :].rearrange("p o n -> p (o n)")
                step(dve.tensor_tensor(THD, decay, decay, ALU.mult))
                step.wait()
                dve.scalar_tensor_tensor(out=RW[:, bass.ds(j, 1), :].rearrange("p o n -> p (o n)"), in0=THD,
                                         scalar=1.0, in1=TH, op0=ALU.add, op1=ALU.mult).then_inc(th_used, 1)

            def rnn_block(j, first=False):
                ahead(split_lo, dve, "rnn", j, 2, 0, units=(0,))
                if not first:
                    rnn_gates(j - 1)
                    step.wait()
                ahead(split_lo, dve, "rnn", j, 2, 0, units=(1,))
                dve.wait_ge(xr_kept, j + 2)
                step(dve.tensor_scalar(XC, XP[:, 0:S], cw2[:, bass.ds(j * 4, 1)], cb2[:, bass.ds(j, 1)],
                                       ALU.mult, ALU.add))
                step.wait()
                for tap in range(1, 4):
                    ins = dve.scalar_tensor_tensor(out=XC, in0=XP[:, tap:tap + S],
                                                   scalar=cw2[:, bass.ds(j * 4 + tap, 1)], in1=XC,
                                                   op0=ALU.mult, op1=ALU.add)
                    if tap < 3:
                        step(ins)
                        step.wait()
                    else:
                        ins.then_inc(xc_ready, 1)
                ahead(split_lo, dve, "rnn", j, 2, 1)
                if not first:
                    rnn_input(j - 1)

            rnn_block(0, first=True)
            rounds = TOPK // 8
            for j in range(1, rounds + 1):
                rnn_block(j)
                next_eight()
            step.wait()
            step(dve.tensor_scalar(IWORK, IWORK, TAKEN / 2, 1.0, ALU.is_le, ALU.subtract))
            step.wait()
            step(dve.scalar_tensor_tensor(out=AMASK, in0=IWORK.rearrange("p t n -> p (t n)"), scalar=-NEG,
                                          in1=c("causal"), op0=ALU.mult, op1=ALU.add))

            with dve.Fori(rounds + 1, KT) as j:
                with step.turns(j - (rounds + 1), 6, KT - rounds - 1):
                    rnn_block(j)
            rnn_gates(KT - 1)
            rnn_input(KT - 1)
            dve.wait_ge(th_used, KT + 1)
            dve.memset(RA[:, :, 0:1], 0.0).then_inc(rw_ready, 1)
            def finish_head(h):
                dve.wait_ge(ga_tanh, h + 2)
                dve.wait_ge(y_made, h + 2)
                dve.wait_ge(gr_used, h + 2)
                step(dve.scalar_tensor_tensor(out=YH, in0=TA, scalar=1.0, in1=banks[6][:, 0:S], op0=ALU.add,
                                              op1=ALU.mult))
                step.wait()
                step(dve.tensor_tensor(YH, YH, HU, ALU.add))
                step.wait()
                dve.tensor_scalar(MIX2[:, bass.ds(h, 1), :].rearrange("p o n -> p (o n)"), YH, 0.5, None, ALU.mult)\
                   .then_inc(head_mixed, 1)

            def one_head(h, first=False):
                row = lambda r: r[:, bass.ds(h, 1), :].rearrange("p o n -> p (o n)")
                ahead(split_lo, dve, "heads", h, 2, 0)
                dve.wait_ge(logits_made, h + 2)
                step(dve.scalar_tensor_tensor(out=LG.rearrange("p t n -> p (t n)"), in0=banks[4][:, :],
                                              scalar=float(P) ** -0.5, in1=AMASK, op0=ALU.mult, op1=ALU.add))
                step.wait()
                step(dve.tensor_reduce(mx[:, 0:2], LG, X_AXIS, ALU.max))
                step.wait()
                dve.tensor_scalar(nm[:, 0:2], mx[:, 0:2], -1.0, None, ALU.mult).then_inc(max_ready, 1)
                if first:
                    dve.wait_ge(rw_root, 1)
                else:
                    finish_head(h - 1)
                dve.wait_ge(v_made, h + 1)
                dve.tensor_copy(VS.rearrange("p k n -> p (k n)"), banks[3][:, 0:S]).then_inc(v_kept, 1)
                step(dve.tensor_tensor(HU, row(RW), row(RX), ALU.mult))
                dve.wait_ge(p_exp, h * 2 + 3)
                step(dve.reciprocal(rec[:, 0:2], esum[:, 0:2]))
                step.wait()
                for t in range(TT):
                    dve.tensor_scalar(LG[:, t, :], LG[:, t, :], rec[:, t:t + 1], None, ALU.mult)\
                       .then_inc(p_ready, 1)
                step(dve.tensor_tensor_scan(HU, row(RA), HU, 0.0, ALU.mult, ALU.add))
                dve.wait_ge(gr_tanh, h + 1)
                step.wait()
                dve.scalar_tensor_tensor(out=HU, in0=TG, scalar=1.0, in1=HU, op0=ALU.add, op1=ALU.mult)\
                   .then_inc(gr_used, 1)
                ahead(split_lo, dve, "heads", h, 2, 1)

            one_head(0, first=True)
            with dve.Fori(1, H2) as h:
                with step.turns(h - 1, 7, H2 - 1):
                    one_head(h)

            for k in range(4):
                if k == 2:
                    finish_head(H2 - 1)
                dve.wait_ge(act_hi_ready, 4 * KT + 4 * k + 4)
                dve.tensor_tensor(act_lo[:, 4 * k:4 * k + 4, :], MIX2[:, 4 * k:4 * k + 4, :],
                                  act_hi[:, 4 * k:4 * k + 4, :].bitcast(F32), ALU.subtract).then_inc(act_lo_ready, 4)
            add_blocks("w_o")
            for n in range(2):
                dve.wait_ge(added[n], 9)
            normed_rows(4)
            keep_lo(5, pa("ffn_gain"))
            ahead(split_lo, dve, "w_o", 0, 8, 15)

            def top16(vals, idx, work):
                step(dve.max(vals[:, 0:8], work))
                step.wait()
                step(dve.max_index(idx[:, 0:8], vals[:, 0:8], work))
                step.wait()
                step(dve.match_replace(work, vals[:, 0:8], work, TAKEN))
                step.wait()
                step(dve.max(vals[:, 8:16], work))
                step.wait()
                return dve.max_index(idx[:, 8:16], vals[:, 8:16], work)

            for h in range(PH):
                ahead(split_lo, dve, "wqu", h, 4, 0)
                for a in range(2):
                    ahead(split_lo, dve, "wqu", h, 4, 1 + a)
                    dve.wait_ge(ps_kept[a], h + 2)
                    for t in range(TT):
                        ins = top16(V12[:, h, a, t, :], I12[:, h, a, t, :], PS[:, a, t, :])
                        if t == TT - 1:
                            ins.then_inc(ps_used[a], 1)
                        else:
                            step(ins)
                ahead(split_lo, dve, "wqu", h, 4, 3)
                for a in range(2):
                    dve.wait_ge(ps_used[a], h + 2)
                for t in range(TT):
                    step(dve.tensor_tensor(CAND[:, t, :].rearrange("p (a b) -> p a b", a=PK),
                                           V12[:, h, 0, t, :].unsqueeze(2).broadcast_to([P, PK, PK]),
                                           V12[:, h, 1, t, :].unsqueeze(1).broadcast_to([P, PK, PK]), ALU.add))
                    step.wait()
                    step(top16(CV[:, h, t, :], CP[:, h, t, :], CAND[:, t, :]))
            step.wait()
            lows = iter(range(2 * PH))

            def more(count=1):
                for _ in range(count):
                    ahead(split_lo, dve, "u_decode", 0, 2, next(lows))

            cv = CV.rearrange("p h t k -> p (h t) k")
            step(dve.tensor_copy(crec, cv[:, :, 0:1].rearrange("p a o -> p (a o)")))
            step.wait()
            dve.tensor_tensor(cv, cv, crec.unsqueeze(2).broadcast_to([P, PH * TT, PK]), ALU.subtract)\
               .then_inc(pick_diff, 1)
            more()
            cp = CP.rearrange("p h t k -> p (h t k)")
            step(dve.tensor_scalar(CAU[:, 0, :], cp, 4, None, ALU.logical_shift_right))
            step(dve.tensor_scalar(CAU[:, 1, :], cp, 15, None, ALU.bitwise_and))
            step(dve.tensor_copy(I12F.rearrange("p h a t k -> p (h a t k)"),
                                 I12.rearrange("p h a t k -> p (h a t k)")))
            step.wait()
            step(dve.tensor_copy(CA.rearrange("p a n -> p (a n)"), CAU.rearrange("p a n -> p (a n)")))
            more()
            step.wait()
            for a in range(2):
                step(dve.tensor_tensor(EQ.rearrange("p (n j) -> p n j", j=PK),
                                       CA[:, a, :].unsqueeze(2).broadcast_to([P, SLOT_N * TT, PK]),
                                       iota[:, 0:PK].unsqueeze(1).broadcast_to([P, SLOT_N * TT, PK]), ALU.is_equal))
                more(2)
                step.wait()
                for h in range(PH):
                    eq = EQ[:, h * TT * PK * PK:(h + 1) * TT * PK * PK].rearrange("p (t k j) -> p t k j", t=TT, k=PK)
                    step(dve.tensor_tensor(eq, eq, I12F[:, h, a, :, :].unsqueeze(2).broadcast_to([P, TT, PK, PK]),
                                           ALU.mult))
                    if h % 4 == 3:
                        more()
                step.wait()
                step(dve.tensor_reduce(PICK[:, a, :, :, :].rearrange("p h t k -> p (h t k)"),
                                       EQ.rearrange("p (n j) -> p n j", j=PK), X_AXIS, ALU.add))
                more(2)
                step.wait()
            dve.wait_ge(pick_exp, 1)
            step(dve.tensor_reduce(csum, cv, X_AXIS, ALU.add))
            more()
            step.wait()
            step(dve.reciprocal(crec, csum))
            step.wait()
            step(dve.tensor_tensor(PICK[:, 2, :, :, :].rearrange("p h t k -> p (h t) k"), cv,
                                   crec.unsqueeze(2).broadcast_to([P, PH * TT, PK]), ALU.mult))
            step.wait()
            for a in range(3):
                ins = dve.tensor_copy(PICKT[:, a, :, :, :].rearrange("p t h k -> p h t k"), PICK[:, a, :, :, :])
                ins.then_inc(picks_ready, 1)
            for k in lows:
                ahead(split_lo, dve, "u_decode", 0, 2, k)

            dve.wait_ge(slots_kept, 3)
            with dve.Fori(0, S // 16) as i:
                for n in range(2):
                    for s in range(8):
                        tok = i * 16 + (8 * n + s)
                        dve.wait_ge(hot_used[s % 4], i * 4 + (2 * n + s // 4) + 1)
                        dve.tensor_scalar(hot[:, 0, s % 4, :], iota, slot_t[:, 0, bass.ds(tok, 1)],
                                          slot_t[:, 2, bass.ds(tok, 1)], ALU.is_equal, ALU.mult).then_inc(hot1, 1)
                        if s % 4 == 3:
                            ahead(split_lo, dve, "u_gates", i, 2, n, units=(s // 4,))
            for n in range(2):
                dve.wait_ge(gate_kept[n], S // 8 + 1)

            with dve.Fori(0, EARLY // 2) as i:
                for n in range(2):
                    ahead(split_lo, dve, "u_late", i, 2, n)
                    dve.wait_ge(gelu_ready[n], i + (EARLY // 2 + 1) + 1)
                    late = G[:, bass.ds(i * 2 + (EARLY + n), 1), :].rearrange("p o n -> p (o n)")
                    dve.tensor_tensor(late, GZ[:, n, :], late, ALU.mult).then_inc(act_ready[n], 1)
                    dve.wait_ge(z_back[n], i * 16 + 16)
                    back = G[:, bass.ds(i * 2 + n, 1), :].rearrange("p o n -> p (o n)")
                    dve.tensor_tensor(back, GB[:, n, :], back, ALU.mult).then_inc(early_ready[n], 1)

            def expert_lo(b, n, need):
                dve.wait_ge(eh_ready, need)
                dve.tensor_tensor(act_lo[:, n, :], G[:, bass.ds(b, 1), :].rearrange("p o n -> p (o n)"),
                                  act_hi[:, n, :].bitcast(F32), ALU.subtract).then_inc(el_ready, 1)

            for n in range(2):
                dve.wait_ge(act_ready[n], EARLY // 2 + 1)
                dve.wait_ge(early_ready[n], EARLY // 2 + 1)
            for n in range(2):
                expert_lo(n, n, n + 1)
            with dve.Fori(0, NB // 2 - 1) as i:
                for n in range(2):
                    ahead(split_lo, dve, "v", i, 2, n)
                    expert_lo(i * 2 + (2 + n), n, i * 2 + (3 + n))

            for cb in range(4):
                dve.wait_ge(unit_done, UNITS - 1 + cb // 2)
                for t in range(TT):
                    if not cb:
                        dve.wait_ge(xf_ready[t], 16)
                    xs = XF[:, t, cb * 512:(cb + 1) * 512]
                    dve.tensor_tensor(xs, xs, banks[4 * t + cb][:, :], ALU.add).then_inc(y_added, 1)
            dve.wait_ge(fin_squares, 4 * TT)
            step(dve.tensor_reduce(ss, ss4.rearrange("p (t b) -> p t b", b=4), X_AXIS, ALU.add))
            step.wait()
            root(0, ss, D, std, rstd, fin_squares, fin_mean, fin_std, 4 * TT)
            dve.wait_ge(final_ready, 16)
            for t in range(TT):
                for half in range(2):
                    cols = slice(half * 1024, (half + 1) * 1024)
                    dve.scalar_tensor_tensor(out=OUT[:, t, cols], in0=XF[:, t, cols], scalar=rstd[:, t:t + 1],
                                             in1=final_row[:, cols], op0=ALU.mult, op1=ALU.mult)\
                       .then_inc(fin_ready, 1)

        @block.tensor
        def _(pe):
            def turn_rows(n, fill):
                for k in range(KT):
                    if k % 4 == 0:
                        pe.wait_ge(normed, 4 * n + k // 4 + 1)
                    if k >= 8:
                        pe.wait_ge(act_lo_ready, fill * KT + k - 7)
                    for t in range(TT):
                        ins = pe.transpose(banks[k % 8][:, t * P:(t + 1) * P], XN[:, t, k * P:(k + 1) * P], ident)
                    ins.then_inc(turned, 1)
                pe.wait_ge(act_lo_ready, fill * KT + 10)

            pe.wait_ge(ple_done, 1)
            for cb in range(4):
                pe.wait_ge(lo_ready, cb + 1)
                for kk in range(2):
                    hi = w_hi[:, cb, kk * 512:(kk + 1) * 512]
                    lo = w_lo[:, cb, kk * 512:(kk + 1) * 512]
                    for t in range(TT):
                        o = banks[2 * cb + t][:, :]
                        a_hi = act_hi[:, kk, t * P:(t + 1) * P]
                        a_lo = act_lo[:, kk, t * P:(t + 1) * P]
                        pe.matmul(o, a_hi, hi, start=(kk == 0), stop=False)
                        pe.matmul(o, a_hi, lo, start=False, stop=False)
                        mm = pe.matmul(o, a_lo, hi, start=False, stop=(kk == 1))
                mm.then_inc(unit_done, 1)
            pe.wait_ge(const_ready, 32)
            pe.wait_ge(ple_taken, 9)
            turn_rows(0, 0)
            with pe.Fori(0, 2) as i:
                for n in range(2):
                    pe.wait_ge(qkvg_taken_s[n], i + 1)
                    pe.wait_ge(qkvg_taken_v[n], i + 1)
                    tokens_out(pe, "qkvg", i, 8, 4 * n, [banks[2 * n][:, :], banks[2 * n + 1][:, :]], 1)
            pe.wait_ge(qkvg_taken_s[0], 3)
            pe.wait_ge(qkvg_taken_v[0], 3)
            tokens_out(pe, "qkvg", 0, 8, 16, [banks[0][:, :], banks[1][:, :]], 1)
            pe.wait_ge(qk_ready, 1)
            for k in range(8):
                for t in range(TT):
                    pe.transpose(banks[4 + k // 2][:, (k % 2) * S + t * P:(k % 2) * S + (t + 1) * P],
                                 ZT[:, t, k * P:(k + 1) * P], ident).then_inc(qk_turned, 1)
            pe.wait_ge(qkvg_taken_s[1], 3)
            pe.wait_ge(qkvg_taken_v[1], 3)
            for g in range(KVH):
                for t in range(TT):
                    off = (t * KVH + g) * P
                    pe.transpose(banks[2 + g // 2][:, (g % 2) * S + t * P:(g % 2) * S + (t + 1) * P],
                                 KD[:, off:off + P], ident).then_inc(qk_turned, 1)

            def conv_pair(j, n):
                pe.wait_ge([conv_gate_used, conv_h_used, conv_h_used, conv_b_used][n], j + 1)
                columns_out(pe, pair_of("conv", j, 4, n), n % 2, banks[n][:, 0:S])

            pe.wait_ge(qkvg_taken_s[0], 4)
            pe.wait_ge(qkvg_taken_v[0], 4)
            order = [0, 2, 1, 3]
            with pe.Fori(0, TT) as t:
                with pe.Fori(0, KVH) as g:
                    j = t * KVH + g
                    conv_pair(j, 0)
                    pe.wait_ge(staged, j * 2 + 2)
                    pe.wait_ge(mix_used, j + 1)
                    pe.wait_ge(qk_kept, 12)
                    for h in range(GROUP):
                        lo = (h % 2) * HD
                        ins = pe.matmul(banks[4 + h % 2][:, (h // 2) * S:(h // 2 + 1) * S],
                                        QST[lo:lo + HD, h // 2, :], KST[lo:lo + HD, :], start=True, stop=True)
                    ins.then_inc(scored, 1)
                    conv_pair(j, 1)
                    conv_pair(j, 2)
                    pe.wait_ge(exps, j * 5 + 4)
                    pe.wait_ge(probs_kept, j * 2 + 1)
                    for kb in range(2):
                        for h in range(GROUP):
                            ins = pe.transpose(banks[6 + kb][:, h * P:(h + 1) * P],
                                               SC[:, h * S + kb * P:h * S + (kb + 1) * P], ident)
                    ins.then_inc(probs_turned, 1)
                    conv_pair(j, 3)
                    pe.wait_ge(probs_kept, j * 2 + 3)
                    for h in range(GROUP):
                        for kb in range(2):
                            ins = pe.matmul(banks[4][:, order[h] * HD:(order[h] + 1) * HD],
                                            ET[:, kb * 512 + h * P:kb * 512 + (h + 1) * P],
                                            VP[:, bass.ds(t + kb, 1), bass.ds(g * HD, HD)]
                                            .rearrange("p o n -> p (o n)"), start=(kb == 0), stop=(kb == 1))
                    ins.then_inc(mixed, 1)

            pe.wait_ge(mix_used, CONV_J + 1)
            pe.wait_ge(conv_b_used, CONV_J + 1)
            for k in range(8):
                for t in range(TT):
                    ins = pe.transpose(banks[k][:, t * P:(t + 1) * P], YM[:, t, k * P:(k + 1) * P], ident)
                ins.then_inc(ym_turned, 1)
            pe.wait_ge(act_lo_ready, KT + 8)

            def blocks_out(part, taken, base, fills):
                with pe.Fori(0, 2) as i:
                    for n in range(2):
                        pe.wait_ge(taken[n], i * 2 + base + 1)
                        tokens_out(pe, part, i, 8, 4 * n, [banks[2 * n][:, :], banks[2 * n + 1][:, :]], fills)

            blocks_out("w_out", added, 0, 2)
            turn_rows(1, 2)
            blocks_out("gate", gated, 0, 3)
            turn_rows(2, 3)

            tokens_out(pe, "ckv", 0, 4, 0, [banks[0][:, :], banks[1][:, :]], 4)
            columns_out(pe, pair_of("kiwi", 0, 2, 0), 0, banks[2][:, 0:S])
            for u in range(2):
                pe.wait_ge(lo_ready, 2 * pair_of("kiwi", 0, 2, 1) + u + 1)
                pe.matmul(banks[7][:, 0:2], w_hi[:, 2 + u, 0:P], act_hi[:, 0, 0:2], start=True, stop=True)\
                  .then_inc(unit_done, 1)
            pe.wait_ge(kwt_kept, 1)
            for t in range(TT):
                ins = pe.transpose(banks[3][:, t * P:(t + 1) * P], KWT[:, t * P:(t + 1) * P], ident)
            ins.then_inc(kw_turned, 1)
            def index_queries(i, n):
                columns_out(pe, pair_of("qi", i, 2, n), n % 2, banks[n % 2][:, 0:S])

            def index_scores(i, n):
                pe.wait_ge(qi_kept, i * 2 + n + 1)
                pe.wait_ge(rel_ready, i * 4 + 2 * n + 1)
                for hh in range(2):
                    for t in range(TT):
                        ins = pe.matmul(banks[4 + hh][:, t * S:(t + 1) * S],
                                        QIS[hh * ID:(hh + 1) * ID, n, t * P:(t + 1) * P],
                                        KIT[hh * ID:(hh + 1) * ID, :], start=True, stop=True)
                ins.then_inc(qi_scored, 1)

            pe.wait_ge(ckv_kept, 2)
            for n in range(2):
                index_queries(0, n)
            pe.wait_ge(ckv_normed, 2)
            for k in range(RT):
                for t in range(TT):
                    ins = pe.transpose(banks[4 + k // 2][:, (k % 2) * S + t * P:(k % 2) * S + (t + 1) * P],
                                       CKV[:, t, k * P:(k + 1) * P], ident)
                ins.then_inc(ckv_turned, 1)
            pe.wait_ge(ki_ready, 1)
            for t in range(TT):
                ins = pe.transpose(banks[6][:, t * P:(t + 1) * P], KID[:, t, :], ident)
            ins.then_inc(ckv_turned, 1)
            pe.wait_ge(ckvt_kept, RT + 1)

            with pe.Fori(0, IH // 4 - 1) as i:
                for n in range(2):
                    index_scores(i, n)
                    index_queries(i, n + 2)
            for n in range(2):
                index_scores(IH // 4 - 1, n)

            def rnn_gates(j):
                pe.wait_ge(xc_ready, j + 2)
                pe.wait_ge(w_staged, j + 1)
                pe.wait_ge(rg_exp, j * 2 + 1)
                for a in range(2):
                    ins = pe.matmul(banks[4][:, a * S:(a + 1) * S], WST[:, a * P:(a + 1) * P], XC, start=True,
                                    stop=True)
                ins.then_inc(rg_done, 1)

            def rnn_block(j, first=False):
                pe.wait_ge(xr_kept, j + 1)
                columns_out(pe, pair_of("rnn", j, 2, 0), 0, banks[0][:, 0:S])
                if not first:
                    rnn_gates(j - 1)
                pe.wait_ge(q2_kept, j + 1)
                columns_out(pe, pair_of("rnn", j, 2, 1), 1, banks[1][:, 0:S])

            def keys_values(h):
                pe.wait_ge(ukv_ready, h * 16 + 16)
                pe.wait_ge(k_kept, h + 1)
                for k in range(RT):
                    ins = pe.matmul(banks[2][:, 0:S], UKV[:, k, :], CKVT[:, k, :], start=(k == 0), stop=(k == RT - 1))
                ins.then_inc(k_made, 1)
                pe.wait_ge(v_kept, h + 1)
                for st in range(2):
                    for k in range(RT):
                        ins = pe.matmul(banks[3][:, st * P:(st + 1) * P], CKVT[:, k, st * P:(st + 1) * P],
                                        UKV[:, RT + k, :], start=(k == 0), stop=(k == RT - 1))
                ins.then_inc(v_made, 1)

            pe.wait_ge(rel_ready, 2 * IH // 2 + 1)
            rnn_block(0, first=True)
            with pe.Fori(1, KT) as j:
                rnn_block(j)
            keys_values(0)
            rnn_gates(KT - 1)

            def output(h):
                pe.wait_ge(p_kept, h + 2)
                pe.wait_ge(v_kept, h + 2)
                if not isinstance(h, int) or h:
                    pe.wait_ge(head_mixed, h + 1)
                for st in range(2):
                    ins = pe.matmul(banks[6][:, 0:S], VS[:, st, :], PTS[:, st * S:(st + 1) * S], start=(st == 0),
                                    stop=(st == 1))
                ins.then_inc(y_made, 1)

            def one_head(h, first=False, last=False):
                pe.wait_ge(gr_used, h + 1)
                columns_out(pe, pair_of("heads", h, 2, 0), 0, banks[0][:, 0:S])
                if not first:
                    output(h - 1)
                pe.wait_ge(k_kept, h + 2)
                pe.wait_ge(q_staged, h + 1)
                pe.wait_ge(p_exp, h * 2 + 1)
                for t in range(TT):
                    ins = pe.matmul(banks[4][:, t * S:(t + 1) * S], QS2[:, t * P:(t + 1) * P], KTS, start=True,
                                    stop=True)
                ins.then_inc(logits_made, 1)
                pe.wait_ge(ga_tanh, h + 1)
                columns_out(pe, pair_of("heads", h, 2, 1), 1, banks[1][:, 0:S])
                if not last:
                    keys_values(h + 1)
                pe.wait_ge(p_ready, h * 2 + 2)
                pe.wait_ge(p_kept, h + 1)
                for st in range(2):
                    for t in range(TT):
                        ins = pe.transpose(banks[5][:, st * S + t * P:st * S + (t + 1) * P],
                                           LG[:, t, st * P:(st + 1) * P], ident)
                ins.then_inc(p_turned, 1)

            one_head(0, first=True)
            with pe.Fori(1, H2 - 1) as h:
                one_head(h)
            one_head(H2 - 1, last=True)
            output(H2 - 1)

            pe.wait_ge(act_lo_ready, 4 * KT + 8)
            blocks_out("w_o", added, 4, 5)
            turn_rows(3, 5)
            def experts_in(pair, b2, n, units=(0, 1)):
                if units[0] == 0:
                    pe.wait_ge(gelu_ready[n], b2 + 1)
                columns_out(pe, pair, n, banks[2 + n][:, 0:S], units)

            pe.wait_ge(keys_ready, 16)
            with pe.Fori(0, PH) as h:
                for a in range(2):
                    pe.wait_ge(pq_kept[a], h)
                    columns_out(pe, pair_of("wqu", h, 4, a), a, banks[a][:, 0:S], fills=6)
                for a in range(2):
                    pe.wait_ge(pq_kept[a], h + 1)
                    pe.wait_ge(ps_kept[a], h + 1)
                    for t in range(TT):
                        ins = pe.matmul(banks[4 + a][:, t * P:(t + 1) * P], PQS[:, a, t * P:(t + 1) * P], KEYT[:, a, :],
                                        start=True, stop=True)
                    ins.then_inc(ps_made[a], 1)
                    experts_in(pair_of("wqu", h, 4, 2 + a), h, a)
            with pe.Fori(0, PH) as i:
                for n in range(2):
                    experts_in(pair_of("u_decode", i, 2, n), i + PH, n)
            for a in range(2):
                pe.wait_ge(ps_kept[a], PH + 1)
            for a in range(3):
                pe.wait_ge(picks_ready, a + 1)
                for t in range(TT):
                    pe.transpose(banks[4 + a][:, t * P:(t + 1) * P],
                                 PICKT[:, a, t, :, :].rearrange("p h k -> p (h k)"),
                                 ident).then_inc(picks_turned, 1)
            with pe.Fori(0, S // 16) as i:
                for n in range(2):
                    for m in range(2):
                        experts_in(pair_of("u_gates", i, 2, n), i + 2 * PH, n, units=(m,))
                        pe.wait_ge(gate_kept[m], i * 2 + n + 1)
                        for s in range(4):
                            pe.wait_ge(hot1, i * 16 + (8 * n + 4 * m + s + 1))
                            pe.wait_ge(hot2, i * 16 + (8 * n + 4 * m + s + 1) + 1)
                            pe.matmul(banks[m][:, s * P:(s + 1) * P], hot[:, 1, s, :], hot[:, 0, s, :], start=True,
                                      stop=True).then_inc(hot_used[s], 1)
            with pe.Fori(0, EARLY // 2) as i:
                for n in range(2):
                    experts_in(pair_of("u_late", i, 2, n), i + EARLY // 2, n)
            def expert(i, n, first=False, last=False):
                pe.wait_ge(el_ready, i * 2 + n + 1)
                if first:
                    for m in range(2):
                        pe.wait_ge(gelu_ready[m], NB // 2 + 1)
                        pe.wait_ge(gate_kept[m], S // 8 + 1)
                for u in range(2):
                    pe.wait_ge(lo_ready, 2 * pair_of("v", i, 2, n) + u + 1)
                    s = unit_slot(n, u)
                    for t in range(TT):
                        for cc in range(2):
                            o = banks[4 * t + 2 * u + cc][:, :]
                            a_hi = act_hi[:, n, t * P:(t + 1) * P]
                            a_lo = act_lo[:, n, t * P:(t + 1) * P]
                            hi = w_hi[:, s, cc * 512:(cc + 1) * 512]
                            lo = w_lo[:, s, cc * 512:(cc + 1) * 512]
                            pe.matmul(o, a_hi, hi, start=first, stop=False, skip_group_check=True)
                            pe.matmul(o, a_hi, lo, start=False, stop=False, skip_group_check=True)
                            mm = pe.matmul(o, a_lo, hi, start=False, stop=last, skip_group_check=True)
                    mm.then_inc(unit_done, 1)

            expert(0, 0, first=True)
            expert(0, 1)
            with pe.Fori(1, NB // 2 - 1) as i:
                expert(i, 0)
                expert(i, 1)
            expert(NB // 2 - 1, 0)
            expert(NB // 2 - 1, 1, last=True)


def _columns(w):
    n = w.shape[1] // P
    return w.reshape(2, 8, P, n, P).transpose(3, 0, 2, 1, 4).reshape(2 * n, P, UNIT)


def _tokens(w):
    n = w.shape[1] // 512
    return w.reshape(8, 2, P, n, 512).transpose(3, 0, 2, 1, 4).reshape(8 * n, P, UNIT)


def _interleave(parts, n):
    return np.stack([a.reshape(n, 2, P, UNIT) for a in parts], 1).reshape(-1, P, UNIT)


def _by_partition(v):
    return np.ascontiguousarray(v.reshape(-1, P).T)


def _stream(i):
    w1, w2 = i["w_in"][0], i["w_in_2"][0]
    o = QKVG_W
    cb, cc, ch, gc = (_columns(w1[:, o + n * 1024:o + (n + 1) * 1024]) for n in range(4))
    cut = {"xr": (0, 2048), "q": (2048, 4096), "ckv": (4096, 4608), "qi": (4608, 5632), "kw": (5632, 5712),
           "gr": (5712, 7760), "ga": (7760, 9808)}
    part = {k: w2[:, a:b] for k, (a, b) in cut.items()}
    kw = np.pad(part["kw"], ((0, 0), (0, P - 80)))
    u = i["peer_u_2"][0].reshape(NB, P, 2, 8, P).transpose(0, 2, 4, 3, 1).reshape(2 * NB, P, UNIT)
    v = i["peer_v_2"][0].reshape(NB, P, 2, UNIT).transpose(0, 2, 1, 3).reshape(2 * NB, P, UNIT)
    wq = _columns(i["peer_wq_2"][0])
    wqu = np.stack([a.reshape(PH, 4, P, UNIT) for a in (wq, u[0:4 * PH])], 1).reshape(-1, P, UNIT)
    return np.concatenate([
        i["w_ple_proj"][0].reshape(2, P, 4, 512).transpose(2, 1, 0, 3).reshape(4, P, UNIT),
        _tokens(w1[:, :o]),
        _interleave([gc, cc, ch, cb], CONV_J),
        _tokens(i["w_out"][0]),
        _tokens(i["w_ple_gate"][0]),
        _tokens(part["ckv"]),
        _columns(kw), np.zeros((2, P, UNIT), np.float32),
        _columns(part["qi"]),
        _interleave([_columns(part["xr"]), _columns(part["q"])], KT),
        _interleave([_columns(part["gr"]), _columns(part["ga"])], KT),
        _tokens(i["w_o_2"][0]),
        wqu,
        u[4 * PH:], v,
    ])


def _constants():
    f = np.float32
    q = np.arange(P)[:, None]
    j = np.arange(2 * P)[None, :]
    inside = (j > q) & (j <= q + P)
    band = [np.where(inside & (j >= P), 0, NEG), np.where(inside, 0, NEG)]
    causal = [np.where(j <= q + t * P, 0, NEG) for t in range(TT)]
    freq = np.power(f(500000.0), -np.arange(HALF, dtype=f) * f(2.0) / f(ROT))
    ang = np.arange(S, dtype=f)[:, None] * freq[None, :]
    rope = [fn(ang).reshape(TT, P, HALF).transpose(1, 0, 2).reshape(P, -1) for fn in (np.cos, np.sin)]
    iota = np.broadcast_to(np.arange(P), (P, P))
    return np.concatenate([np.eye(P), iota, *band, *causal, *rope], 1).astype(f)


def _parameters(i):
    def rep(v):
        return np.broadcast_to(v.reshape(1, -1), (P, v.size))

    sinks = i["attn_sinks"][0].reshape(KVH, 2, 2).transpose(0, 2, 1)
    cw = i["conv_w"][0].reshape(3, CONV_J, P).transpose(2, 1, 0).reshape(P, -1)
    cw2 = i["conv_w_2"][0].reshape(4, KT, P).transpose(2, 1, 0).reshape(P, -1)
    return np.concatenate([
        _by_partition(i["norm_gain"]), _by_partition(i["ple_gate_norm_gain"]), _by_partition(i["norm_mix_g_2"]),
        _by_partition(i["norm_ffn_g_2"]), cw, cw2, _by_partition(i["conv_b_2"]), _by_partition(i["rg_ba_2"]),
        _by_partition(i["rg_bx_2"]), _by_partition(i["rg_lambda_2"]), _by_partition(i["kv_norm_g_2"]),
        rep(i["q_norm_gain"]), rep(i["k_norm_gain"]), rep(sinks), rep(i["idx_ln_g_2"]),
        rep(i["idx_ln_b_2"]),
    ], 1)


def _arrays(i):
    uk = i["w_uk_2"][0].reshape(H2, RT, P, P).transpose(0, 2, 1, 3)
    uv = i["w_uv_2"][0].reshape(H2, RT, P, P).transpose(0, 2, 1, 3)
    return {
        "stream": _stream(i),
        "x": np.ascontiguousarray(i["x"]),
        "p_t": np.ascontiguousarray(i["p"][0, 0].T.reshape(2, P, S).transpose(1, 0, 2).reshape(P, -1)),
        "rows": np.stack([np.broadcast_to(i[n].reshape(1, D), (P, D))
                          for n in ("ple_norm_gain", "b_ple_gate", "norm_final_g_2")]),
        "consts": _constants(),
        "params": _parameters(i),
        "rg_w": np.stack([i["rg_wa_2"][0], i["rg_wx_2"][0]], 1).transpose(2, 0, 1, 3).reshape(P, -1).copy(),
        "ukv": np.concatenate([uk, uv], 2).reshape(H2, P, 8 * P),
        "keys_t": np.concatenate([i["peer_keys1_2"][0].T, i["peer_keys2_2"][0].T], 1),
    }


def kernel(**inputs):
    import concourse.bacc as bacc
    from concourse.bass_utils import run_bass_kernel_spmd as run

    arrays = _arrays({k: np.asarray(v) for k, v in inputs.items()})
    nc = bacc.Bacc("TRN2", target_bir_lowering=False, num_devices=1, dynamic_dma_scratch_size=1024)
    args = {k: nc.dram_tensor(f"in_{k}", a.shape, F32, kind="ExternalInput").ap() for k, a in arrays.items()}
    out = nc.dram_tensor("out", (1, S, D), F32, kind="ExternalOutput").ap()
    build(nc, out=out, **args)
    r = run(nc, [{f"in_{k}": a for k, a in arrays.items()}], core_ids=[0])
    return r.results[0]["out"]
```
